# Optimizing a Trainium2 kernel written in Bass

```python
import numpy as np
import jax
import jax.numpy as jnp
from jax import lax
import jax, jax.numpy as jnp

D_MODEL = 1024
BATCH = 1
SEQ = 256
DEPTH = 2

HEAD_DIM = 64
ROT_DIM = HEAD_DIM // 4
ROPE_THETA = 500000.0
NORM_EPS = 1e-6
Q_BLOCK = 128
D_FF = 2816
NEG_INF = -1e30

A_GROUPS = 4
A_CHUNK = 128
A_WIDTH = A_GROUPS * HEAD_DIM
B_HEADS = 12
B_KV_HEADS = 3
B_WIDTH = B_HEADS * HEAD_DIM
B_KV_WIDTH = B_KV_HEADS * HEAD_DIM
CMP_LEN = 32
CMP_STRIDE = 16
CMP_HIDDEN = 256
SLC_BLOCK = 64
SLC_TOPN = 8
WINDOW = 512
N_BRANCH = 3
FORCE_SCORE = 1e4
C_HEADS = 8
C_WIDTH = C_HEADS * HEAD_DIM
IDX_HEADS = 4
IDX_DIM = 32
IDX_ROT = IDX_DIM // 4
DSA_TOPK = 256
D_HEADS = 8
D_WIDTH = D_HEADS * HEAD_DIM
MOBA_BLOCK = 256
MOBA_TOPK = 3

EVEN_SPLITS = (2 * A_WIDTH, B_WIDTH) + (B_KV_WIDTH,) * 6 + (B_HEADS * N_BRANCH,)
ODD_SPLITS = (C_WIDTH, HEAD_DIM, HEAD_DIM, IDX_HEADS * IDX_DIM, IDX_DIM, IDX_HEADS, D_WIDTH, D_WIDTH, D_WIDTH)
EVEN_IN = sum(EVEN_SPLITS)
ODD_IN = sum(ODD_SPLITS)
MIX_OUT = A_WIDTH + B_WIDTH
N_EVEN = (DEPTH + 1) // 2
N_ODD = DEPTH // 2


def rmsnorm(x, g):
    xf = x.astype(jnp.float32)
    y = xf * lax.rsqrt(jnp.mean(xf * xf, axis=-1, keepdims=True) + NORM_EPS)
    return (y * g.astype(jnp.float32)).astype(x.dtype)

def rope_tables(positions, rot_dim):
    inv_freq = ROPE_THETA ** (-jnp.arange(0, rot_dim, 2, dtype=jnp.float32) / rot_dim)
    ang = positions.astype(jnp.float32)[..., None] * inv_freq
    return jnp.cos(ang), jnp.sin(ang)

def partial_rope(x, cos, sin):
    half = cos.shape[-1]
    bshape = cos.shape[:2] + (1,) * (x.ndim - 3) + (half,)
    c = cos.reshape(bshape).astype(x.dtype)
    s = sin.reshape(bshape).astype(x.dtype)
    x1, x2, rest = x[..., :half], x[..., half:2 * half], x[..., 2 * half:]
    return jnp.concatenate([x1 * c - x2 * s, x2 * c + x1 * s, rest], axis=-1)

def masked_softmax(s, mask):
    s = jnp.where(mask, s.astype(jnp.float32), NEG_INF)
    return jnp.where(mask, jax.nn.softmax(s, axis=-1), 0.0)

def swiglu_ffn(x, g, w_gate, w_up, w_down):
    h = rmsnorm(x, g)
    return (jax.nn.silu(h @ w_gate) * (h @ w_up)) @ w_down

def split_cols(z, sizes):
    return jnp.split(z, [int(c) for c in np.cumsum(sizes)[:-1]], axis=-1)

def rows(a, b, q0):
    return lax.dynamic_slice_in_dim(a[b], q0, Q_BLOCK, axis=0)

def map_query_blocks(fn, batch, seq):
    n_qb = seq // Q_BLOCK

    def step(i):
        return fn(i // n_qb, (i % n_qb) * Q_BLOCK)

    out = lax.map(step, jnp.arange(batch * n_qb, dtype=jnp.int32))
    return out.reshape((batch, seq) + out.shape[2:])

def chunked_gmlp(z, sgu_norm, sgu_w, sgu_b):
    bsz, seq, _ = z.shape
    u, v = jnp.split(jax.nn.gelu(z), 2, axis=-1)
    v = rmsnorm(v, sgu_norm).reshape(bsz, seq // A_CHUNK, A_CHUNK, A_GROUPS, HEAD_DIM)
    causal = jnp.tril(jnp.ones((A_CHUNK, A_CHUNK), dtype=bool))
    w = jnp.where(causal, sgu_w, jnp.zeros_like(sgu_w))
    mixed = jnp.einsum('gts,bcsgd->bctgd', w, v) + sgu_b.T[:, :, None]
    return u * mixed.reshape(bsz, seq, A_WIDTH)

def compress_blocks(t, pos_emb, w1, w2):
    bsz, seq = t.shape[:2]
    n_cmp = (seq - CMP_LEN) // CMP_STRIDE + 1
    idx = jnp.arange(n_cmp)[:, None] * CMP_STRIDE + jnp.arange(CMP_LEN)[None, :]
    blk = t[:, idx] + pos_emb[:, None, :]
    blk = jnp.moveaxis(blk, 3, 2).reshape(bsz, n_cmp, B_KV_HEADS, CMP_LEN * HEAD_DIM)
    return jax.nn.gelu(blk @ w1) @ w2

def cmp_to_slc_overlap(n_cmp, n_slc):
    c0 = np.arange(n_cmp) * CMP_STRIDE
    s0 = np.arange(n_slc) * SLC_BLOCK
    m = (c0[:, None] < s0[None, :] + SLC_BLOCK) & (c0[:, None] + CMP_LEN > s0[None, :])
    return jnp.asarray(m, dtype=jnp.float32)

def nsa_attention(q_rot, q_raw, k_cmp, v_cmp, k_slc, v_slc, k_win, v_win, gates):
    bsz, seq = q_rot.shape[:2]
    grp = B_HEADS // B_KV_HEADS
    scale = HEAD_DIM ** -0.5
    n_cmp = k_cmp.shape[1]
    n_slc = seq // SLC_BLOCK
    top_n = min(SLC_TOPN, n_slc)
    overlap = cmp_to_slc_overlap(n_cmp, n_slc)
    cmp_end = jnp.arange(n_cmp) * CMP_STRIDE + CMP_LEN - 1
    blk_id = jnp.arange(n_slc)
    k_blk = k_slc.reshape(bsz, n_slc, SLC_BLOCK, B_KV_HEADS, HEAD_DIM).transpose(0, 3, 1, 2, 4)
    v_blk = v_slc.reshape(bsz, n_slc, SLC_BLOCK, B_KV_HEADS, HEAD_DIM).transpose(0, 3, 1, 2, 4)
    pad = jnp.zeros((bsz, WINDOW, B_KV_HEADS, HEAD_DIM), k_win.dtype)
    k_win_p = jnp.concatenate([pad, k_win], axis=1)
    v_win_p = jnp.concatenate([pad, v_win], axis=1)
    g_idx = jnp.arange(B_KV_HEADS)[:, None, None]
    win_off = jnp.arange(Q_BLOCK + WINDOW) - WINDOW

    def block(b, q0):
        t = q0 + jnp.arange(Q_BLOCK)
        qr = rows(q_rot, b, q0).reshape(Q_BLOCK, B_KV_HEADS, grp, HEAD_DIM)
        qn = rows(q_raw, b, q0).reshape(Q_BLOCK, B_KV_HEADS, grp, HEAD_DIM)
        s_c = jnp.einsum('qgrd,ngd->grqn', qn, k_cmp[b]) * scale
        p_c = masked_softmax(s_c, cmp_end[None, :] <= t[:, None])
        o_c = jnp.einsum('grqn,ngd->qgrd', p_c.astype(v_cmp.dtype), v_cmp[b])
        imp = jnp.einsum('grqn,nj->gqj', p_c, overlap)
        admissible = blk_id[None, :] * SLC_BLOCK <= t[:, None]
        forced = (blk_id[None, :] == 0) | (blk_id[None, :] == t[:, None] // SLC_BLOCK)
        imp = jnp.where(admissible, jnp.where(forced, FORCE_SCORE, imp), NEG_INF)
        _, sel = lax.top_k(imp, top_n)
        sel_ok = jnp.take_along_axis(jnp.broadcast_to(admissible, imp.shape), sel, axis=-1)
        ks = k_blk[b][g_idx, sel].reshape(B_KV_HEADS, Q_BLOCK, top_n * SLC_BLOCK, HEAD_DIM)
        vs = v_blk[b][g_idx, sel].reshape(B_KV_HEADS, Q_BLOCK, top_n * SLC_BLOCK, HEAD_DIM)
        tok = (sel[..., None] * SLC_BLOCK + jnp.arange(SLC_BLOCK)).reshape(B_KV_HEADS, Q_BLOCK, top_n * SLC_BLOCK)
        m_s = (tok <= t[None, :, None]) & jnp.repeat(sel_ok, SLC_BLOCK, axis=-1)
        s_s = jnp.einsum('qgrd,gqkd->grqk', qr, ks) * scale
        p_s = masked_softmax(s_s, m_s[:, None])
        o_s = jnp.einsum('grqk,gqkd->qgrd', p_s.astype(vs.dtype), vs)
        kw = lax.dynamic_slice_in_dim(k_win_p[b], q0, Q_BLOCK + WINDOW, axis=0)
        vw = lax.dynamic_slice_in_dim(v_win_p[b], q0, Q_BLOCK + WINDOW, axis=0)
        s_pos = q0 + win_off
        m_w = (s_pos[None, :] <= t[:, None]) & (s_pos[None, :] > t[:, None] - WINDOW) & (s_pos[None, :] >= 0)
        s_w = jnp.einsum('qgrd,kgd->grqk', qr, kw) * scale
        p_w = masked_softmax(s_w, m_w)
        o_w = jnp.einsum('grqk,kgd->qgrd', p_w.astype(vw.dtype), vw)
        g = rows(gates, b, q0).reshape(Q_BLOCK, B_KV_HEADS, grp, N_BRANCH)
        o = g[..., 0:1] * o_c + g[..., 1:2] * o_s + g[..., 2:3] * o_w
        return o.reshape(Q_BLOCK, B_WIDTH)

    return map_query_blocks(block, bsz, seq)

def dsa_attention(q, k, v, q_idx, k_idx, w_idx):
    bsz, seq = q.shape[:2]
    top_k = min(DSA_TOPK, seq // 4)
    scale = HEAD_DIM ** -0.5
    key_pos = jnp.arange(seq)

    def block(b, q0):
        t = q0 + jnp.arange(Q_BLOCK)
        qb = rows(q, b, q0)
        logits = jnp.einsum('qhd,sd->qhs', rows(q_idx, b, q0), k_idx[b]).astype(jnp.float32) * IDX_DIM ** -0.5
        score = jnp.einsum('qh,qhs->qs', rows(w_idx, b, q0).astype(jnp.float32), jax.nn.relu(logits)) * IDX_HEADS ** -0.5
        score = jnp.where(key_pos[None, :] <= t[:, None], score, NEG_INF)
        _, sel = lax.top_k(score, top_k)
        ok = sel <= t[:, None]
        ks = k[b][sel]
        vs = v[b][sel]
        s = jnp.einsum('qhd,qkd->hqk', qb, ks) * scale
        p = masked_softmax(s, ok[None])
        o = jnp.einsum('hqk,qkd->qhd', p.astype(vs.dtype), vs)
        return o.reshape(Q_BLOCK, C_WIDTH)

    return map_query_blocks(block, bsz, seq)

def moba_attention(q, k, v):
    bsz, seq = q.shape[:2]
    n_blk = -(-seq // MOBA_BLOCK)
    pad = n_blk * MOBA_BLOCK - seq
    scale = HEAD_DIM ** -0.5
    k_blk = jnp.pad(k, ((0, 0), (0, pad), (0, 0), (0, 0))).reshape(bsz, n_blk, MOBA_BLOCK, D_HEADS, HEAD_DIM).transpose(0, 3, 1, 2, 4)
    v_blk = jnp.pad(v, ((0, 0), (0, pad), (0, 0), (0, 0))).reshape(bsz, n_blk, MOBA_BLOCK, D_HEADS, HEAD_DIM).transpose(0, 3, 1, 2, 4)
    k_mean = k_blk.mean(axis=3)
    top_k = min(MOBA_TOPK, n_blk - 1)
    blk_id = jnp.arange(n_blk)
    h_idx = jnp.arange(D_HEADS)[:, None, None]

    def block(b, q0):
        t = q0 + jnp.arange(Q_BLOCK)
        qb = rows(q, b, q0)
        own = q0 // MOBA_BLOCK
        k_own = lax.dynamic_index_in_dim(k_blk[b], own, axis=1, keepdims=False)
        v_own = lax.dynamic_index_in_dim(v_blk[b], own, axis=1, keepdims=False)
        own_pos = own * MOBA_BLOCK + jnp.arange(MOBA_BLOCK)
        s_own = jnp.einsum('qhd,hkd->hqk', qb, k_own) * scale
        m_own = jnp.broadcast_to(own_pos[None, :] <= t[:, None], s_own.shape)
        if top_k == 0:
            p = masked_softmax(s_own, m_own)
            o = jnp.einsum('hqk,hkd->qhd', p.astype(v_own.dtype), v_own)
        else:
            gate = jnp.einsum('qhd,hjd->hqj', qb, k_mean[b]).astype(jnp.float32)
            gate = jnp.where(blk_id < own, gate, NEG_INF)
            _, sel = lax.top_k(gate, top_k)
            ok = sel < own
            n_sel = top_k * MOBA_BLOCK
            ks = k_blk[b][h_idx, sel].reshape(D_HEADS, Q_BLOCK, n_sel, HEAD_DIM)
            vs = v_blk[b][h_idx, sel].reshape(D_HEADS, Q_BLOCK, n_sel, HEAD_DIM)
            s_sel = jnp.einsum('qhd,hqkd->hqk', qb, ks) * scale
            m_sel = jnp.repeat(ok, MOBA_BLOCK, axis=-1)
            p = masked_softmax(jnp.concatenate([s_sel, s_own], axis=-1), jnp.concatenate([m_sel, m_own], axis=-1))
            o = (jnp.einsum('hqk,hqkd->qhd', p[..., :n_sel].astype(vs.dtype), vs)
                 + jnp.einsum('hqk,hkd->qhd', p[..., n_sel:].astype(v_own.dtype), v_own))
        return o.reshape(Q_BLOCK, D_WIDTH)

    return map_query_blocks(block, bsz, seq)

def even_mixer(h, cos, sin, w_in, sgu_norm, sgu_w, sgu_b, cmp_pos_k, cmp_w1_k, cmp_w2_k,
               cmp_pos_v, cmp_w1_v, cmp_w2_v, w_out):
    bsz, seq, _ = h.shape
    a_in, q, kc, vc, ksl, vsl, kw, vw, gl = split_cols(h @ w_in, EVEN_SPLITS)

    def kv(t):
        return t.reshape(bsz, seq, B_KV_HEADS, HEAD_DIM)

    q_raw = q.reshape(bsz, seq, B_HEADS, HEAD_DIM)
    a_out = chunked_gmlp(a_in, sgu_norm, sgu_w, sgu_b)
    b_out = nsa_attention(partial_rope(q_raw, cos, sin), q_raw,
                          compress_blocks(kv(kc), cmp_pos_k, cmp_w1_k, cmp_w2_k),
                          compress_blocks(kv(vc), cmp_pos_v, cmp_w1_v, cmp_w2_v),
                          partial_rope(kv(ksl), cos, sin), kv(vsl),
                          partial_rope(kv(kw), cos, sin), kv(vw),
                          jax.nn.sigmoid(gl).reshape(bsz, seq, B_HEADS, N_BRANCH))
    return jnp.concatenate([a_out, b_out], axis=-1) @ w_out

def odd_mixer(h, cos, sin, cos_i, sin_i, w_in, w_out):
    bsz, seq, _ = h.shape
    qc, kc, vc, qi, ki, wi, qd, kd, vd = split_cols(h @ w_in, ODD_SPLITS)
    c_out = dsa_attention(partial_rope(qc.reshape(bsz, seq, C_HEADS, HEAD_DIM), cos, sin),
                          partial_rope(kc, cos, sin), vc,
                          partial_rope(qi.reshape(bsz, seq, IDX_HEADS, IDX_DIM), cos_i, sin_i),
                          partial_rope(ki, cos_i, sin_i), wi)
    d_out = moba_attention(partial_rope(qd.reshape(bsz, seq, D_HEADS, HEAD_DIM), cos, sin),
                           partial_rope(kd.reshape(bsz, seq, D_HEADS, HEAD_DIM), cos, sin),
                           vd.reshape(bsz, seq, D_HEADS, HEAD_DIM))
    return jnp.concatenate([c_out, d_out], axis=-1) @ w_out

def first_inputs(seed: int = 0) -> dict:
    key = jax.random.key(seed)
    keys = iter(jax.random.split(key, 40))

    def nrm(shape, scale):
        return jax.random.normal(next(keys), shape, jnp.float32) * scale

    def gain(shape):
        return 1.0 + nrm(shape, 0.1)

    x = nrm((BATCH, SEQ, D_MODEL), 1.0)
    offset = jax.random.randint(next(keys), (BATCH, 1), 0, 4096, dtype=jnp.int32)
    positions = offset + jnp.arange(SEQ, dtype=jnp.int32)[None, :]
    return {
        'x': x,
        'positions': positions,
        'ffn1_norm': gain((DEPTH, D_MODEL)),
        'ffn1_w_gate': nrm((DEPTH, D_MODEL, D_FF), D_MODEL ** -0.5),
        'ffn1_w_up': nrm((DEPTH, D_MODEL, D_FF), D_MODEL ** -0.5),
        'ffn1_w_down': nrm((DEPTH, D_FF, D_MODEL), D_FF ** -0.5),
        'mix_norm': gain((DEPTH, D_MODEL)),
        'ffn2_norm': gain((DEPTH, D_MODEL)),
        'ffn2_w_gate': nrm((DEPTH, D_MODEL, D_FF), D_MODEL ** -0.5),
        'ffn2_w_up': nrm((DEPTH, D_MODEL, D_FF), D_MODEL ** -0.5),
        'ffn2_w_down': nrm((DEPTH, D_FF, D_MODEL), D_FF ** -0.5),
        'ev_w_in': nrm((N_EVEN, D_MODEL, EVEN_IN), D_MODEL ** -0.5),
        'ev_sgu_norm': gain((N_EVEN, A_WIDTH)),
        'ev_sgu_w': nrm((N_EVEN, A_GROUPS, A_CHUNK, A_CHUNK), A_CHUNK ** -0.5),
        'ev_sgu_b': gain((N_EVEN, A_GROUPS, A_CHUNK)),
        'ev_cmp_pos_k': nrm((N_EVEN, CMP_LEN, HEAD_DIM), 0.1),
        'ev_cmp_w1_k': nrm((N_EVEN, CMP_LEN * HEAD_DIM, CMP_HIDDEN), (CMP_LEN * HEAD_DIM) ** -0.5),
        'ev_cmp_w2_k': nrm((N_EVEN, CMP_HIDDEN, HEAD_DIM), CMP_HIDDEN ** -0.5),
        'ev_cmp_pos_v': nrm((N_EVEN, CMP_LEN, HEAD_DIM), 0.1),
        'ev_cmp_w1_v': nrm((N_EVEN, CMP_LEN * HEAD_DIM, CMP_HIDDEN), (CMP_LEN * HEAD_DIM) ** -0.5),
        'ev_cmp_w2_v': nrm((N_EVEN, CMP_HIDDEN, HEAD_DIM), CMP_HIDDEN ** -0.5),
        'ev_w_out': nrm((N_EVEN, MIX_OUT, D_MODEL), MIX_OUT ** -0.5),
        'od_w_in': nrm((N_ODD, D_MODEL, ODD_IN), D_MODEL ** -0.5),
        'od_w_out': nrm((N_ODD, MIX_OUT, D_MODEL), MIX_OUT ** -0.5),
        'final_norm': gain((D_MODEL,)),
    }

def first_block(x, positions, ffn1_norm, ffn1_w_gate, ffn1_w_up, ffn1_w_down, mix_norm,
              ffn2_norm, ffn2_w_gate, ffn2_w_up, ffn2_w_down, ev_w_in, ev_sgu_norm, ev_sgu_w,
              ev_sgu_b, ev_cmp_pos_k, ev_cmp_w1_k, ev_cmp_w2_k, ev_cmp_pos_v, ev_cmp_w1_v,
              ev_cmp_w2_v, ev_w_out, od_w_in, od_w_out, final_norm):
    cos, sin = rope_tables(positions, ROT_DIM)
    cos_i, sin_i = rope_tables(positions, IDX_ROT)
    for i in range(DEPTH):
        x = x + 0.5 * swiglu_ffn(x, ffn1_norm[i], ffn1_w_gate[i], ffn1_w_up[i], ffn1_w_down[i])
        h = rmsnorm(x, mix_norm[i])
        if i % 2 == 0:
            e = i // 2
            x = x + even_mixer(h, cos, sin, ev_w_in[e], ev_sgu_norm[e], ev_sgu_w[e], ev_sgu_b[e],
                               ev_cmp_pos_k[e], ev_cmp_w1_k[e], ev_cmp_w2_k[e],
                               ev_cmp_pos_v[e], ev_cmp_w1_v[e], ev_cmp_w2_v[e], ev_w_out[e])
        else:
            o = i // 2
            x = x + odd_mixer(h, cos, sin, cos_i, sin_i, od_w_in[o], od_w_out[o])
        x = x + 0.5 * swiglu_ffn(x, ffn2_norm[i], ffn2_w_gate[i], ffn2_w_up[i], ffn2_w_down[i])
    return rmsnorm(x, final_norm)


DEPTH_2 = 1

A_WIDTH_2 = D_MODEL // 2
A_HEAD = 64
A_HEADS = A_WIDTH_2 // A_HEAD
A_DECAY_RANK = 64
A_ICLR_RANK = 64
A_GATE_RANK = 128
GN_EPS = 64e-5
B_WIDTH_2 = D_MODEL // 2
B_BLOCKS = 8
B_BLOCK = B_WIDTH_2 // B_BLOCKS
CONV_WIDTH = 4
LRU_C = 8.0
IN_COLS = 3 * A_WIDTH_2 + 2 * B_WIDTH_2 + 2 * D_MODEL
N_GROUPS = 4
EXPERTS_PER_GROUP = 8
N_EXPERTS = N_GROUPS * EXPERTS_PER_GROUP
TOP_K = 2
D_EXPERT = 256
EPS = 1e-6


def rmsnorm_2(x, g):
    xf = x.astype(jnp.float32)
    y = xf * lax.rsqrt(jnp.mean(xf * xf, axis=-1, keepdims=True) + EPS)
    return (y * g.astype(jnp.float32)).astype(x.dtype)

def modulate(h, shift, scale):
    return h * (1 + scale[:, None, :]) + shift[:, None, :]

def token_shift(t):
    return jnp.pad(t, ((0, 0), (1, 0), (0, 0)))[:, :-1]

def rwkv7_time_mix(xn, rkv, mu_rkv, mu_wag, w0, w1, w2, a0, a1, a2, g1, g2,
                   k_k, k_a, r_k, lnx_g, lnx_b):
    bsz, seq, _ = xn.shape
    f32 = jnp.float32
    rkv = rkv + (token_shift(rkv) - rkv) * mu_rkv
    r, k, v = jnp.split(rkv, 3, axis=-1)
    dx = token_shift(xn) - xn
    xw = xn + dx * mu_wag[0]
    xa = xn + dx * mu_wag[1]
    xg = xn + dx * mu_wag[2]
    w_log = -jax.nn.softplus(-(w0 + jnp.tanh(xw @ w1) @ w2)) - 0.5
    decay = jnp.exp(-jnp.exp(w_log.astype(f32)))
    a = jax.nn.sigmoid(a0 + (xa @ a1) @ a2)
    g = jax.nn.sigmoid(xg @ g1) @ g2
    heads = lambda t: t.reshape(bsz, seq, A_HEADS, A_HEAD)
    kk = heads((k * k_k).astype(f32))
    kk = kk * lax.rsqrt(jnp.sum(kk * kk, axis=-1, keepdims=True) + 1e-12)
    k = k * (1 + (a - 1) * k_a)
    r_h, k_h, v_h, a_h = (heads(t.astype(f32)) for t in (r, k, v, a))
    w_h = heads(decay)
    seq_first = lambda t: jnp.moveaxis(t, 1, 0)
    xs = tuple(seq_first(t) for t in (r_h, w_h, k_h, v_h, -kk, kk * a_h))

    def step(state, inp):
        r_t, w_t, k_t, v_t, a_t, b_t = inp
        sa = jnp.einsum('bhvk,bhk->bhv', state, a_t)
        state = (state * w_t[:, :, None, :] + sa[..., None] * b_t[:, :, None, :]
                 + v_t[..., None] * k_t[:, :, None, :])
        y_t = jnp.einsum('bhvk,bhk->bhv', state, r_t)
        return state, y_t

    state0 = jnp.zeros((bsz, A_HEADS, A_HEAD, A_HEAD), f32)
    _, y = lax.scan(step, state0, xs)
    y = jnp.moveaxis(y, 0, 1)
    mean = jnp.mean(y, axis=-1, keepdims=True)
    var = jnp.mean(jnp.square(y - mean), axis=-1, keepdims=True)
    y = ((y - mean) * lax.rsqrt(var + GN_EPS)).reshape(bsz, seq, A_WIDTH_2)
    y = y * lnx_g.astype(f32) + lnx_b.astype(f32)
    bonus = jnp.sum(r_h * k_h * r_k.astype(f32), axis=-1, keepdims=True) * v_h
    y = y + bonus.reshape(bsz, seq, A_WIDTH_2)
    return (y * g.astype(f32)).astype(xn.dtype)

def rglru_branch(xb, gb, conv_w, conv_b, w_rgate, b_rgate, w_igate, b_igate, lam):
    bsz, seq, _ = xb.shape
    f32 = jnp.float32
    xc = lax.conv_general_dilated(
        xb, conv_w, window_strides=(1,), padding=((CONV_WIDTH - 1, 0),),
        dimension_numbers=('NWC', 'WIO', 'NWC'), feature_group_count=B_WIDTH_2) + conv_b
    xblk = xc.reshape(bsz, seq, B_BLOCKS, B_BLOCK)
    gate_r = jax.nn.sigmoid((jnp.einsum('bsgi,gij->bsgj', xblk, w_rgate)
                             .reshape(bsz, seq, B_WIDTH_2) + b_rgate).astype(f32))
    gate_i = jax.nn.sigmoid((jnp.einsum('bsgi,gij->bsgj', xblk, w_igate)
                             .reshape(bsz, seq, B_WIDTH_2) + b_igate).astype(f32))
    log_a = -LRU_C * gate_r * jax.nn.softplus(-lam.astype(f32))
    a = jnp.exp(log_a)
    u = jnp.sqrt(-jnp.expm1(2.0 * log_a)) * (gate_i * xc.astype(f32))

    def combine(left, right):
        a_l, u_l = left
        a_r, u_r = right
        return a_l * a_r, a_r * u_l + u_r

    _, h = lax.associative_scan(combine, (a, u), axis=1)
    return (h * jax.nn.gelu(gb.astype(f32))).astype(xb.dtype)

def hier_moe(h, w_rg, b_rg, w_re, b_re, w1e, w3e, w2e):
    bsz, seq, d = h.shape
    f32 = jnp.float32
    t = h.reshape(-1, d)
    pg = jax.nn.softmax((t @ w_rg + b_rg).astype(f32), axis=-1)
    pg_top, g_idx = lax.top_k(pg, 1)
    le = (t @ w_re + b_re).astype(f32).reshape(-1, N_GROUPS, EXPERTS_PER_GROUP)
    le_sel = jnp.take_along_axis(le, g_idx[:, :, None], axis=1)[:, 0]
    pe = jax.nn.softmax(le_sel, axis=-1)
    pe_top, e_idx = lax.top_k(pe, TOP_K)
    pe_top = pe_top / jnp.sum(pe_top, axis=-1, keepdims=True)
    wts = pg_top * pe_top
    flat_idx = g_idx * EXPERTS_PER_GROUP + e_idx
    cw = jnp.sum(jax.nn.one_hot(flat_idx, N_EXPERTS, dtype=f32) * wts[..., None], axis=1)
    cw = cw.astype(h.dtype)
    out = jnp.zeros_like(t)
    for e in range(N_EXPERTS):
        he = jax.nn.silu(t @ w1e[e]) * (t @ w3e[e])
        out = out + cw[:, e:e + 1] * (he @ w2e[e])
    return out.reshape(bsz, seq, d)

def second_inputs(seed: int = 0) -> dict:
    key = jax.random.key(seed)
    ks = iter(jax.random.split(key, 64))
    nrm = lambda shape, s: jax.random.normal(next(ks), shape, jnp.float32) * s
    uni = lambda shape, lo, hi: jax.random.uniform(next(ks), shape, jnp.float32, lo, hi)
    L, D, A, Bw, F = DEPTH_2, D_MODEL, A_WIDTH_2, B_WIDTH_2, D_EXPERT
    x = nrm((BATCH, SEQ, D), 1.0)
    c = nrm((BATCH, D), 1.0)
    w_ada = nrm((L, D, 6 * D), D ** -0.5)
    b_ada = nrm((L, 6 * D), 0.02)
    g_mix = 1.0 + nrm((L, D), 0.02)
    w_in = nrm((L, D, IN_COLS), D ** -0.5)
    mu_rkv = uni((L, 3 * A), 0.0, 1.0)
    mu_wag = uni((L, 3, D), 0.0, 1.0)
    w0 = uni((L, A), -6.0, -1.0)
    w1 = nrm((L, D, A_DECAY_RANK), D ** -0.5)
    w2 = nrm((L, A_DECAY_RANK, A), 0.5 * A_DECAY_RANK ** -0.5)
    a0 = nrm((L, A), 0.1)
    a1 = nrm((L, D, A_ICLR_RANK), D ** -0.5)
    a2 = nrm((L, A_ICLR_RANK, A), 0.5 * A_ICLR_RANK ** -0.5)
    g1 = nrm((L, D, A_GATE_RANK), D ** -0.5)
    g2 = nrm((L, A_GATE_RANK, A), A_GATE_RANK ** -0.5)
    k_k = 0.85 + nrm((L, A), 0.02)
    k_a = 1.0 + nrm((L, A), 0.02)
    r_k = nrm((L, A_HEADS, A_HEAD), 0.1)
    lnx_g = 1.0 + nrm((L, A), 0.02)
    lnx_b = nrm((L, A), 0.02)
    conv_w = nrm((L, CONV_WIDTH, 1, Bw), CONV_WIDTH ** -0.5)
    conv_b = nrm((L, Bw), 0.02)
    w_rgate = nrm((L, B_BLOCKS, B_BLOCK, B_BLOCK), B_BLOCK ** -0.5)
    b_rgate = nrm((L, Bw), 0.02)
    w_igate = nrm((L, B_BLOCKS, B_BLOCK, B_BLOCK), B_BLOCK ** -0.5)
    b_igate = nrm((L, Bw), 0.02)
    s = uni((L, Bw), 0.9, 0.999) ** (1.0 / LRU_C)
    lam = jnp.log(s) - jnp.log1p(-s)
    p_a = nrm((L, A, D), A ** -0.5)
    p_b = nrm((L, Bw, D), Bw ** -0.5)
    w_out = nrm((L, D, D), D ** -0.5)
    g_ffn = 1.0 + nrm((L, D), 0.02)
    w_rg = nrm((L, D, N_GROUPS), D ** -0.5)
    b_rg = nrm((L, N_GROUPS), 0.01)
    w_re = nrm((L, D, N_EXPERTS), D ** -0.5)
    b_re = nrm((L, N_EXPERTS), 0.01)
    w1e = nrm((L, N_EXPERTS, D, F), D ** -0.5)
    w3e = nrm((L, N_EXPERTS, D, F), D ** -0.5)
    w2e = nrm((L, N_EXPERTS, F, D), F ** -0.5)
    g_final = 1.0 + nrm((D,), 0.02)
    w_ada_f = nrm((D, 2 * D), D ** -0.5)
    b_ada_f = nrm((2 * D,), 0.02)
    return {'x': x, 'c': c, 'w_ada': w_ada, 'b_ada': b_ada, 'g_mix': g_mix, 'w_in': w_in,
            'mu_rkv': mu_rkv, 'mu_wag': mu_wag, 'w0': w0, 'w1': w1, 'w2': w2,
            'a0': a0, 'a1': a1, 'a2': a2, 'g1': g1, 'g2': g2, 'k_k': k_k, 'k_a': k_a,
            'r_k': r_k, 'lnx_g': lnx_g, 'lnx_b': lnx_b, 'conv_w': conv_w, 'conv_b': conv_b,
            'w_rgate': w_rgate, 'b_rgate': b_rgate, 'w_igate': w_igate, 'b_igate': b_igate,
            'lam': lam, 'p_a': p_a, 'p_b': p_b, 'w_out': w_out, 'g_ffn': g_ffn,
            'w_rg': w_rg, 'b_rg': b_rg, 'w_re': w_re, 'b_re': b_re,
            'w1e': w1e, 'w3e': w3e, 'w2e': w2e,
            'g_final': g_final, 'w_ada_f': w_ada_f, 'b_ada_f': b_ada_f}

def second_block(x, c, w_ada, b_ada, g_mix, w_in, mu_rkv, mu_wag, w0, w1, w2, a0, a1, a2,
              g1, g2, k_k, k_a, r_k, lnx_g, lnx_b, conv_w, conv_b, w_rgate, b_rgate,
              w_igate, b_igate, lam, p_a, p_b, w_out, g_ffn, w_rg, b_rg, w_re, b_re,
              w1e, w3e, w2e, g_final, w_ada_f, b_ada_f):
    c_act = jax.nn.silu(c)
    o1 = 3 * A_WIDTH_2
    o2 = o1 + B_WIDTH_2
    o3 = o2 + B_WIDTH_2
    o4 = o3 + D_MODEL
    for l in range(DEPTH_2):
        mod = c_act @ w_ada[l] + b_ada[l]
        sh1, sc1, gt1, sh2, sc2, gt2 = jnp.split(mod, 6, axis=-1)
        h = modulate(rmsnorm_2(x, g_mix[l]), sh1, sc1)
        proj = h @ w_in[l]
        y_a = rwkv7_time_mix(h, proj[..., :o1], mu_rkv[l], mu_wag[l], w0[l], w1[l], w2[l],
                             a0[l], a1[l], a2[l], g1[l], g2[l], k_k[l], k_a[l], r_k[l],
                             lnx_g[l], lnx_b[l])
        y_b = rglru_branch(proj[..., o1:o2], proj[..., o2:o3], conv_w[l], conv_b[l],
                           w_rgate[l], b_rgate[l], w_igate[l], b_igate[l], lam[l])
        merged = (jax.nn.sigmoid(proj[..., o3:o4]) * (y_a @ p_a[l])
                  + jax.nn.sigmoid(proj[..., o4:]) * (y_b @ p_b[l]))
        x = x + gt1[:, None, :] * (merged @ w_out[l])
        h2 = modulate(rmsnorm_2(x, g_ffn[l]), sh2, sc2)
        x = x + gt2[:, None, :] * hier_moe(h2, w_rg[l], b_rg[l], w_re[l], b_re[l],
                                           w1e[l], w3e[l], w2e[l])
    shf, scf = jnp.split(c_act @ w_ada_f + b_ada_f, 2, axis=-1)
    return modulate(rmsnorm_2(x, g_final), shf, scf)


def setup_inputs(seed=0):
    out = dict(first_inputs(seed))
    for name, value in second_inputs(seed + 1).items():
        if name != "x":
            out[name + "_2"] = value
    return out


def reference(
    x, positions, ffn1_norm, ffn1_w_gate, ffn1_w_up, ffn1_w_down, mix_norm, ffn2_norm,
    ffn2_w_gate, ffn2_w_up, ffn2_w_down, ev_w_in, ev_sgu_norm, ev_sgu_w, ev_sgu_b, ev_cmp_pos_k,
    ev_cmp_w1_k, ev_cmp_w2_k, ev_cmp_pos_v, ev_cmp_w1_v, ev_cmp_w2_v, ev_w_out, od_w_in,
    od_w_out, final_norm, c_2, w_ada_2, b_ada_2, g_mix_2, w_in_2, mu_rkv_2, mu_wag_2, w0_2,
    w1_2, w2_2, a0_2, a1_2, a2_2, g1_2, g2_2, k_k_2, k_a_2, r_k_2, lnx_g_2, lnx_b_2, conv_w_2,
    conv_b_2, w_rgate_2, b_rgate_2, w_igate_2, b_igate_2, lam_2, p_a_2, p_b_2, w_out_2, g_ffn_2,
    w_rg_2, b_rg_2, w_re_2, b_re_2, w1e_2, w3e_2, w2e_2, g_final_2, w_ada_f_2, b_ada_f_2,
):
    x = first_block(
        x, positions, ffn1_norm, ffn1_w_gate, ffn1_w_up, ffn1_w_down, mix_norm, ffn2_norm,
        ffn2_w_gate, ffn2_w_up, ffn2_w_down, ev_w_in, ev_sgu_norm, ev_sgu_w, ev_sgu_b,
        ev_cmp_pos_k, ev_cmp_w1_k, ev_cmp_w2_k, ev_cmp_pos_v, ev_cmp_w1_v, ev_cmp_w2_v,
        ev_w_out, od_w_in, od_w_out, final_norm,
    )
    return second_block(
        x, c_2, w_ada_2, b_ada_2, g_mix_2, w_in_2, mu_rkv_2, mu_wag_2, w0_2, w1_2, w2_2, a0_2,
        a1_2, a2_2, g1_2, g2_2, k_k_2, k_a_2, r_k_2, lnx_g_2, lnx_b_2, conv_w_2, conv_b_2,
        w_rgate_2, b_rgate_2, w_igate_2, b_igate_2, lam_2, p_a_2, p_b_2, w_out_2, g_ffn_2,
        w_rg_2, b_rg_2, w_re_2, b_re_2, w1e_2, w3e_2, w2e_2, g_final_2, w_ada_f_2, b_ada_f_2,
    )


_drawn_inputs = setup_inputs


def setup_inputs(seed=0):
    import zlib

    import numpy as np

    out = dict(_drawn_inputs(seed))
    spreads = {}
    factors = {'ev_cmp_pos_k': 4.312,
     'g_mix_2': 3.409,
     'w1_2': 3.445,
     'w2_2': 3.109,
     'a0_2': 3.999,
     'k_k_2': 62.1,
     'k_a_2': 2.902,
     'lnx_g_2': 58.16,
     'lnx_b_2': 40.218,
     'b_rgate_2': 34.49,
     'b_igate_2': 18.587,
     'g_ffn_2': 2.749,
     'b_rg_2': 6.04,
     'b_re_2': 27.786,
     'g_final_2': 28.014,
     'conv_b_2': 7.695,
     'b_ada_f_2': 3.105}
    for name, (base, spread) in spreads.items():
        noise = np.random.default_rng([zlib.crc32(name.encode()), seed]).standard_normal(out[name].shape)
        drawn = base * np.exp(spread * noise) if base else spread * noise
        out[name] = jnp.asarray(drawn.astype(out[name].dtype))
    for name, factor in factors.items():
        out[name] = (out[name] * factor).astype(out[name].dtype)
    return out
```

```python
from contextlib import ExitStack

import numpy as np
import concourse.bass as bass
from concourse import mybir

ALU = mybir.AluOpType
ACT = mybir.ActivationFunctionType
F32 = mybir.dt.float32
F32R = mybir.dt.float32r
I32 = mybir.dt.int32
U32 = mybir.dt.uint32
AX = mybir.AxisListType

P = 128
T = 256
D = 1024
NEG = -1e30
RING = 4
SLOT = 2048
NAR = 25900

UNITS = {"ffn": 11, "moe": 32}


def slot_order():
    o = []

    def units(tag, n):
        for u in range(n):
            o.extend([(tag + "g", u), (tag + "u", u), (tag + "d", u)])

    units("f1_0", 11)
    o.extend([("evin", g, a) for g in range(5) for a in range(2)])
    o.extend([("cmpk", 0), ("cmpk", 1), ("cmpv", 0), ("cmpv", 1)])
    o.extend([("evout", g) for g in range(4)])
    units("f2_0", 11)
    units("f1_1", 11)
    o.extend([("odin", g, a) for g in range(5) for a in range(2)])
    o.extend([("odout", g) for g in range(4)])
    units("f2_1", 11)
    o.extend([("ada", g) for g in range(32)])
    o.extend([("win2", g) for g in range(18)])
    o.extend([("pb", g) for g in range(2)] + [("pa", g) for g in range(2)])
    o.extend([("wout2", g) for g in range(4)])
    units("moe", 32)
    return o


COLS = [
    ("n1_0", 8), ("nm_0", 8), ("n2_0", 8), ("n1_1", 8), ("nm_1", 8), ("n2_1", 8), ("nf", 8),
    ("g_mix", 8), ("g_ffn", 8), ("g_final", 8), ("c", 8), ("b_ada", 64),
    ("mu_rkv", 12), ("mu_wag", 24), ("w0", 4), ("a0", 4), ("k_k", 4), ("k_a", 4), ("r_k", 4),
    ("lnx_g", 4), ("lnx_b", 4), ("conv_w", 16), ("conv_b", 4), ("b_r", 4), ("b_i", 4), ("lam", 4),
    ("sgu_b", 4), ("sgu_wT", 512), ("sgu_n", 256), ("w2k", 128), ("w2v", 128), ("pos_k", 16), ("pos_v", 16),
    ("lw1", 512), ("la1", 512), ("lg1", 1024), ("lw2", 512), ("la2", 512), ("lg2", 512),
    ("wr", 512), ("wi", 512), ("wre", 288), ("bre", 36),
]
CONSTS = [
    ("ident", 128), ("ones", 128), ("bones", 128), ("triT", 128), ("madd0", 128), ("madd1", 256),
    ("cm01", 30), ("cmadd", 30), ("inv", 8), ("gmask", 512), ("seg", 256),
] + [(f"lv{m}", 128) for m in range(6)] + [(f"lt{m}", 128) for m in range(6)]


def offsets(spec):
    at, out = 0, {}
    for n, w in spec:
        out[n] = (at, w)
        at += w
    return out, at


COFF, NCOL = offsets(COLS)
KOFF, NCON = offsets(CONSTS)


def const_array():
    a = np.zeros((P, NCON), np.float32)

    def put(n, v):
        o, w = KOFF[n]
        a[:v.shape[0], o:o + w] = v.reshape(v.shape[0], w)

    i = np.arange(P)
    put("ident", np.eye(P))
    put("ones", np.ones((P, P)))
    put("bones", (i[:, None] // 64 == i[None, :] // 64) * 1.0)
    put("triT", (i[:, None] <= i[None, :]) * 1.0)
    tri = np.where(i[None, :] <= i[:, None], 0.0, NEG)
    put("madd0", tri)
    put("madd1", np.concatenate([np.zeros((P, P)), tri], 1))
    t = i[:, None, None] + 128 * np.arange(2)[None, :, None]
    ok = (np.arange(15)[None, None, :] * 16 + 31) <= t
    put("cm01", ok * 1.0)
    put("cmadd", np.where(ok, 0.0, NEG))
    inv = np.float32(500000.0) ** (-np.arange(0, 16, 2, dtype=np.float32) / np.float32(16))
    put("inv", np.broadcast_to(inv[None, :], (P, 8)))
    same = i[:, None] // 64 == i[None, :] // 64
    su = same & (i[:, None] < i[None, :])
    u = same & (i[:, None] <= i[None, :])
    put("gmask", np.stack([su, u, su, u], 1) * 1.0)
    put("seg", np.broadcast_to((np.arange(256) % 64 != 0)[None, :] * 1.0, (P, 256)))
    for n in range(6):
        m = 1 << n
        lo = (i[:, None] // (2 * m) == i[None, :] // (2 * m)) & (i[:, None] // m % 2 == 1) & (i[None, :] // m % 2 == 0)
        put(f"lv{n}", lo * 1.0)
        put(f"lt{n}", lo.T * 1.0)
    return a


class Tok:

    def __init__(self, sem=None, val=None):
        self.sem, self.val, self.used = sem, val, False


class Prog:

    ENG = ("pe", "act", "dve", "pool", "sp")

    def __init__(self, nc, ctx):
        self.nc = nc
        self.q = {e: [] for e in self.ENG}
        self.sem = {e: ctx.enter_context(nc.semaphore("s_" + e)) for e in self.ENG}
        self.last = {e: None for e in self.ENG}

    def op(self, e, fn, after=(), chain=None):
        t = Tok(self.sem[e])
        after = [a for a in flat(after) if a is not None]
        if (chain if chain is not None else e in ("act", "dve", "pool")) and self.last[e] is not None:
            after.append(self.last[e])
        for a in after:
            a.used = True
        self.q[e].append((fn, after, t, 1))
        if fn is not None:
            self.last[e] = t
        return t

    def dma(self, e, fn, sem, val, after=()):
        t = Tok(sem, val)
        after = [a for a in flat(after) if a is not None]
        for a in after:
            a.used = True
        self.q[e].append((fn, after, t, 16))
        return t

    def emit(self, block):
        for e in self.ENG:
            n = 0
            for fn, after, t, inc in self.q[e]:
                if inc == 1 and t.used:
                    n += 1
                    t.val = n
        reg = {"pe": block.tensor, "act": block.scalar, "dve": block.vector, "pool": block.gpsimd, "sp": block.sync}
        for e in self.ENG:
            def body(eng, e=e):
                seen = {}
                for fn, after, t, inc in self.q[e]:
                    need = {}
                    for a in after:
                        if a.val > seen.get(id(a.sem), 0):
                            need[id(a.sem)] = max(need.get(id(a.sem), (0, None))[0], a.val), a.sem
                    for k, (v, s) in need.items():
                        eng.wait_ge(s, v)
                        seen[k] = v
                    ins = fn(eng) if fn is not None else None
                    if ins is not None and (inc == 16 or t.used):
                        ins.then_inc(t.sem, inc)
            reg[e](body)


def flat(x):
    if x is None or isinstance(x, Tok):
        return [x] if x is not None else []
    out = []
    for y in x:
        out += flat(y)
    return out


def build(nc, W, S, K, XI, POS, OUT):
    with ExitStack() as ctx:
        def sb(name, shape, dt=F32):
            return ctx.enter_context(nc.sbuf_tensor(name, shape, dt))

        g = Prog(nc, ctx)
        op = g.op
        order = slot_order()

        ring = sb("ring", [P, RING, SLOT])
        cols = sb("cols", [P, NCOL])
        cons = sb("cons", [P, NCON])
        XT = sb("XT", [P, 8, T])
        HT = sb("HT", [P, 8, T])
        SQ = sb("SQ", [P, 8, T])
        RS = sb("RS", [P, T])
        pos = sb("pos", [P, 2], I32)
        UB = sb("UB", [P, 8, T])
        sg, at = UB[:, 0:4, :], UB[:, 4:8, :]
        small = sb("small", [P, 512])
        AR = sb("AR", [P, NAR])
        ps = ctx.enter_context(nc.psum_tensor("ps", [P, 8, 512], F32))
        wsem = [ctx.enter_context(nc.semaphore(f"w{i}")) for i in range(RING)]
        isem = [ctx.enter_context(nc.semaphore(f"i{i}")) for i in range(5)]
        osem = ctx.enter_context(nc.semaphore("o"))

        def C(n, a=None, b=None):
            o, w = COFF[n]
            a, b = (0, w) if a is None else (a, b)
            return cols[:, o + a:o + b]

        def KC(n, a=None, b=None):
            o, w = KOFF[n]
            a, b = (0, w) if a is None else (a, b)
            return cons[:, o + a:o + b]

        ident = KC("ident")

        t_x = g.dma("act", lambda e: e.dma_start(XT[:, :, :], XI), isem[0], 16)
        t_k = g.dma("act", lambda e: e.dma_start(cons[:, :], K), isem[1], 16)
        t_c = g.dma("act", lambda e: e.dma_start(cols[:, :], S), isem[2], 16)
        t_p = g.dma("act", lambda e: e.dma_start(pos[:, :], POS), isem[3], 16)

        class Slot:
            pass

        st = {"load": 0, "take": 0}
        freed = {}

        def load(after=()):
            n = st["load"]
            if n >= len(order):
                return
            st["load"] += 1
            freed[n] = g.dma("sp", lambda e, n=n: e.dma_start(ring[:, n % RING, :], W[n]),
                             wsem[n % RING], 16 * (n // RING + 1), after)

        for _ in range(RING):
            load()

        def take(key):
            n = st["take"]
            assert order[n] == key, (order[n], key)
            st["take"] += 1
            s = Slot()
            s.t, s.n = freed[n], n
            s.ap = ring[:, n % RING, :]
            return s

        read = {}

        def done(s, tok):
            read[s.n] = tok
            while st["load"] < len(order) and st["load"] - RING in read:
                load([read[st["load"] - RING]])

        def mm(out, lhsT, rhs, start, stop, after=(), skip=False, tr=False):
            if tr:
                return op("pe", lambda e: e.transpose(out, lhsT, rhs), after)
            return op("pe", lambda e: e.matmul(out, lhsT, rhs, start=start, stop=stop, skip_group_check=skip), after)

        def tt(e, out, a, b, o, after=(), chain=None):
            return op(e, lambda q: q.tensor_tensor(out, a, b, o), after, chain)

        def ts(e, out, a, s1, s2, o0, o1=None, after=(), chain=None):
            if o1 is None:
                return op(e, lambda q: q.tensor_scalar(out, a, s1, None, o0), after, chain)
            return op(e, lambda q: q.tensor_scalar(out, a, s1, s2, o0, o1), after, chain)

        def rsq(out, a, after=(), pw=-0.5):
            x = act(out, a, ACT.Sqrt, [after, g.last["dve"]])
            if pw < 0:
                return op("dve", lambda q: q.reciprocal(out, out), [x])
            op("dve", None, [x], chain=False)
            return x

        def stt(out, a, s, b, o0, o1, after=(), chain=None):
            return op("dve", lambda q: q.scalar_tensor_tensor(out=out, in0=a, scalar=s, in1=b, op0=o0, op1=o1), after, chain)

        def act(out, a, f, after=(), chain=None, **kw):
            return op("act", lambda q: q.activation(out, a, f, **kw), after, chain)

        def cp(e, out, a, after=(), chain=None):
            if e == "act":
                return act(out, a, ACT.Copy, after, chain)
            return op(e, lambda q: q.tensor_copy(out, a), after, chain)

        bank = {i: [] for i in range(8)}

        def norm(gain, xtoks, eps, shift=None, gaintok=(), out=HT, bk=7, outfree=()):
            tk = []
            for i in range(4):
                tk.append(act(SQ[:, 2 * i:2 * i + 2, :], XT[:, 2 * i:2 * i + 2, :], ACT.Square, [xtoks, t_k]))
            for k in range(8):
                m = mm(ps[:, bk, 0:T], KC("ones"), SQ[:, k, :], k == 0, k == 7, [tk[k // 2], bank[bk] if k == 0 else ()])
            a = ts("dve", RS[:, :], ps[:, bk, 0:T], 1.0 / D, eps, ALU.mult, ALU.add, [m])
            bank[bk] = [a]
            rsq(RS[:, :], RS[:, :], pw=-0.5)
            r = []
            for k in range(8):
                x = stt(out[:, k, :], XT[:, k, :], gain[:, k:k + 1], RS[:, :], ALU.mult, ALU.mult, [t_c, gaintok, outfree], chain=k == 0)
                if shift is not None:
                    x = ts("dve", out[:, k, :], out[:, k, :], shift[:, k:k + 1], None, ALU.add, after=[gaintok, x])
                r.append(x)
            return r

        def units(tag, n, ht, scale_unit=None):
            pend = None
            last = None
            firstw = [list(bank[b]) for b in range(4)]
            nb = 4 if scale_unit is None else 3

            def down(u, sd, toks, last):
                w = sd.ap.rearrange("p (j n) -> p j n", j=2)
                m = None
                for d in range(8):
                    for j in range(2):
                        first = u == 0 and j == 0 and d % 2 == 0
                        m = mm(ps[:, d // 2, (d % 2) * T:(d % 2) * T + T], w[:, j, d * 128:(d + 1) * 128],
                               at[:, (2 * u + j) % 4, :], first, last and j == 1, [sd.t, toks[j], firstw[d // 2] if first else ()], skip=True)
                done(sd, m)
                return m

            dtok = {}
            for u in range(n):
                sgt, sup = take((tag + "g", u)), take((tag + "u", u))
                sd = take((tag + "d", u))
                wg = sgt.ap.rearrange("p (k n) -> p k n", k=8)
                wu = sup.ap.rearrange("p (k n) -> p k n", k=8)
                toks = []
                cwp = None
                if scale_unit is not None:
                    if u == 0:
                        nextcw = scale_unit(0)
                    cwp = nextcw
                for j in range(2):
                    i = (2 * u + j)
                    b = 4 + i % nb
                    for k in range(8):
                        mg = mm(ps[:, b, 0:T], wg[:, k, j * 128:(j + 1) * 128], HT[:, k, :], k == 0, k == 7,
                                [sgt.t, ht[k], bank[b] if k == 0 else ()])
                    for k in range(8):
                        mu = mm(ps[:, b, T:2 * T], wu[:, k, j * 128:(j + 1) * 128], HT[:, k, :], k == 0, k == 7, [sup.t])
                    si = i % 4
                    a = act(sg[:, si, :], ps[:, b, 0:T], ACT.Silu, [mu, dtok.get(("m", i - 4))], chain=False)
                    x = tt("dve", at[:, si, :], sg[:, si, :], ps[:, b, T:2 * T], ALU.mult,
                           [a, mu, dtok.get(u - 2)], chain=False)
                    dtok[("m", i)] = x
                    bank[b] = [x]
                    if cwp is not None:
                        x = tt("dve", at[:, si, :], at[:, si, :], cwp[0], ALU.mult, [x, cwp[1]])
                        bank[7] = [x]
                    toks.append(x)
                done(sgt, mg)
                done(sup, mu)
                if pend is not None:
                    dtok[pend[0]] = down(*pend, False)
                if scale_unit is not None and u + 1 < n:
                    nextcw = scale_unit(u + 1)
                pend = (u, sd, toks)
            last = down(*pend, True)
            return last

        def ffn(tag, gain, xtoks):
            ht = norm(gain, xtoks, 1e-6)
            m = units(tag, 11, ht)
            r = []
            for b in range(4):
                xv = XT[:, 2 * b:2 * b + 2, :].rearrange("p a t -> p (a t)")
                x = stt(xv, ps[:, b, :], 0.5, xv, ALU.mult, ALU.add, [m], chain=False)
                bank[b] = [x]
                r.append(x)
            return r

        def proj_tok(tag, ncol, Z, ht, free=()):
            r = []
            for gi in range(5):
                w = min(512, ncol - 512 * gi)
                sl = [take((tag, gi, a)) for a in range(2)]
                for th in range(2):
                    b = (2 * gi + th) % 8
                    for k in range(8):
                        s = sl[k // 4]
                        wv = s.ap.rearrange("p (k n) -> p k n", k=4)
                        m = mm(ps[:, b, 0:w], HT[:, k, th * 128:(th + 1) * 128], wv[:, k % 4, 0:w], k == 0, k == 7,
                               [s.t, ht[k], bank[b] if k == 0 else ()])
                    x = cp("act" if th else "dve", Z[:, th, 512 * gi:512 * gi + w], ps[:, b, 0:w], [m, free], chain=False)
                    bank[b] = [x]
                    r.append(x)
                done(sl[0], m)
                done(sl[1], m)
            return r

        def proj_out(tag, O, otoks, xin):
            OT = HT
            tks = {}
            for n in range(4):
                b = n
                for q in range(4):
                    th, k = divmod(4 * n + q, 8)
                    m = mm(ps[:, b, q * 128:(q + 1) * 128], O[:, th, k * 128:(k + 1) * 128], ident, 1, 1,
                           [otoks, bank[b] if q == 0 else ()], tr=True)
                th, k0 = divmod(4 * n, 8)
                x = cp("act" if n % 2 else "dve", OT[:, k0:k0 + 4, th * 128:(th + 1) * 128],
                       ps[:, b, :].rearrange("p (k t) -> p k t", k=4), [m], chain=False)
                bank[b] = [x]
                tks[n] = x
            r = []
            for gi in range(4):
                s = take((tag, gi))
                w = s.ap.rearrange("p (k n) -> p k n", k=8)
                b = 4 + gi
                for j in range(2):
                    for k in range(8):
                        m = mm(ps[:, b, j * T:(j + 1) * T], w[:, k, j * 128:(j + 1) * 128], OT[:, k, :], k == 0, k == 7,
                               [s.t, list(tks.values()), bank[b] if k == 0 and j == 0 else ()])
                done(s, m)
                xv = XT[:, 2 * gi:2 * gi + 2, :].rearrange("p a t -> p (a t)")
                x = tt("dve", xv, ps[:, b, :], xv, ALU.add, [m], chain=False)
                bank[b] = [x]
                r.append(x)
            return r

        posf = small[:, 0:2]
        ang = small[:, 16:32]
        kk_ = small[:, 32:48]
        cosT = small[:, 64:80]
        sinT = small[:, 80:96]
        cp("dve", posf, pos[:, :], [t_p])
        for th in range(2):
            ts("dve", ang[:, th * 8:(th + 1) * 8], KC("inv"), posf[:, th:th + 1], None, ALU.mult, after=[t_k])
        MAGIC = 12582912.0
        ts("dve", kk_, ang, float(1 / (2 * np.pi)), None, ALU.mult)
        ts("dve", kk_, kk_, MAGIC, None, ALU.add)
        ts("dve", kk_, kk_, MAGIC, None, ALU.subtract)
        c1 = 6.28125
        c2 = float(np.float32(np.round((2 * np.pi - c1) * 2 ** 20) / 2 ** 20))
        c3 = float(2 * np.pi - c1 - c2)
        for c in (c1, c2, c3):
            stt(ang, kk_, -c, ang, ALU.mult, ALU.add)
        PI = 3.1415925
        ts("dve", ang, ang, PI, -PI, ALU.min, ALU.max)
        ts("dve", kk_, ang, -1.0, None, ALU.mult)
        tt("dve", kk_, kk_, ang, ALU.max)
        t = ts("dve", kk_, kk_, -1.0, float(np.pi / 2), ALU.mult, ALU.add)
        act(sinT, ang, ACT.Sin, [t])
        t_rope = act(cosT, kk_, ACT.Sin)

        def rope(Z, c0, nh, hd, half, tmp, after):
            zv = Z[:, :, c0:c0 + nh * hd].rearrange("p a (h d) -> p a h d", d=hd)
            x1, x2 = zv[:, :, :, 0:half], zv[:, :, :, half:2 * half]
            step = 8 // half
            sh = [P, 2, nh, half]
            cs = cosT.rearrange("p (a f s) -> p a f s", a=2, s=step)[:, :, :, 0].unsqueeze(2).broadcast_to(sh)
            sn = sinT.rearrange("p (a f s) -> p a f s", a=2, s=step)[:, :, :, 0].unsqueeze(2).broadcast_to(sh)
            n = 2 * nh * half
            t1 = tmp[:, 0:n].rearrange("p (a h f) -> p a h f", a=2, h=nh)
            t2 = tmp[:, n:2 * n].rearrange("p (a h f) -> p a h f", a=2, h=nh)
            tt("dve", t1, x1, sn, ALU.mult, [after, t_rope])
            tt("dve", t2, x2, sn, ALU.mult)
            tt("dve", x1, x1, cs, ALU.mult)
            tt("dve", x2, x2, cs, ALU.mult)
            tt("dve", x1, x1, t2, ALU.subtract)
            return tt("dve", x2, x2, t1, ALU.add)

        evn = [0]

        def ev():
            evn[0] += 1
            return "act" if evn[0] % 2 else "dve"

        def headT(Z, c0, nh, dst, after, banks, hd=64):
            r = []
            jobs = [(th, h) for th in range(2) for h in range(nh)]
            for i in range(0, len(jobs), 4):
                grp = jobs[i:i + 4]
                b = banks[(i // 4) % len(banks)]
                for q, (th, h) in enumerate(grp):
                    m = mm(ps[0:hd, b, q * 128:(q + 1) * 128], Z[:, th, c0 + h * hd:c0 + (h + 1) * hd], ident, 1, 1,
                           [after, bank[b] if q == 0 else ()], tr=True)
                x = cp(ev(), dst.rearrange("d a h t -> d (a h) t")[:, i:i + len(grp), :],
                       ps[0:hd, b, 0:128 * len(grp)].rearrange("d (h t) -> d h t", t=128), [m], chain=False)
                bank[b] = [x]
                r.append(x)
            return r

        def attention(items, SB, PT, stats, maskof, finish):
            n = len(items)
            stage = {}

            def s_stage(i):
                br, th, heads, qT, kT, V, deps = items[i]
                nk = 128 * (th + 1)
                b0 = 2 * (i % 2)
                sview = ps[:, b0:b0 + 2, :].rearrange("p b n -> p (b n)")[:, 0:4 * nk]
                for q, h in enumerate(heads):
                    for kb in range(th + 1):
                        m = mm(sview[:, q * nk + kb * 128:q * nk + kb * 128 + 128], qT(h)[:, th, :], kT(h)[:, kb, :], True, True,
                               [deps, bank[b0] if q == 0 else (), bank[b0 + 1] if q == 0 else ()])
                sbv = SB[:, i % 2, 0:4 * nk].rearrange("p (h k) -> p h k", h=4)
                mk, mt = maskof(br, th)
                mk = mk.unsqueeze(1).broadcast_to([P, 4, nk])
                x = stt(sbv, sview.rearrange("p (h k) -> p h k", h=4), 0.125, mk, ALU.mult, ALU.add,
                        [m, mt, stage.get(("pt", i - 2))])
                bank[b0] = bank[b0 + 1] = [x]
                mx = stats[:, i, 0:4]
                op("dve", lambda e: e.tensor_reduce(mx, sbv, AX.X, ALU.max))
                y = ts("dve", mx, mx, -1.0, None, ALU.mult)
                for q in range(4):
                    z = act(sbv[:, q, :], sbv[:, q, :], ACT.Exp, [y], chain=False, bias=stats[:, i, q:q + 1],
                            accum_out=stats[:, i, 4 + q:5 + q])
                w = op("dve", lambda e: e.reciprocal(stats[:, i, 8:12], stats[:, i, 4:8]), [z])
                stage[("e", i)] = z
                stage[("r", i)] = w

            def o_stage(i):
                br, th, heads, qT, kT, V, deps = items[i]
                nk = 128 * (th + 1)
                sbv = SB[:, i % 2, 0:4 * nk].rearrange("p (h k) -> p h k", h=4)
                ob = 6 + i % 2
                blk = [(q, kb) for q in range(4) for kb in range(th + 1)]
                ptk = []
                for c in range(0, len(blk), 4):
                    b = 4 + (c // 4)
                    for w, (q, kb) in enumerate(blk[c:c + 4]):
                        m = mm(ps[:, b, w * 128:(w + 1) * 128], sbv[:, q, kb * 128:(kb + 1) * 128], ident, 1, 1,
                               [stage[("e", i)], bank[b] if w == 0 else ()], tr=True)
                    x = cp("act" if c else "dve", PT[:, i % 2, c * 128:c * 128 + 512], ps[:, b, :], [m, stage.get(("o", i - 2))], chain=False)
                    bank[b] = [x]
                    ptk.append(x)
                stage[("pt", i)] = m
                for q, h in enumerate(heads):
                    for kb in range(th + 1):
                        w = blk.index((q, kb))
                        m = mm(ps[:, ob, q * 64:(q + 1) * 64], PT[:, i % 2, w * 128:(w + 1) * 128], V(h, kb),
                               kb == 0, kb == th, [ptk, bank[ob] if q == 0 and kb == 0 else ()])
                stage[("o", i)] = m
                x = finish(i, items[i], ps[:, ob, 0:256].rearrange("p (h d) -> p h d", h=4), stats[:, i, 8:12], [m, stage[("r", i)]])
                bank[ob] = [x]
                return x

            s_stage(0)
            for i in range(n):
                if i + 1 < n:
                    s_stage(i + 1)
                last = o_stage(i)
            return last

        def carve():
            at_ = [0]

            def get(n):
                a = at_[0]
                at_[0] += n
                assert at_[0] <= NAR, at_[0]
                return AR[:, a:a + n]
            return get

        xt = ffn("f1_0", C("n1_0"), [t_x])
        ht = norm(C("nm_0"), xt, 1e-6)
        get = carve()
        Z = get(2 * 2468).rearrange("p (a n) -> p a n", a=2)
        O = get(2 * 1024).rearrange("p (a n) -> p a n", a=2)
        zt = proj_tok("evin", 2468, Z, ht)
        QN = get(3072)[0:64, :].rearrange("p (a h t) -> p a h t", a=2, h=12)
        zt_all = zt
        tqn = headT(Z, 512, 12, QN, zt_all, [0, 1])
        kv2 = get(2 * 2 * 192 * 2).rearrange("p (a w h c d) -> p a w h c d", a=2, w=2, h=3, c=2)
        t2 = []
        for a in range(2):
            for w in range(2):
                src = Z[:, a, 1664 + 192 * w:1664 + 192 * (w + 1)].rearrange("p (h d) -> p h d", h=3)
                t2.append(op("pool", lambda e, a=a, w=w, src=src: e.tensor_copy(
                    kv2[:, a, w], src.unsqueeze(2).broadcast_to([P, 3, 2, 64])), [zt_all]))
        kct = get(2 * 3 * T).rearrange("p (w h t) -> p w h t", w=2, h=3)
        ktk = []
        for w in range(2):
            for h in range(3):
                b = 2 + (3 * w + h) % 2
                for a in range(2):
                    m = mm(ps[:, b, a * 128:(a + 1) * 128], kv2[:, a, w, h].rearrange("p c d -> p (c d)"), ident, 1, 1,
                           [t2, bank[b] if a == 0 else ()], tr=True)
                x1 = cp("act", kct[0:64, w, h, :], ps[0:64, b, 0:T], [m], chain=False)
                x2 = cp("dve", kct[64:128, w, h, 0:T - 1], ps[64:128, b, 1:T], [m], chain=False)
                bank[b] = [x1, x2]
                ktk += [x1, x2]
        blk = get(2 * 16 * 45).rearrange("p (w l h n) -> p w l h n", w=2, l=16, h=3)
        btk = []
        for w, pn in enumerate(("pos_k", "pos_v")):
            for h in range(3):
                base = kct[:, w, h, :]
                lo = base.rearrange("p (n l c) -> p l n c", n=16, c=2)[:, 0:8, 0:15, 0]
                hi = base.rearrange("p (n l c) -> p l n c", n=16, c=2)[:, 0:8, 1:16, 0]
                pv = C(pn).unsqueeze(2)
                tt("dve", blk[:, w, 0:8, h, :], lo, pv[:, 0:8].broadcast_to([P, 8, 15]), ALU.add, [ktk, t_c], chain=False)
                btk.append(tt("dve", blk[:, w, 8:16, h, :], hi, pv[:, 8:16].broadcast_to([P, 8, 15]), ALU.add, [ktk], chain=False))
        hid = get(2 * 2 * 45).rearrange("p (w c n) -> p w c n", w=2, c=2)
        htk = []
        for w, tag in enumerate(("cmpk", "cmpv")):
            s0, s1 = take((tag, 0)), take((tag, 1))
            for c in range(2):
                b = 4 + 2 * w + c
                for lp in range(16):
                    s = (s0, s1)[lp // 8]
                    wv = s.ap.rearrange("p (l n) -> p l n", l=8)
                    m = mm(ps[:, b, 0:45], wv[:, lp % 8, c * 128:(c + 1) * 128], blk[:, w, lp].rearrange("p h n -> p (h n)"),
                           lp == 0, lp == 15, [s.t, btk, bank[b] if lp == 0 else ()])
                x = act(hid[:, w, c, :], ps[:, b, 0:45], ACT.Gelu_apprx_tanh, [m])
                bank[b] = [x]
                htk.append(x)
            done(s0, m)
            done(s1, m)
        uv = get(2 * 512).rearrange("p (a n) -> p a n", a=2)
        tuv = act(uv, Z[:, :, 0:512], ACT.Gelu_apprx_tanh, [zt_all])
        KCT = get(48)[0:64, 0:45]
        for c in range(2):
            m = mm(ps[0:64, 4, 0:45], C("w2k", 64 * c, 64 * c + 64), hid[:, 0, c, :], c == 0, c == 1, [htk, bank[4]])
        tkc = cp("dve", KCT, ps[0:64, 4, 0:45], [m])
        bank[4] = [tkc]
        hd = get(2 * 3 * 128).rearrange("p (c g r n) -> p c g r n", c=2, g=3, r=4)
        op("dve", lambda e: e.memset(hd, 0.0))
        for c in range(2):
            thd = op("dve", lambda e, c=c: e.tensor_copy(
                hd[:, c, :, :, 0:15], hid[:, 1, c, :].rearrange("p (g n) -> p g n", g=3).unsqueeze(2).broadcast_to([P, 3, 4, 15])), [htk])
        VB = get(3 * 256).rearrange("p (g r d) -> p g r d", g=3, r=4)
        op("dve", lambda e: e.memset(VB, 0.0))
        for gi in range(3):
            for c in range(2):
                m = mm(ps[:, 5, gi * 64:(gi + 1) * 64], hd[:, c, gi].rearrange("p r n -> p (r n)"), C("w2v", 64 * c, 64 * c + 64),
                       c == 0, c == 1, [thd, bank[5] if c == 0 and gi == 0 else ()])
        for gi in range(3):
            for r in range(4):
                tvb = cp("dve", VB[32 * r:32 * r + 32, gi, r, :], ps[32 * r:32 * r + 32, 5, gi * 64:(gi + 1) * 64], [m])
        bank[5] = [tvb]
        tmp = get(2 * 576)
        trq = rope(Z, 512, 18, 64, 8, tmp, [zt_all, tqn])
        QT = get(3072)[0:64, :].rearrange("p (a h t) -> p a h t", a=2, h=12)
        KT = get(2 * 3 * 2 * 128)[0:64, :].rearrange("p (a h t) -> p a h t", a=2, h=6)
        tq = headT(Z, 512, 12, QT, trq, [0, 1])
        tk = headT(Z, 1280, 6, KT, trq, [2, 3])
        gts = get(72).rearrange("p (a n) -> p a n", a=2)
        tg = act(gts, Z[:, :, 2432:2468], ACT.Sigmoid, [zt_all])
        gv = gts.rearrange("p a (h r) -> p a h r", r=3)
        v = uv[:, :, 256:512]
        ssq = small[:, 100:102]
        for a in range(2):
            op("dve", lambda e, a=a: e.tensor_tensor_reduce(out=SQ[:, a, :], in0=v[:, a, :], in1=v[:, a, :], scale=1.0, scalar=0.0,
                                                            op0=ALU.mult, op1=ALU.add, accum_out=ssq[:, a:a + 1]), [tuv, ht])
        ts("dve", ssq, ssq, 1.0 / 256, 1e-6, ALU.mult, ALU.add)
        rsq(ssq, ssq, pw=-0.5)
        for a in range(2):
            tvn = stt(v[:, a, :], v[:, a, :], ssq[:, a:a + 1], C("sgu_n"), ALU.mult, ALU.mult)
        sw = C("sgu_wT").rearrange("p (g t) -> p g t", g=4)
        tsw = tt("dve", sw, sw, KC("triT").unsqueeze(1).broadcast_to([P, 4, 128]), ALU.mult)
        for a in range(2):
            for gi in range(4):
                m = mm(ps[:, 6 + a, gi * 64:(gi + 1) * 64], sw[:, gi, :], v[:, a, gi * 64:(gi + 1) * 64], True, True,
                       [tvn, tsw, bank[6 + a] if gi == 0 else ()])
            for gi in range(4):
                x = stt(O[:, a, gi * 64:(gi + 1) * 64], ps[:, 6 + a, gi * 64:(gi + 1) * 64], C("sgu_b", gi, gi + 1),
                        uv[:, a, gi * 64:(gi + 1) * 64], ALU.add, ALU.mult, [m], chain=False)
            bank[6 + a] = [x]
        Ob = O[:, :, 256:1024].rearrange("p a (h d) -> p a h d", h=12)
        pc = get(2 * 12 * 32).rearrange("p (a h n) -> p a h n", a=2, h=12)
        op("dve", lambda e: e.memset(pc, 0.0))
        cst = small[:, 128:200].rearrange("p (k a h) -> p k a h", k=3, a=2)
        for a in range(2):
            for h in range(12):
                m = mm(ps[:, 4 + a, h * 15:(h + 1) * 15], QN[:, a, h, :], KCT[:, (h // 4) * 15:(h // 4) * 15 + 15], True, True,
                       [tqn, tkc, bank[4 + a] if h == 0 else ()])
            pv = pc[:, a, :, 0:15]
            ma = KC("cmadd", 15 * a, 15 * a + 15).unsqueeze(1).broadcast_to([P, 12, 15])
            m01 = KC("cm01", 15 * a, 15 * a + 15).unsqueeze(1).broadcast_to([P, 12, 15])
            x = stt(pv, ps[:, 4 + a, 0:180].rearrange("p (h n) -> p h n", h=12), 0.125, ma, ALU.mult, ALU.add, [m])
            bank[4 + a] = [x]
            op("dve", lambda e, a=a, pv=pv: e.tensor_reduce(cst[:, 0, a, :], pv, AX.X, ALU.max))
            x = tt("dve", pv, pv, cst[:, 0, a, :].unsqueeze(2).broadcast_to([P, 12, 15]), ALU.subtract)
            x = act(pv, pv, ACT.Exp, [x])
            op("dve", lambda e, a=a, pv=pv: e.tensor_reduce(cst[:, 1, a, :], pv, AX.X, ALU.add), [x])
            op("dve", lambda e, a=a: e.reciprocal(cst[:, 1, a, :], cst[:, 1, a, :]))
            tt("dve", cst[:, 1, a, :], cst[:, 1, a, :], gv[:, a, :, 0], ALU.mult, [tg])
            tpc = tt("dve", pv, pv, m01, ALU.mult)
        pct = get(2 * 3 * 128).rearrange("p (a g t) -> p a g t", a=2, g=3)
        for a in range(2):
            for gi in range(3):
                m = mm(ps[:, 6 + a, gi * 128:(gi + 1) * 128], pc[:, a, 4 * gi:4 * gi + 4, :].rearrange("p h n -> p (h n)"), ident, 1, 1,
                       [tpc, bank[6 + a] if gi == 0 else ()], tr=True)
            x = cp("act", pct[:, a], ps[:, 6 + a, 0:384].rearrange("p (g t) -> p g t", g=3), [m])
            bank[6 + a] = [x]
            for gi in range(3):
                b = 4 + gi // 2
                m = mm(ps[:, b, (gi % 2) * 256:(gi % 2) * 256 + 256], pct[:, a, gi, :], VB[:, gi].rearrange("p r d -> p (r d)"), True, True,
                       [x, tvb, bank[4], bank[5]])
            ov = ps[:, 4:6, :].rearrange("p b (h d) -> p (b h) d", d=64)[:, 0:12, :]
            x = tt("dve", Ob[:, a], ov, cst[:, 1, a, :].unsqueeze(2).broadcast_to([P, 12, 64]), ALU.mult, [m])
            bank[4] = bank[5] = [x]
        tcmp = x
        SB = SQ[:, :, :].rearrange("p (a b) t -> p a (b t)", a=2)
        PT = HT[:, :, :].rearrange("p (a b) t -> p a (b t)", a=2)
        stats = small[:, 200:344].rearrange("p (i n) -> p i n", n=12)
        otmp = get(256).rearrange("p (h d) -> p h d", h=4)
        items = []
        for br in range(2):
            for th in range(2):
                for gi in range(3):
                    items.append((br, th, [4 * gi + r for r in range(4)],
                                  lambda h: QT[:, :, h, :],
                                  lambda h, br=br: KT[:, :, 3 * br + h // 4, :],
                                  lambda h, kb, br=br: Z[:, kb, 2048 + 192 * br + 64 * (h // 4):2048 + 192 * br + 64 * (h // 4) + 64],
                                  [tq, tk, zt_all]))

        def fin_even(i, item, o, r, after):
            br, th, heads = item[0], item[1], item[2]
            tt("dve", r, r, gv[:, th, heads[0]:heads[0] + 4, 1 + br], ALU.mult, after)
            y = tt("dve", otmp, o, r.unsqueeze(2).broadcast_to([P, 4, 64]), ALU.mult)
            z = Ob[:, th, heads[0]:heads[0] + 4, :]
            fin_last[0] = tt("dve", z, z, otmp, ALU.add)
            return y

        fin_last = [None]
        attention(items, SB, PT, stats, lambda br, th: (KC("madd%d" % th), t_k), fin_even)
        xt = proj_out("evout", O, [fin_last[0]], xt)
        xt = ffn("f2_0", C("n2_0"), xt)

        xt = ffn("f1_1", C("n1_1"), xt)
        ht = norm(C("nm_1"), xt, 1e-6)
        get = carve()
        Z = get(2 * 2340).rearrange("p (a n) -> p a n", a=2)
        O = get(2 * 1024).rearrange("p (a n) -> p a n", a=2)
        zt = proj_tok("odin", 2340, Z, ht)
        tmp = get(2 * 800)
        r1 = rope(Z, 2176, 5, 32, 4, tmp, zt)
        tmp2 = tmp
        r2 = rope(Z, 0, 25, 64, 8, tmp2, zt)
        IT = get(2 * 5 * 128)[0:32, :].rearrange("p (a h t) -> p a h t", a=2, h=5)
        ti = headT(Z, 2176, 5, IT, r1, [0, 1], hd=32)
        QT = get(2 * 17 * 128)[0:64, :].rearrange("p (a h t) -> p a h t", a=2, h=17)
        tq = headT(Z, 0, 17, QT, r2, [2, 3])
        KT = get(2 * 8 * 128)[0:64, :].rearrange("p (a h t) -> p a h t", a=2, h=8)
        tk = headT(Z, 1088, 8, KT, r2, [4, 5])
        wi = small[:, 104:112].rearrange("p (a h) -> p a h", a=2)
        twi = ts("dve", wi, Z[:, :, 2336:2340], 0.5, None, ALU.mult)
        MS = get(384)
        wk = get(256)
        rl = get(1024)
        m8 = small[:, 112:120]
        mtok = []
        for th in range(2):
            nk = 128 * (th + 1)
            for h in range(4):
                b = 6 + h // 2
                for kb in range(th + 1):
                    m = mm(ps[:, b, (h % 2) * nk + kb * 128:(h % 2) * nk + kb * 128 + 128], IT[:, th, h, :], IT[:, kb, 4, :], True, True,
                           [ti, bank[6], bank[7]])
            rv = rl[:, 0:4 * nk].rearrange("p (b n) -> p b n", b=2)
            x = ts("dve", rv, ps[:, 6:8, 0:2 * nk], float(32 ** -0.5), 0.0, ALU.mult, ALU.max, after=[m])
            bank[6] = bank[7] = [x]
            rh = rl[:, 0:4 * nk].rearrange("p (h n) -> p h n", h=4)
            ms = MS[:, 0:128] if th == 0 else MS[:, 128:384]
            w_ = wk[:, 0:nk]
            ts("dve", w_, rh[:, 0, :], wi[:, th, 0:1], None, ALU.mult)
            for h in range(1, 4):
                stt(w_, rh[:, h, :], wi[:, th, h:h + 1], w_, ALU.mult, ALU.add)
            tt("dve", w_, w_, KC("madd%d" % th), ALU.add)
            for r in range(8):
                op("dve", lambda e, w_=w_: e.max(m8, w_))
                op("dve", lambda e, w_=w_: e.match_replace(w_, m8, w_, -3e38))
            ts("dve", ms, w_, -2e38, NEG, ALU.is_gt, ALU.mult)
            mtok.append(tt("dve", ms, ms, KC("madd%d" % th), ALU.add))
        SB = SQ[:, :, :].rearrange("p (a b) t -> p a (b t)", a=2)
        PT = HT[:, :, :].rearrange("p (a b) t -> p a (b t)", a=2)
        items = []
        for br in (1, 0):
            for th in range(2):
                for gi in range(2):
                    heads = [4 * gi + r for r in range(4)]
                    if br == 0:
                        items.append((0, th, heads, lambda h: QT[:, :, h, :], lambda h: QT[:, :, 8, :],
                                      lambda h, kb: Z[:, kb, 1600:1664], [tq, zt]))
                    else:
                        items.append((1, th, heads, lambda h: QT[:, :, 9 + h, :], lambda h: KT[:, :, h, :],
                                      lambda h, kb: Z[:, kb, 1664 + 64 * h:1728 + 64 * h], [tq, tk, zt]))
        Oh = O.rearrange("p a (h d) -> p a h d", d=64)

        def fin_odd(i, item, o, r, after):
            br, th, heads = item[0], item[1], item[2]
            h0 = heads[0] + 8 * br
            fin_last[0] = tt("dve", Oh[:, th, h0:h0 + 4, :], o, r.unsqueeze(2).broadcast_to([P, 4, 64]), ALU.mult, after)
            return fin_last[0]

        attention(items, SB, PT, stats,
                  lambda br, th: (KC("madd%d" % th), t_k) if br else ((MS[:, 0:128] if th == 0 else MS[:, 128:384]), mtok), fin_odd)
        xt = proj_out("odout", O, [fin_last[0]], xt)
        xt = ffn("f2_1", C("n2_1"), xt)

        xt = norm(C("nf"), xt, 1e-6, out=XT)
        MOD = small[:, 344:408]
        cs = small[:, 408:416]
        t0 = act(cs, C("c"), ACT.Silu, [t_c])
        for gi in range(32):
            s = take(("ada", gi))
            w = s.ap.rearrange("p (k n) -> p k n", k=8)
            for j in range(2):
                for k in range(8):
                    m = mm(ps[:, 6, 2 * gi + j:2 * gi + j + 1], w[:, k, j * 128:(j + 1) * 128], cs[:, k:k + 1], k == 0, k == 7,
                           [s.t, t0, bank[6] if gi == 0 and j == 0 and k == 0 else ()])
            done(s, m)
        tmod = tt("dve", MOD, ps[:, 6, 0:64], C("b_ada"), ALU.add, [m])
        bank[6] = [tmod]
        gm = small[:, 416:440]
        for n, (gn, o) in enumerate((("g_mix", 8), ("g_ffn", 32), ("g_final", 56))):
            tgm = stt(gm[:, 8 * n:8 * n + 8], MOD[:, o:o + 8], 1.0, C(gn), ALU.add, ALU.mult)
        ht = norm(gm[:, 0:8], xt, 1e-6, shift=MOD[:, 0:8], gaintok=[tgm, tmod])
        get = carve()
        RKV = get(12 * T).rearrange("p (c t) -> p c t", c=12)
        XG = get(8 * T + 12)
        XB = XG[:, 0:4 * (T + 3)].rearrange("p (c t) -> p c t", c=4)
        GB = XG[:, 4 * (T + 3):8 * T + 12].rearrange("p (c t) -> p c t", c=4)
        SG = get(16 * T).rearrange("p (c t) -> p c t", c=16)
        tz = op("pool", lambda e: e.memset(XB[:, :, 0:3], 0.0), [xt])
        pj = []
        for gi in range(18):
            s = take(("win2", gi))
            w = s.ap.rearrange("p (k n) -> p k n", k=8)
            b = gi % 4
            for j in range(2):
                for k in range(8):
                    m = mm(ps[:, b, j * T:(j + 1) * T], w[:, k, j * 128:(j + 1) * 128], HT[:, k, :], k == 0, k == 7,
                           [s.t, ht[k], bank[b] if k == 0 and j == 0 else ()])
            done(s, m)
            c = 2 * gi
            pv = ps[:, b, :].rearrange("p (c t) -> p c t", c=2)
            if c < 12:
                x = cp("dve", RKV[:, c:c + 2, :], pv, [m], chain=False)
            elif c < 16:
                x = cp("dve", XB[:, c - 12:c - 10, 3:T + 3], pv, [m], chain=False)
            elif c < 20:
                x = act(GB[:, c - 16:c - 14, :], pv, ACT.Gelu_apprx_tanh, [m], chain=False)
            else:
                x = act(SG[:, c - 20:c - 18, :], pv, ACT.Sigmoid, [m], chain=False)
            bank[b] = [x]
            pj.append(x)
        DX = SQ
        xm = get(8 * T).rearrange("p (c t) -> p c t", c=8)
        tt("dve", DX[:, :, 1:T], HT[:, :, 0:T - 1], HT[:, :, 1:T], ALU.subtract, [ht])
        tdx = ts("dve", DX[:, :, 0:1], HT[:, :, 0:1], -1.0, None, ALU.mult, chain=False)
        LW = get(4 * T).rearrange("p (c t) -> p c t", c=4)
        AI = get(4 * T).rearrange("p (c t) -> p c t", c=4)
        GG_ = get(4 * T).rearrange("p (c t) -> p c t", c=4)
        lr = get(T)
        free = None
        outs = {}
        for n, (w1n, w2n, r, dst) in enumerate((("lw1", "lw2", 64, LW), ("la1", "la2", 64, AI), ("lg1", "lg2", 128, GG_))):
            tk_ = []
            for k in range(8):
                tk_.append(stt(xm[:, k, :], DX[:, k, :], C("mu_wag", 8 * n + k, 8 * n + k + 1), HT[:, k, :], ALU.mult, ALU.add,
                               [free, tdx], chain=False))
            for k in range(8):
                m = mm(ps[0:r, 4, 0:T], C(w1n, r * k, r * k + r), xm[:, k, :], k == 0, k == 7, [tk_[k], bank[4] if k == 0 else ()])
            free = m
            f = {0: ACT.Tanh, 1: ACT.Copy, 2: ACT.Sigmoid}[n]
            x = act(lr[0:r, :], ps[0:r, 4, 0:T], f, [m, outs.get("m")])
            bank[4] = [x]
            for c in range(4):
                b = 5 + c // 2
                m = mm(ps[:, b, (c % 2) * T:(c % 2) * T + T], C(w2n, 128 * c, 128 * c + 128)[0:r, :], lr[0:r, :], True, True,
                       [x, bank[b] if c % 2 == 0 else ()])
            outs["m"] = m
            for c in range(4):
                b = 5 + c // 2
                src = ps[:, b, (c % 2) * T:(c % 2) * T + T]
                if n == 0:
                    x = act(dst[:, c, :], src, ACT.Sigmoid, [m, t_c], bias=C("w0", c, c + 1))
                elif n == 1:
                    x = act(dst[:, c, :], src, ACT.Sigmoid, [m, t_c], bias=C("a0", c, c + 1))
                else:
                    x = cp("act", dst[:, c, :], src, [m])
                bank[b] = [x]
            outs[n] = x
        sp = small[:, 440:472].rearrange("p (n c) -> p n c", c=4)
        lam = C("lam")
        ts("dve", sp[:, 0], lam, -1.0, None, ALU.mult, after=[t_c])
        tt("dve", sp[:, 1], sp[:, 0], lam, ALU.max)
        x = ts("dve", sp[:, 0], sp[:, 0], 0.0, None, ALU.max)
        x = act(sp[:, 2], sp[:, 1], ACT.Exp, [x], scale=-1.0)
        ts("dve", sp[:, 3], sp[:, 2], 2.0, None, ALU.add, after=[x])
        op("dve", lambda e: e.reciprocal(sp[:, 3], sp[:, 3]))
        tt("dve", sp[:, 3], sp[:, 3], sp[:, 2], ALU.mult)
        tt("dve", sp[:, 4], sp[:, 3], sp[:, 3], ALU.mult)
        ts("dve", sp[:, 5], sp[:, 4], 1.0 / 17, 1.0 / 15, ALU.mult, ALU.add)
        for d in (13, 11, 9, 7, 5, 3, 1):
            tt("dve", sp[:, 5], sp[:, 5], sp[:, 4], ALU.mult)
            ts("dve", sp[:, 5], sp[:, 5], 1.0 / d, None, ALU.add)
        tt("dve", sp[:, 5], sp[:, 5], sp[:, 3], ALU.mult)
        stt(sp[:, 5], sp[:, 5], 2.0, sp[:, 0], ALU.mult, ALU.add)
        tsp = ts("dve", sp[:, 6], sp[:, 5], -8.0, None, ALU.mult)
        XC = get(4 * T).rearrange("p (c t) -> p c t", c=4)
        for c in range(4):
            ts("dve", XC[:, c, :], XB[:, c, 0:T], C("conv_w", 4 * c, 4 * c + 1), C("conv_b", c, c + 1), ALU.mult, ALU.add, after=[pj, tz])
            for j in range(1, 4):
                txc = stt(XC[:, c, :], XB[:, c, j:T + j], C("conv_w", 4 * c + j, 4 * c + j + 1), XC[:, c, :], ALU.mult, ALU.add)
        GR, GI = xm[:, 0:4, :], xm[:, 4:8, :]
        for wn, bn, dst in (("wr", "b_r", GR), ("wi", "b_i", GI)):
            for c in range(4):
                b = c // 2
                m = mm(ps[:, b, (c % 2) * T:(c % 2) * T + T], C(wn, 128 * c, 128 * c + 128), XC[:, c, :], True, True,
                       [txc, bank[b] if c % 2 == 0 else ()])
            for c in range(4):
                b = c // 2
                tgr = act(dst[:, c, :], ps[:, b, (c % 2) * T:(c % 2) * T + T], ACT.Sigmoid, [m, free], bias=C(bn, c, c + 1))
                bank[b] = [tgr]
        for c in range(4):
            x = ts("dve", GR[:, c, :], GR[:, c, :], sp[:, 6, c:c + 1], None, ALU.mult, after=[tgr, tsp])
        x = act(GR, GR, ACT.Tanh, [x])
        A_, U_ = XB[:, :, 0:T], RKV
        B_ = DX[:, 0:4, :]
        ts("dve", B_, GR, -1.0, 1.0, ALU.mult, ALU.add, after=[x, free])
        op("dve", lambda e: e.reciprocal(B_, B_))
        stt(A_, GR, 1.0, B_, ALU.add, ALU.mult)
        rsq(A_, A_, pw=0.5)
        stt(GR, GR, -2.0, B_, ALU.mult, ALU.mult)
        rsq(GR, GR, pw=0.5)
        tt("dve", GI, GI, XC, ALU.mult)
        tt("dve", GR, GR, GI, ALU.mult)
        for c in range(4):
            op("dve", lambda e, c=c: e.tensor_tensor_scan(XC[:, c, :], A_[:, c, :], GR[:, c, :], 0.0, ALU.mult, ALU.add))
        YB = GB
        tyb = tt("dve", YB, XC, GB, ALU.mult)
        MG = HT

        def proj_p(tag, Y, ytok, half, acc, b0):
            for gi in range(2):
                s = take((tag, gi))
                w = s.ap.rearrange("p (k n) -> p k n", k=4)
                for j in range(4):
                    b = b0 + j // 2
                    for k in range(4):
                        m = mm(ps[:, b, (j % 2) * T:(j % 2) * T + T], w[:, k, j * 128:(j + 1) * 128], Y[:, k, :], k == 0, k == 3,
                               [s.t, ytok, bank[b] if k == 0 and j % 2 == 0 else ()])
                    if j % 2 == 1:
                        c = 4 * gi + j - 1
                        pv = ps[:, b, :].rearrange("p (c t) -> p c t", c=2)
                        sgv = SG[:, half + c:half + c + 2, :]
                        if not acc:
                            x = tt("dve", MG[:, c:c + 2, :], sgv, pv, ALU.mult, [m, free, ht])
                            bank[b] = [x]
                        else:
                            x = tt("dve", sgv, sgv, pv, ALU.mult, [m])
                            bank[b] = [x]
                            x = tt("dve", MG[:, c:c + 2, :], MG[:, c:c + 2, :], sgv, ALU.add)
                done(s, m)
            return x

        proj_p("pb", YB, tyb, 8, False, 0)

        d4 = DX[:, 4:8, :]
        for q in range(3):
            X = RKV[:, 4 * q:4 * q + 4, :]
            tt("dve", d4[:, :, 1:T], X[:, :, 0:T - 1], X[:, :, 1:T], ALU.subtract, [pj])
            ts("dve", d4[:, :, 0:1], X[:, :, 0:1], -1.0, None, ALU.mult)
            for c in range(4):
                x = stt(X[:, c, :], d4[:, c, :], C("mu_rkv", 4 * q + c, 4 * q + c + 1), X[:, c, :], ALU.mult, ALU.add)
        Rr, Kr, Vr = RKV[:, 0:4, :], RKV[:, 4:8, :], RKV[:, 8:12, :]
        KKn = xm[:, 0:4, :]
        for c in range(4):
            ts("dve", KKn[:, c, :], Kr[:, c, :], C("k_k", c, c + 1), None, ALU.mult)
        x = tt("dve", d4, KKn, KKn, ALU.mult)
        for c in range(4):
            m = mm(ps[:, 4 + c // 2, (c % 2) * T:(c % 2) * T + T], KC("bones"), d4[:, c, :], True, True, [x, bank[4 + c // 2] if c % 2 == 0 else ()])
        pv = ps[:, 4:6, :].rearrange("p b (c t) -> p (b c) t", c=2)
        x = ts("dve", d4, pv, 1e-12, None, ALU.add, after=[m, outs[2]])
        bank[4] = bank[5] = [x]
        rsq(d4, d4)
        tt("dve", KKn, KKn, d4, ALU.mult)
        for c in range(4):
            ts("dve", d4[:, c, :], AI[:, c, :], 1.0, C("k_a", c, c + 1), ALU.subtract, ALU.mult)
        stt(Kr, d4, 1.0, Kr, ALU.add, ALU.mult)
        for c in range(4):
            x = stt(d4[:, c, :], Rr[:, c, :], C("r_k", c, c + 1), Kr[:, c, :], ALU.mult, ALU.mult)
        for c in range(4):
            m = mm(ps[:, 4 + c // 2, (c % 2) * T:(c % 2) * T + T], KC("bones"), d4[:, c, :], True, True, [x, bank[4 + c // 2] if c % 2 == 0 else ()])
        BN = XC
        x = tt("dve", BN, pv, Vr, ALU.mult, [m])
        bank[4] = bank[5] = [x]
        ts("dve", LW, LW, -float(np.exp(-0.5)), None, ALU.mult, after=[outs[0]])
        CU = DX[:, 0:4, :]
        for c in range(4):
            op("dve", lambda e, c=c: e.tensor_tensor_scan(CU[:, c, :], KC("seg"), LW[:, c, :], 0.0, ALU.mult, ALU.add))
        x = tt("dve", LW, CU, LW, ALU.subtract)
        PP = xm[:, 4:8, :]
        te = act(LW, LW, ACT.Exp, [x])
        te = act(PP, CU, ACT.Exp)
        te = act(CU, CU, ACT.Exp, scale=-1.0)
        GXt = get(8 * T).rearrange("p (c j w t) -> p c j w t", c=4, j=2, w=2)
        KKj = KKn.rearrange("p c (j t) -> p c j t", j=2)
        for c in range(4):
            stt(GXt[:, c, :, 0, :], KKj[:, c], -1.0, LW[:, c, :].rearrange("p (j t) -> p j t", j=2), ALU.mult, ALU.mult, [te])
            tt("dve", GXt[:, c, :, 1, :], Rr[:, c, :].rearrange("p (j t) -> p j t", j=2), PP[:, c, :].rearrange("p (j t) -> p j t", j=2), ALU.mult)
        BT = AI
        tt("dve", BT, KKn, AI, ALU.mult, [outs[1]])
        tt("dve", BT, BT, CU, ALU.mult)
        KTt = Kr
        tk_ = tt("dve", KTt, Kr, CU, ALU.mult)
        PPe = small[:, 472:488].rearrange("p (q c) -> p q c", q=4)
        for q in range(4):
            tpe = cp("dve", PPe[:, q, :], PP[:, :, 64 * q + 63])
        TM = {}
        tmt = {}
        spaces = [LW, xm[:, 0:4, :], xm[:, 4:8, :], DX[:, 0:4, :]]
        srcs = {"b": lambda c, j: BT[:, c, 128 * j:128 * j + 128], "k": lambda c, j: KTt[:, c, 128 * j:128 * j + 128],
                "a": lambda c, j: GXt[:, c, j, 0, :], "v": lambda c, j: Vr[:, c, 128 * j:128 * j + 128]}
        for n, nm in enumerate(("b", "k", "a", "v")):
            dst = spaces[n].rearrange("p c t -> p (c t)").rearrange("p (j c t) -> p j c t", j=2, c=4)
            TM[nm] = dst
            tmt[nm] = []
            for j in range(2):
                b = 4 + (2 * n + j) % 4
                for c in range(4):
                    m = mm(ps[:, b, c * 128:(c + 1) * 128], srcs[nm](c, j), ident, 1, 1, [tpe, tk_, bank[b] if c == 0 else ()], tr=True)
                x = cp("dve", dst[:, j], ps[:, b, :].rearrange("p (c t) -> p c t", c=4), [m])
                bank[b] = [x]
                tmt[nm].append(x)
        SA = d4.rearrange("p c t -> p (c t)").rearrange("p (j h v) -> p j h v", j=2, h=8)
        UT = Rr.rearrange("p c t -> p (c t)").rearrange("p (q c v) -> p q c v", q=4, c=4)
        GM = get(16 * 512).rearrange("p (i n) -> p i n", i=16)
        tG = {}
        for h in range(8):
            r0, c = 64 * (h % 2), h // 2
            for j in range(2):
                i = 2 * h + j
                b = (i // 2) % 2 * 2 + (h % 2) + 4 * (j)
                rr = GXt[r0:r0 + 64, c, j].rearrange("p w t -> p (w t)")
                mm(ps[:, b, 0:256], BT[r0:r0 + 64, c, 128 * j:128 * j + 128], rr, True, True, [tk_, tmt["v"], bank[b]])
                m = mm(ps[:, b, 256:512], KTt[r0:r0 + 64, c, 128 * j:128 * j + 128], rr, True, True)
                x = tt("dve", GM[:, i, :], ps[:, b, :], KC("gmask"), ALU.mult, [m], chain=False)
                bank[b] = [x]
                tG[i] = x
        gall = list(tG.values())
        TN = XG[:, 0:2048].rearrange("p (i t) -> p i t", i=16)
        TTt = RKV[:, 4:12, :].rearrange("p c t -> p (c t)").rearrange("p (i t) -> p i t", i=16)
        XX = UB[:, :, :].rearrange("p c t -> p (c t)").rearrange("p (i t) -> p i t", i=16)
        x1 = op("dve", lambda e: e.tensor_copy(TN, ident.unsqueeze(1).broadcast_to([P, 16, 128])), gall)
        x2 = op("dve", lambda e: e.tensor_copy(TTt, ident.unsqueeze(1).broadcast_to([P, 16, 128])))
        l0 = KC("lv0").bitcast(U32)
        t0m = KC("lt0").bitcast(U32)
        tT = {}
        for q in range(4):
            b = q
            for w in range(4):
                i = 4 * q + w
                m = mm(ps[:, b, w * 128:(w + 1) * 128], GM[:, i, 0:128], ident, True, True, [x2, bank[b] if w == 0 else ()])
            op("dve", lambda e, q=q: e.copy_predicated(TTt[:, 4 * q:4 * q + 4, :], t0m.unsqueeze(1).broadcast_to([P, 4, 128]),
                                                       GM[:, 4 * q:4 * q + 4, 0:128]))
            x = op("dve", lambda e, q=q, b=b: e.copy_predicated(
                TN[:, 4 * q:4 * q + 4, :], l0.unsqueeze(1).broadcast_to([P, 4, 128]), ps[:, b, :].rearrange("p (w t) -> p w t", w=4)), [m])
            bank[b] = [x]
            tT[q] = x
        for n in range(1, 6):
            lv = KC(f"lv{n}").bitcast(U32).unsqueeze(1).broadcast_to([P, 4, 128])
            lt = KC(f"lt{n}").bitcast(U32).unsqueeze(1).broadcast_to([P, 4, 128])
            tx = {}
            for q in range(4):
                b = q
                for w in range(4):
                    i = 4 * q + w
                    m = mm(ps[:, b, w * 128:(w + 1) * 128], GM[:, i, 0:128], TN[:, i, :], True, True, [tT[q], bank[b] if w == 0 else ()])
                tx[q] = cp("act", XX[:, 4 * q:4 * q + 4, :], ps[:, b, :].rearrange("p (w t) -> p w t", w=4), [m])
                bank[b] = [tx[q]]
            for q in range(4):
                b1, b2 = 4 + (2 * q) % 4, 4 + (2 * q + 1) % 4
                for w in range(4):
                    i = 4 * q + w
                    m2 = mm(ps[:, b2, w * 128:(w + 1) * 128], XX[:, i, :], TTt[:, i, :], True, True, [tx[q], bank[b2] if w == 0 else ()])
                m1 = None
                if n < 5:
                    for w in range(4):
                        i = 4 * q + w
                        m1 = mm(ps[:, b1, w * 128:(w + 1) * 128], TTt[:, i, :], XX[:, i, :], True, True, [tx[q], bank[b1] if w == 0 else ()])
                x = op("dve", lambda e, q=q, b2=b2, lt=lt: e.copy_predicated(
                    TTt[:, 4 * q:4 * q + 4, :], lt, ps[:, b2, :].rearrange("p (w t) -> p w t", w=4)), [m2, m1])
                bank[b2] = [x]
                if n < 5:
                    x = op("dve", lambda e, q=q, b1=b1, lv=lv: e.copy_predicated(
                        TN[:, 4 * q:4 * q + 4, :], lv, ps[:, b1, :].rearrange("p (w t) -> p w t", w=4)), [m1])
                    bank[b1] = [x]
                tT[q] = x
        AV = TN[:, 0:8, :].rearrange("p n t -> p (n t)").rearrange("p (i v) -> p i v", i=16)
        for i in range(16):
            h, j = divmod(i, 2)
            b = i // 8
            m = mm(ps[:, b, (i % 8) * 64:(i % 8) * 64 + 64], GM[:, i, 256:384], TM["v"][:, j, h // 2, 64 * (h % 2):64 * (h % 2) + 64], True, True,
                   [tT[3], tmt["v"], bank[b] if i % 8 == 0 else ()])
        for b in range(2):
            tav = cp("dve", AV[:, 8 * b:8 * b + 8, :], ps[:, b, :].rearrange("p (i v) -> p i v", i=8), [m])
            bank[b] = [tav]
        WT = XX[:, 0:8, :].rearrange("p (c j) t -> p c j t", c=4)
        for i in range(16):
            h, j = divmod(i, 2)
            r0, c = 64 * (h % 2), h // 2
            b = 2 + c // 2
            o = ((c % 2) * 2 + j) * 128
            m = mm(ps[r0:r0 + 64, b, o:o + 128], TM["a"][:, j, c, r0:r0 + 64], TTt[:, i, :], True, True,
                   [tT[0], tT[1], tT[2], tT[3], tmt["a"], bank[b] if i % 8 == 0 else ()], skip=True)
        for b in range(2):
            twt = cp("dve", WT[:, 2 * b:2 * b + 2], ps[:, 2 + b, :].rearrange("p (c j t) -> p c j t", c=2, j=2), [m])
            bank[2 + b] = [twt]
        tu = None
        tsa = {}
        for q in range(4):
            j, b0 = q // 2, 64 * (q % 2)
            for h in range(8):
                r0, c = 64 * (h % 2), h // 2
                bb = 4 + h % 2
                o = c * 64
                if q:
                    mm(ps[b0:b0 + 64, bb, o:o + 64], WT[r0:r0 + 64, c, j, b0:b0 + 64], UT[r0:r0 + 64, q, c, :], True, False,
                       [tu, twt, bank[bb]], skip=True)
                m = mm(ps[b0:b0 + 64, bb, o:o + 64], TTt[:, 2 * h + j, b0:b0 + 64], AV[:, 2 * h + j, :], q == 0, True,
                       [tav, twt, bank[bb]], skip=True)
            for pr in range(2):
                x = cp("dve", SA[b0:b0 + 64, j, :, :].rearrange("p (c r) v -> p c r v", r=2)[:, :, pr, :],
                       ps[b0:b0 + 64, 4 + pr, 0:256].rearrange("p (c v) -> p c v", c=4), [m])
                bank[4 + pr] = [x]
            tsa[q] = x
            if q < 3:
                for h in range(8):
                    r0, c = 64 * (h % 2), h // 2
                    o = c * 64
                    mm(ps[r0:r0 + 64, 6, o:o + 64], TM["k"][b0:b0 + 64, j, c, r0:r0 + 64], TM["v"][b0:b0 + 64, j, c, r0:r0 + 64], True, False,
                       [tmt["v"], tmt["k"], tmt["b"], bank[6]], skip=True)
                    m = mm(ps[r0:r0 + 64, 6, o:o + 64], TM["b"][b0:b0 + 64, j, c, r0:r0 + 64], SA[b0:b0 + 64, j, h, :], False, True, [x], skip=True)
                src = ps[:, 6, 0:256].rearrange("p (c v) -> p c v", c=4)
                un = UT[:, q + 1]
                if q:
                    x = tt("dve", un, src, UT[:, q], ALU.add, [m])
                    bank[6] = [x]
                    tu = tt("dve", un, un, PPe[:, q, :].unsqueeze(2).broadcast_to([P, 4, 64]), ALU.mult)
                else:
                    tu = tt("dve", un, src, PPe[:, q, :].unsqueeze(2).broadcast_to([P, 4, 64]), ALU.mult, [m])
                    bank[6] = [tu]
        for h in range(8):
            r0, c = 64 * (h % 2), h // 2
            b = 2 * (h % 2) + c // 2
            for j in range(2):
                o = (c % 2) * T + j * 128
                out = ps[r0:r0 + 64, b, o:o + 128]
                i = 2 * h + j
                mm(out, TM["v"][:, j, c, r0:r0 + 64], GM[:, i, 384:512], True, False, [tsa[3], tu, bank[b]], skip=True)
                m = mm(out, SA[:, j, h, :], GM[:, i, 128:256], False, j == 0 and False, [], skip=True)
                for qq in (2 * j, 2 * j + 1):
                    if qq == 0:
                        continue
                    m = mm(ps[r0:r0 + 64, b, o + 64 * (qq % 2):o + 64 * (qq % 2) + 64], UT[r0:r0 + 64, qq, c, :],
                           GXt[r0:r0 + 64, c, j, 1, 64 * (qq % 2):64 * (qq % 2) + 64], False, True, [], skip=True)
        Y = RKV[:, 0:4, :]
        for pr in range(2):
            x = cp("dve", Y[64 * pr:64 * pr + 64], ps[64 * pr:64 * pr + 64, 2 * pr:2 * pr + 2, :].rearrange("p b (c t) -> p (b c) t", c=2), [m])
            bank[2 * pr] = bank[2 * pr + 1] = [x]
        Y2 = RKV[:, 4:8, :]

        def headsum(src, after, b0=4):
            for c in range(4):
                m = mm(ps[:, b0 + c // 2, (c % 2) * T:(c % 2) * T + T], KC("bones"), src[:, c, :], True, True, [after, bank[b0 + c // 2] if c % 2 == 0 else ()])
            return m

        m = headsum(Y, [x])
        x = stt(Y, pv, -1.0 / 64, Y, ALU.mult, ALU.add, [m])
        bank[4] = bank[5] = [x]
        x = tt("dve", Y2, Y, Y, ALU.mult)
        m = headsum(Y2, [x])
        x = ts("dve", Y2, pv, 1.0 / 64, 64e-5, ALU.mult, ALU.add, after=[m])
        bank[4] = bank[5] = [x]
        rsq(Y2, Y2, pw=-0.5)
        tt("dve", Y, Y, Y2, ALU.mult)
        for c in range(4):
            ts("dve", Y[:, c, :], Y[:, c, :], C("lnx_g", c, c + 1), C("lnx_b", c, c + 1), ALU.mult, ALU.add)
        tt("dve", Y, Y, BN, ALU.add)
        tya = tt("dve", Y, Y, GG_, ALU.mult, [outs[2]])
        tmg = proj_p("pa", Y, tya, 0, True, 6)
        r = []
        for gi in range(4):
            s = take(("wout2", gi))
            w = s.ap.rearrange("p (k n) -> p k n", k=8)
            b = gi
            for jj in range(2):
                for k in range(8):
                    m = mm(ps[:, b, jj * T:(jj + 1) * T], w[:, k, jj * 128:(jj + 1) * 128], MG[:, k, :], k == 0, k == 7,
                           [s.t, tmg, bank[b] if k == 0 and jj == 0 else ()])
            done(s, m)
            for jj in range(2):
                c = 2 * gi + jj
                x = stt(XT[:, c, :], ps[:, b, jj * T:(jj + 1) * T], MOD[:, 16 + c:17 + c], XT[:, c, :], ALU.mult, ALU.add, [m], chain=False)
            bank[b] = [x]
            r.append(x)
        xt = r
        ht = norm(gm[:, 8:16], xt, 1e-6, shift=MOD[:, 24:32], gaintok=[tgm], outfree=[m])
        get = carve()
        LG = get(2 * 36).rearrange("p (a n) -> p a n", a=2)
        for th in range(2):
            for k in range(8):
                m = mm(ps[:, 4 + th, 0:36], HT[:, k, th * 128:(th + 1) * 128], C("wre", 36 * k, 36 * k + 36), k == 0, k == 7,
                       [ht[k], bank[4 + th] if k == 0 else ()])
        x = tt("dve", LG, ps[:, 4:6, 0:36], C("bre").unsqueeze(1).broadcast_to([P, 2, 36]), ALU.add, [m])
        bank[4] = bank[5] = [x]
        st8 = get(32 * 2).rearrange("p (n a) -> p n a", a=2)
        gsel = get(8).rearrange("p (a g) -> p a g", a=2)
        le = LG[:, :, 4:36].rearrange("p a (g e) -> p a g e", g=4)
        lg = LG[:, :, 0:4]
        op("dve", lambda e: e.tensor_reduce(st8[:, 0, :], lg, AX.X, ALU.max))
        b4 = st8[:, 0, :].unsqueeze(2).broadcast_to([P, 2, 4])
        tt("dve", gsel, lg, b4, ALU.subtract)
        eg = get(8).rearrange("p (a g) -> p a g", a=2)
        x = ts("dve", gsel, gsel, 0.0, None, ALU.is_ge)
        x = tt("dve", eg, lg, b4, ALU.subtract)
        x = act(eg, eg, ACT.Exp, [x])
        op("dve", lambda e: e.tensor_reduce(st8[:, 1, :], eg, AX.X, ALU.add), [x])
        op("dve", lambda e: e.reciprocal(st8[:, 1, :], st8[:, 1, :]))
        for gi in range(1, 4):
            for g2 in range(gi):
                stt(gsel[:, :, gi], gsel[:, :, g2], 0.0, gsel[:, :, gi], ALU.is_equal, ALU.mult)
        gm1 = get(8).rearrange("p (a g) -> p a g", a=2)
        ts("dve", gm1, gsel, 1.0, 1e30, ALU.subtract, ALU.mult)
        EL = get(64).rearrange("p (a g e) -> p a g e", a=2, g=4)
        tt("dve", EL, le, gm1.unsqueeze(3).broadcast_to([P, 2, 4, 8]), ALU.add)
        ELf = EL.rearrange("p a g e -> p a (g e)")
        WKf = get(64).rearrange("p (a n) -> p a n", a=2)
        M8 = get(32).rearrange("p (a n) -> p a n", a=2)
        for a in range(2):
            op("dve", lambda e, a=a: e.max(M8[:, a, 0:8], ELf[:, a, :]))
            op("dve", lambda e, a=a: e.memset(M8[:, a, 8:16], -3e38))
            op("dve", lambda e, a=a: e.tensor_copy(M8[:, a, 8:10], M8[:, a, 0:2]))
            op("dve", lambda e, a=a: e.match_replace(WKf[:, a, :], M8[:, a, 8:16], ELf[:, a, :], -3e38))
        sel2 = get(64).rearrange("p (a n) -> p a n", a=2)
        ts("dve", sel2, WKf, -2e38, None, ALU.is_lt)
        tt("dve", ELf, ELf, M8[:, :, 0:1].broadcast_to([P, 2, 32]), ALU.subtract)
        x = ts("dve", ELf, ELf, -200.0, None, ALU.max)
        x = act(ELf, ELf, ACT.Exp, [x])
        tt("dve", ELf, ELf, sel2, ALU.mult, [x])
        op("dve", lambda e: e.tensor_reduce(st8[:, 2, :], ELf, AX.X, ALU.add))
        op("dve", lambda e: e.reciprocal(st8[:, 2, :], st8[:, 2, :]))
        tt("dve", st8[:, 2, :], st8[:, 2, :], st8[:, 1, :], ALU.mult)
        x = tt("dve", ELf, ELf, st8[:, 2, :].unsqueeze(2).broadcast_to([P, 2, 32]), ALU.mult)
        for a in range(2):
            m = mm(ps[0:32, 6, a * 128:(a + 1) * 128], ELf[:, a, :], ident, 1, 1, [x, bank[6] if a == 0 else ()], tr=True)
        CW = get(T)
        tcw = cp("dve", CW[0:32, :], ps[0:32, 6, 0:T], [m])
        bank[6] = [tcw]

        def scale_unit(u):
            o = 0
            m = mm(ps[:, 7, o:o + T], ident[0:32, u:u + 1].broadcast_to([32, 128]), CW[0:32, :], True, True,
                   [tcw, bank[7]])
            return ps[:, 7, o:o + T], m

        m = units("moe", 32, ht, scale_unit)
        r = []
        for c in range(8):
            x = stt(XT[:, c, :], ps[:, c // 2, (c % 2) * T:(c % 2) * T + T], MOD[:, 40 + c:41 + c], XT[:, c, :], ALU.mult, ALU.add, [m], chain=False)
            r.append(x)
            bank[c // 2] = [x]
        ht = norm(gm[:, 16:24], r, 1e-6, shift=MOD[:, 48:56], gaintok=[tgm], outfree=[m])
        for n in range(4):
            to = g.dma("sp", lambda e, n=n: e.dma_start(OUT[:, 2 * n:2 * n + 2, :], HT[:, 2 * n:2 * n + 2, :]), osem, 16 * (n + 1), [ht[2 * n + 1]])
        op("sp", lambda e: e.wait_ge(osem, 64) and None, [])
        assert st["take"] == len(order)
        block = ctx.enter_context(nc.Block())
        g.emit(block)


def pack_weights(i):
    def units(tag, wg, wu, wd):
        n = wd.shape[0] // 256 if wd.ndim == 2 else wd.shape[0]
        for u in range(n):
            if wd.ndim == 2:
                gg, uu, dd = wg[:, 256 * u:256 * u + 256], wu[:, 256 * u:256 * u + 256], wd[256 * u:256 * u + 256]
            else:
                gg, uu, dd = wg[u], wu[u], wd[u]
            out[(tag + "g", u)] = kcols(gg)
            out[(tag + "u", u)] = kcols(uu)
            out[(tag + "d", u)] = kcols(dd)

    def kcols(w):
        k = w.shape[0] // 128
        return w.reshape(k, 128, w.shape[1]).transpose(1, 0, 2).reshape(128, -1)

    out = {}
    for l in range(2):
        units(f"f1_{l}", i["ffn1_w_gate"][l], i["ffn1_w_up"][l], i["ffn1_w_down"][l])
        units(f"f2_{l}", i["ffn2_w_gate"][l], i["ffn2_w_up"][l], i["ffn2_w_down"][l])
    w = i["ev_w_in"][0]
    b = [0, 512, 1280, 1472, 1664, 1856, 2048, 2240, 2432, 2468]
    a_, q, kc, vc, ksl, vsl, kw, vw, gl = [w[:, b[n]:b[n + 1]] for n in range(9)]
    ev = np.concatenate([a_, q, ksl, kw, kc, vc, vsl, vw, gl], 1)
    w = i["od_w_in"][0]
    sz = [512, 64, 64, 128, 32, 4, 512, 512, 512]
    b = [0]
    for s in sz:
        b.append(b[-1] + s)
    qc, kc, vc, qi, ki, wi, qd, kd, vd = [w[:, b[n]:b[n + 1]] for n in range(9)]
    od = np.concatenate([qc, kc, qd, kd, vc, vd, qi, ki, wi], 1)
    for tag, m in (("evin", ev), ("odin", od)):
        m = np.concatenate([m, np.zeros((1024, 2560 - m.shape[1]), m.dtype)], 1)
        for gi in range(5):
            for a in range(2):
                out[(tag, gi, a)] = kcols(m[512 * a:512 * a + 512, 512 * gi:512 * gi + 512])
    for tag, n in (("cmpk", "ev_cmp_w1_k"), ("cmpv", "ev_cmp_w1_v")):
        for a in range(2):
            out[(tag, a)] = kcols(i[n][0][1024 * a:1024 * a + 1024])
    for tag, m in (("evout", i["ev_w_out"][0]), ("odout", i["od_w_out"][0]), ("win2", i["w_in_2"][0]), ("wout2", i["w_out_2"][0]),
                   ("ada", np.concatenate([i["w_ada_2"][0], i["w_ada_f_2"]], 1))):
        for gi in range(m.shape[1] // 256):
            out[(tag, gi)] = kcols(m[:, 256 * gi:256 * gi + 256])
    for tag, m in (("pa", i["p_a_2"][0]), ("pb", i["p_b_2"][0])):
        for gi in range(2):
            out[(tag, gi)] = kcols(m[:, 512 * gi:512 * gi + 512])
    units("moe", i["w1e_2"][0], i["w3e_2"][0], i["w2e_2"][0])
    order = slot_order()
    W = np.empty((len(order), P, SLOT), np.float32)
    for n, k in enumerate(order):
        W[n] = out[k]
    return W


def pack_cols(i):
    a = np.zeros((P, NCOL), np.float32)

    def put(n, v):
        o, w = COFF[n]
        a[:v.shape[0], o:o + w] = v.reshape(v.shape[0], w)

    def col(v):
        return v.reshape(-1, P).T

    for l in range(2):
        put(f"n1_{l}", col(i["ffn1_norm"][l]))
        put(f"nm_{l}", col(i["mix_norm"][l]))
        put(f"n2_{l}", col(i["ffn2_norm"][l]))
    put("nf", col(i["final_norm"]))
    put("g_mix", col(i["g_mix_2"][0]))
    put("g_ffn", col(i["g_ffn_2"][0]))
    put("g_final", col(i["g_final_2"]))
    put("c", col(i["c_2"][0]))
    put("b_ada", col(np.concatenate([i["b_ada_2"][0], i["b_ada_f_2"]])))
    put("mu_rkv", col(i["mu_rkv_2"][0]))
    put("mu_wag", np.ascontiguousarray(i["mu_wag_2"][0].reshape(3, 8, P).transpose(2, 0, 1)).reshape(P, 24))
    for n, k in (("w0", "w0_2"), ("a0", "a0_2"), ("k_k", "k_k_2"), ("k_a", "k_a_2"), ("lnx_g", "lnx_g_2"), ("lnx_b", "lnx_b_2"),
                 ("conv_b", "conv_b_2"), ("b_r", "b_rgate_2"), ("b_i", "b_igate_2"), ("lam", "lam_2"), ("r_k", "r_k_2")):
        put(n, col(i[k][0].reshape(-1)))
    put("conv_w", i["conv_w_2"][0][:, 0, :].reshape(4, 4, P).transpose(2, 1, 0))
    put("sgu_b", i["ev_sgu_b"][0].T)
    put("sgu_wT", i["ev_sgu_w"][0].transpose(2, 0, 1))
    put("sgu_n", np.broadcast_to(i["ev_sgu_norm"][0][None, :], (P, 256)))
    for n, k in (("w2k", "ev_cmp_w2_k"), ("w2v", "ev_cmp_w2_v")):
        put(n, i[k][0].reshape(2, P, 64).transpose(1, 0, 2))
    for n, k in (("pos_k", "ev_cmp_pos_k"), ("pos_v", "ev_cmp_pos_v")):
        put(n, i[k][0].reshape(16, P).T)
    for n, k in (("lw1", "w1_2"), ("la1", "a1_2"), ("lg1", "g1_2")):
        m = i[k][0]
        put(n, m.reshape(8, P, m.shape[1]).transpose(1, 0, 2))
    for n, k in (("lw2", "w2_2"), ("la2", "a2_2"), ("lg2", "g2_2")):
        put(n, i[k][0])
    for n, k in (("wr", "w_rgate_2"), ("wi", "w_igate_2")):
        m = np.zeros((P, 4, P), np.float32)
        for c in range(4):
            m[0:64, c, 0:64] = i[k][0][2 * c]
            m[64:128, c, 64:128] = i[k][0][2 * c + 1]
        put(n, m)
    m = np.concatenate([i["w_rg_2"][0], i["w_re_2"][0]], 1)
    put("wre", m.reshape(8, P, 36).transpose(1, 0, 2))
    put("bre", np.broadcast_to(np.concatenate([i["b_rg_2"][0], i["b_re_2"][0]])[None, :], (P, 36)))
    return a


def kernel(**inputs):
    import concourse.bacc as _bacc
    from concourse.bass_utils import run_bass_kernel_spmd as _run

    i = {k: np.asarray(v) for k, v in inputs.items()}
    nc = _bacc.Bacc("TRN2", target_bir_lowering=False, num_devices=1)
    arrays = {
        "in_w": pack_weights(i), "in_s": pack_cols(i), "in_k": const_array(),
        "in_x": np.ascontiguousarray(i["x"][0].T.reshape(8, P, T).transpose(1, 0, 2)),
        "in_p": np.ascontiguousarray(i["positions"][0].reshape(2, P).T),
    }
    args = [nc.dram_tensor(n, a.shape, mybir.dt.from_np(a.dtype), kind="ExternalInput").ap() for n, a in arrays.items()]
    out = nc.dram_tensor("out_0", (P, 8, T), F32, kind="ExternalOutput").ap()
    build(nc, *args, out)
    r = _run(nc, [arrays], core_ids=[0])
    y = r.results[0]["out_0"]
    return np.ascontiguousarray(y.transpose(1, 0, 2).reshape(D, T).T)[None]
```

```python
from contextlib import ExitStack

import numpy as np
import concourse.bass as bass
from concourse import mybir

ALU = mybir.AluOpType
ACT = mybir.ActivationFunctionType
F32 = mybir.dt.float32
F32R = mybir.dt.float32r
I32 = mybir.dt.int32
U32 = mybir.dt.uint32
AX = mybir.AxisListType

P = 128
T = 256
D = 1024
NEG = -1e30
RING = 4
SLOT = 2048
ADA_IN = ("f2_0", "f1_1", "f2_1")
SPLIT_TAGS = {a + b for a in ("f1_0", "f2_0", "f1_1", "f2_1", "moe") for b in "gud"} | {"evin", "odin", "win2"}
NAR = 30000
SRING = 5

UNITS = {"ffn": 11, "moe": 32}


def slot_order():
    o = []

    ada = [0]

    def units(tag, n):
        for u in range(n):
            o.extend([(tag + "g", u), (tag + "u", u), (tag + "d", u)])
            if tag in ADA_IN and ada[0] < 32:
                o.append(("ada", ada[0]))
                ada[0] += 1

    units("f1_0", 11)
    o.extend([("evin", g, a) for g in range(5) for a in range(2)])
    o.extend([("cmpk", 0), ("cmpk", 1), ("cmpv", 0), ("cmpv", 1)])
    o.extend([("evout", g) for g in range(4)])
    units("f2_0", 11)
    units("f1_1", 11)
    o.extend([("odin", g, a) for g in range(5) for a in range(2)])
    o.extend([("odout", g) for g in range(4)])
    units("f2_1", 11)
    assert ada[0] == 32
    o.extend([("win2", g) for g in range(18)])
    o.extend([("pb", g) for g in range(2)] + [("pa", g) for g in range(2)])
    o.extend([("wout2", g) for g in range(4)])
    units("moe", 32)
    return o


COLS = [
    ("n1_0", 8), ("nm_0", 8), ("n2_0", 8), ("n1_1", 8), ("nm_1", 8), ("n2_1", 8), ("nf", 8),
    ("g_mix", 8), ("g_ffn", 8), ("g_final", 8), ("c", 8), ("b_ada", 64),
    ("mu_rkv", 12), ("mu_wag", 24), ("w0", 4), ("a0", 4), ("k_k", 4), ("k_a", 4), ("r_k", 4),
    ("lnx_g", 4), ("lnx_b", 4), ("conv_w", 16), ("conv_b", 4), ("b_r", 4), ("b_i", 4), ("lam", 4),
    ("sgu_b", 4), ("sgu_wT", 512), ("sgu_n", 256), ("w2k", 128), ("w2v", 128), ("pos_k", 16), ("pos_v", 16),
    ("lw1", 512), ("la1", 512), ("lg1", 1024), ("lw2", 512), ("la2", 512), ("lg2", 512),
    ("wr", 512), ("wi", 512), ("wre", 288), ("bre", 36),
]
CONSTS = [
    ("ident", 128), ("ones", 128), ("bones", 128), ("triT", 128), ("madd0", 128), ("madd1", 256),
    ("cm01", 30), ("cmadd", 30), ("inv", 8), ("gmask", 512), ("seg", 256),
] + [(f"lv{m}", 128) for m in range(6)] + [(f"lt{m}", 128) for m in range(6)]


def offsets(spec):
    at, out = 0, {}
    for n, w in spec:
        out[n] = (at, w)
        at += w
    return out, at


COFF, NCOL = offsets(COLS)
KOFF, NCON = offsets(CONSTS)


def const_array():
    a = np.zeros((P, NCON), np.float32)

    def put(n, v):
        o, w = KOFF[n]
        a[:v.shape[0], o:o + w] = v.reshape(v.shape[0], w)

    i = np.arange(P)
    put("ident", np.eye(P))
    put("ones", np.ones((P, P)))
    put("bones", (i[:, None] // 64 == i[None, :] // 64) * 1.0)
    put("triT", (i[:, None] <= i[None, :]) * 1.0)
    tri = np.where(i[None, :] <= i[:, None], 0.0, NEG)
    put("madd0", tri)
    put("madd1", np.concatenate([np.zeros((P, P)), tri], 1))
    t = i[:, None, None] + 128 * np.arange(2)[None, :, None]
    ok = (np.arange(15)[None, None, :] * 16 + 31) <= t
    put("cm01", ok * 1.0)
    put("cmadd", np.where(ok, 0.0, NEG))
    inv = np.float32(500000.0) ** (-np.arange(0, 16, 2, dtype=np.float32) / np.float32(16))
    put("inv", np.broadcast_to(inv[None, :], (P, 8)))
    same = i[:, None] // 64 == i[None, :] // 64
    su = same & (i[:, None] < i[None, :])
    u = same & (i[:, None] <= i[None, :])
    put("gmask", np.stack([su, u, su, u], 1) * 1.0)
    put("seg", np.broadcast_to((np.arange(256) % 64 != 0)[None, :] * 1.0, (P, 256)))
    for n in range(6):
        m = 1 << n
        lo = (i[:, None] // (2 * m) == i[None, :] // (2 * m)) & (i[:, None] // m % 2 == 1) & (i[None, :] // m % 2 == 0)
        put(f"lv{n}", lo * 1.0)
        put(f"lt{n}", lo.T * 1.0)
    return a


class Tok:

    def __init__(self, sem=None, val=None):
        self.sem, self.val, self.used = sem, val, False


class Prog:

    ENG = ("pe", "act", "dve", "pool", "sp")

    def __init__(self, nc, ctx):
        self.nc = nc
        self.q = {e: [] for e in self.ENG}
        self.sem = {e: ctx.enter_context(nc.semaphore("s_" + e)) for e in self.ENG}
        self.last = {e: None for e in self.ENG}

    def op(self, e, fn, after=(), chain=None):
        t = Tok(self.sem[e])
        after = [a for a in flat(after) if a is not None]
        if (chain if chain is not None else e in ("act", "dve", "pool")) and self.last[e] is not None:
            after.append(self.last[e])
        for a in after:
            a.used = True
        self.q[e].append((fn, after, t, 1))
        if fn is not None:
            self.last[e] = t
        return t

    def dma(self, e, fn, sem, val, after=()):
        t = Tok(sem, val)
        after = [a for a in flat(after) if a is not None]
        for a in after:
            a.used = True
        self.q[e].append((fn, after, t, 16))
        return t

    def emit(self, block):
        for e in self.ENG:
            n = 0
            for fn, after, t, inc in self.q[e]:
                if inc == 1 and t.used:
                    n += 1
                    t.val = n
        reg = {"pe": block.tensor, "act": block.scalar, "dve": block.vector, "pool": block.gpsimd, "sp": block.sync}
        for e in self.ENG:
            def body(eng, e=e):
                seen = {}
                for fn, after, t, inc in self.q[e]:
                    need = {}
                    for a in after:
                        if a.val > seen.get(id(a.sem), 0):
                            need[id(a.sem)] = max(need.get(id(a.sem), (0, None))[0], a.val), a.sem
                    for k, (v, s) in need.items():
                        eng.wait_ge(s, v)
                        seen[k] = v
                    ins = fn(eng) if fn is not None else None
                    if ins is not None and (inc == 16 or t.used):
                        ins.then_inc(t.sem, inc)
            reg[e](body)


def flat(x):
    if x is None or isinstance(x, Tok):
        return [x] if x is not None else []
    out = []
    for y in x:
        out += flat(y)
    return out


def build(nc, W, S, K, XI, POS, OUT):
    with ExitStack() as ctx:
        def sb(name, shape, dt=F32):
            return ctx.enter_context(nc.sbuf_tensor(name, shape, dt))

        g = Prog(nc, ctx)
        op = g.op
        order = slot_order()

        ring = sb("ring", [P, RING, SLOT])
        cols = sb("cols", [P, NCOL])
        cons = sb("cons", [P, NCON])
        XT = sb("XT", [P, 8, T])
        SQ = sb("SQ", [P, 8, T])
        RS = sb("RS", [P, T])
        pos = sb("pos", [P, 2], I32)
        small = sb("small", [P, 512])
        acc = sb("acc", [P, 2, 256])
        with ExitStack() as c2:
            AR = c2.enter_context(nc.sbuf_tensor("AR", [P, NAR], F32))
        with ExitStack() as c2:
            HH = c2.enter_context(nc.sbuf_tensor("HH", [P, 8, T], F32R))
            HL = c2.enter_context(nc.sbuf_tensor("HL", [P, 8, T], F32R))
            AH = c2.enter_context(nc.sbuf_tensor("AH", [P, 4, T], F32R))
            AL = c2.enter_context(nc.sbuf_tensor("AL", [P, 4, T], F32R))
            AF = c2.enter_context(nc.sbuf_tensor("AF", [P, 4, T], F32))
            WGAP = c2.enter_context(nc.sbuf_tensor("WGAP", [P, NAR - 7168 - SRING * 4096], F32))
            WH = c2.enter_context(nc.sbuf_tensor("WH", [P, SRING, SLOT], F32R))
            WL = c2.enter_context(nc.sbuf_tensor("WL", [P, SRING, SLOT], F32R))
        ps = ctx.enter_context(nc.psum_tensor("ps", [P, 8, 512], F32))
        wsem = [ctx.enter_context(nc.semaphore(f"w{i}")) for i in range(RING)]
        isem = [ctx.enter_context(nc.semaphore(f"i{i}")) for i in range(5)]
        osem = ctx.enter_context(nc.semaphore("o"))

        def C(n, a=None, b=None):
            o, w = COFF[n]
            a, b = (0, w) if a is None else (a, b)
            return cols[:, o + a:o + b]

        def KC(n, a=None, b=None):
            o, w = KOFF[n]
            a, b = (0, w) if a is None else (a, b)
            return cons[:, o + a:o + b]

        ident = KC("ident")

        t_x = g.dma("act", lambda e: e.dma_start(XT[:, :, :], XI), isem[0], 16)
        t_k = g.dma("act", lambda e: e.dma_start(cons[:, :], K), isem[1], 16)
        t_c = g.dma("act", lambda e: e.dma_start(cols[:, :], S), isem[2], 16)
        t_p = g.dma("act", lambda e: e.dma_start(pos[:, :], POS), isem[3], 16)

        class Slot:
            pass

        st = {"load": 0, "take": 0}
        freed = {}

        def load(after=()):
            n = st["load"]
            if n >= len(order):
                return
            st["load"] += 1
            freed[n] = g.dma("sp", lambda e, n=n: e.dma_start(ring[:, n % RING, :], W[n]),
                             wsem[n % RING], 16 * (n // RING + 1), after)

        for _ in range(RING):
            load()

        def take(key):
            n = st["take"]
            assert order[n] == key, (order[n], key)
            st["take"] += 1
            s = Slot()
            s.t, s.n = freed[n], n
            s.ap = ring[:, n % RING, :]
            return s

        read = {}

        def done(s, tok):
            read[s.n] = tok
            while st["load"] < len(order) and st["load"] - RING in read:
                load([read[st["load"] - RING]])

        sp_st = {"n": 0, "on": 0}
        sread = {}
        order_split = [i for i, k in enumerate(order) if k[0] in SPLIT_TAGS]
        spos = {i: n for n, i in enumerate(order_split)}
        rpos, rprev, user, cyc = [], [], {}, 0
        for i in order_split:
            cyc = (cyc + 1) % SRING
            if order[i][0] == "win2" and cyc < 2:
                cyc = 2
            rpos.append(cyc)
            rprev.append(user.get(cyc))
            user[cyc] = len(rpos) - 1
        stok = {}
        ssl = {}
        guard = [None]

        def split_upto():
            while sp_st["n"] < min(len(order_split), sp_st["on"]):
                n = sp_st["n"]
                if rprev[n] is not None and rprev[n] not in sread:
                    return
                i = order_split[n]
                if i != st["take"] or i not in freed:
                    return
                s = take(order[i])
                r = rpos[n]
                prev = sread.get(rprev[n])
                hs = []
                for q in range(4):
                    c = slice(q * 512, q * 512 + 512)
                    a = op("act", lambda e, c=c, r=r, s=s: e.activation(WH[:, r, c], s.ap[:, c], ACT.Copy), [s.t, prev, guard], chain=False)
                    b = op("dve", lambda e, c=c, r=r, s=s: e.tensor_tensor(WL[:, r, c], s.ap[:, c], WH[:, r, c].bitcast(F32), ALU.subtract),
                           [s.t, prev, guard, a], chain=False)
                done(s, b)
                stok[n] = b
                sp_st["n"] += 1

        class Pair:
            def __init__(self, h, l, n=None, t=None):
                self.h, self.l, self.n, self.t = h, l, n, t

            def view(self, f):
                return Pair(f(self.h), f(self.l), self.n, self.t)

        def enable(n_tags):
            sp_st["on"] = max([spos[i] for i in order_split if order[i][0] in n_tags]) + 1
            split_upto()

        def wtake(key):
            n = ssl.setdefault("n", 0)
            ssl["n"] = n + 1
            assert order[order_split[n]] == key, (key, order[order_split[n]])
            split_upto()
            r = rpos[n]
            return Pair(WH[:, r, :], WL[:, r, :], n, stok[n])

        def wdone(p, tok):
            sread[p.n] = tok
            split_upto()

        def mm3(out, A, B, start, stop, after=(), skip=False):
            op("pe", lambda e: e.matmul(out, A.h, B.h, start=start, stop=False, skip_group_check=skip), after)
            op("pe", lambda e: e.matmul(out, A.h, B.l, start=False, stop=False, skip_group_check=skip))
            return op("pe", lambda e: e.matmul(out, A.l, B.h, start=False, stop=stop, skip_group_check=skip))

        def mm(out, lhsT, rhs, start, stop, after=(), skip=False, tr=False):
            if tr:
                return op("pe", lambda e: e.transpose(out, lhsT, rhs), after)
            return op("pe", lambda e: e.matmul(out, lhsT, rhs, start=start, stop=stop, skip_group_check=skip), after)

        def tt(e, out, a, b, o, after=(), chain=None):
            return op(e, lambda q: q.tensor_tensor(out, a, b, o), after, chain)

        def ts(e, out, a, s1, s2, o0, o1=None, after=(), chain=None):
            if o1 is None:
                return op(e, lambda q: q.tensor_scalar(out, a, s1, None, o0), after, chain)
            return op(e, lambda q: q.tensor_scalar(out, a, s1, s2, o0, o1), after, chain)

        def rsq(out, a, after=(), pw=-0.5):
            x = act(out, a, ACT.Sqrt, [after, g.last["dve"]])
            if pw < 0:
                return op("dve", lambda q: q.reciprocal(out, out), [x])
            op("dve", None, [x], chain=False)
            return x

        def stt(out, a, s, b, o0, o1, after=(), chain=None):
            return op("dve", lambda q: q.scalar_tensor_tensor(out=out, in0=a, scalar=s, in1=b, op0=o0, op1=o1), after, chain)

        def act(out, a, f, after=(), chain=None, **kw):
            return op("act", lambda q: q.activation(out, a, f, **kw), after, chain)

        def cp(e, out, a, after=(), chain=None):
            if e == "act":
                return act(out, a, ACT.Copy, after, chain)
            return op(e, lambda q: q.tensor_copy(out, a), after, chain)

        MOD = small[:, 344:408]
        warm = small[:, 488:489]
        cs = small[:, 408:416]
        t_cs = act(cs, C("c"), ACT.Silu, [t_c])
        ada_free = {}

        def ada_sum(gi):
            s = take(("ada", gi))
            w = s.ap.rearrange("p (k n) -> p k n", k=8)
            a = acc[:, gi % 2, :]
            x = ts("dve", a, w[:, 0, :], cs[:, 0:1], None, ALU.mult, after=[s.t, t_cs, ada_free.get(gi - 2)], chain=False)
            for k in range(1, 8):
                x = stt(a, w[:, k, :], cs[:, k:k + 1], a, ALU.mult, ALU.add, [x], chain=False)
            done(s, x)
            return x

        def ada_out(gi, x):
            for j in range(2):
                m = mm(ps[:, 7, j:j + 1], acc[:, gi % 2, j * 128:(j + 1) * 128], KC("ones", 0, 1), True, True, [x, bank[7]])
            ada_free[gi] = m
            y = tt("dve", MOD[:, 2 * gi:2 * gi + 2], ps[:, 7, 0:2], C("b_ada", 2 * gi, 2 * gi + 2), ALU.add, [m], chain=False)
            bank[7] = [y]
            return y

        bank = {i: [] for i in range(8)}

        sqread = [None]

        def norm(gain, xtoks, eps, shift=None, gaintok=(), out=SQ, bk=7, outfree=(), split=True, nextf=ACT.Silu):
            tk = []
            for i in range(4):
                xd = xtoks[len(xtoks) // 4 * (i + 1) - 1] if len(xtoks) >= 4 else xtoks
                tk.append(act(SQ[:, 2 * i:2 * i + 2, :], XT[:, 2 * i:2 * i + 2, :], ACT.Square, [xd, t_k, sqread], chain=i == 0))
            act(warm, KC("ones", 0, 1), ACT.Sqrt, chain=False)
            for k in range(8):
                m = mm(ps[:, bk, 0:T], KC("ones"), SQ[:, k, :], k == 0, k == 7, [tk[k // 2], bank[bk] if k == 0 else ()])
            a = ts("dve", RS[:, :], ps[:, bk, 0:T], 1.0 / D, eps, ALU.mult, ALU.add, [m])
            bank[bk] = [a]
            rsq(RS[:, :], RS[:, :], pw=-0.5)
            act(warm, KC("ones", 0, 1), nextf, chain=False)
            r = []
            for k in range(0, 8, 2):
                for kk in (k, k + 1):
                    x = stt(out[:, kk, :], XT[:, kk, :], gain[:, kk:kk + 1], RS[:, :], ALU.mult, ALU.mult, [t_c, gaintok, outfree], chain=kk == 0)
                    if shift is not None:
                        x = ts("dve", out[:, kk, :], out[:, kk, :], shift[:, kk:kk + 1], None, ALU.add, after=[gaintok, x], chain=False)
                if split:
                    y = cp("act", HH[:, k:k + 2, :], out[:, k:k + 2, :], [x, guard], chain=False)
                    z = tt("dve", HL[:, k:k + 2, :], out[:, k:k + 2, :], HH[:, k:k + 2, :].bitcast(F32), ALU.subtract, [y, guard], chain=False)
                    r += [(x, z)] * 2
                else:
                    r += [x] * 2
            return r

        HP = [Pair(HH[:, k, :], HL[:, k, :]) for k in range(8)]

        adan, ada_x, t_mod = [0], [None], [None]

        def units(tag, n, ht, scale_unit=None):
            firstw = [list(bank[b]) for b in range(4)]
            nb = 3 if scale_unit is None else 2
            used = {}
            readd = {}

            def down(u, j, wd, tok, last):
                per = {}
                for d in range(8):
                    first = u == 0 and j == 0 and d % 2 == 0
                    m = mm3(ps[:, d // 2, (d % 2) * T:(d % 2) * T + T], wd.view(lambda w: w[:, j * 1024 + d * 128:j * 1024 + (d + 1) * 128]),
                            Pair(AH[:, (2 * u + j) % 4, :], AL[:, (2 * u + j) % 4, :]), first, last,
                            [wd.t, tok, firstw[d // 2] if first else ()], skip=True)
                    if d % 2:
                        per[d // 2] = m
                readd[2 * u + j] = m
                if j == 1:
                    wdone(wd, m)
                return per

            pend = None
            wds = {}
            for u in range(n):
                wg, wu = wtake((tag + "g", u)), wtake((tag + "u", u))
                if scale_unit is not None and u == 0:
                    nextcw = scale_unit(0)
                for j in range(2):
                    i = 2 * u + j
                    b = 4 + i % nb
                    for k in range(8):
                        mm3(ps[:, b, 0:T], wg.view(lambda w: w[:, k * 256 + j * 128:k * 256 + j * 128 + 128]), HP[k], k == 0, k == 7,
                            [wg.t, ht[k], bank[b] if k == 0 else ()])
                    for k in range(8):
                        mu = mm3(ps[:, b, T:2 * T], wu.view(lambda w: w[:, k * 256 + j * 128:k * 256 + j * 128 + 128]), HP[k], k == 0, k == 7, [wu.t])
                    if j == 1:
                        wdone(wg, mu)
                        wdone(wu, mu)
                    si = i % 4
                    a = act(AF[:, si, :], ps[:, b, 0:T], ACT.Silu, [mu, used.get(i - 4), guard], chain=False)
                    x = tt("dve", AF[:, si, :], AF[:, si, :], ps[:, b, T:2 * T], ALU.mult, [a, mu], chain=False)
                    bank[b] = [x]
                    if scale_unit is not None:
                        x = tt("dve", AF[:, si, :], AF[:, si, :], nextcw[0], ALU.mult, [x, nextcw[1]], chain=False)
                        bank[6 + u % 2] = [x]
                    y = cp("act", AH[:, si, :], AF[:, si, :], [x, readd.get(i - 4)], chain=False)
                    z = tt("dve", AL[:, si, :], AF[:, si, :], AH[:, si, :].bitcast(F32), ALU.subtract, [y, readd.get(i - 4)], chain=False)
                    used[i] = z
                    if pend is not None:
                        m = down(*pend, False)
                    if scale_unit is not None and j == 1 and u + 1 < n:
                        nextcw = scale_unit(u + 1)
                    if j == 0:
                        wds[u] = wtake((tag + "d", u))
                        if ada_x[0] is not None:
                            t_mod[0] = ada_out(*ada_x[0])
                            ada_x[0] = None
                        if tag in ADA_IN and adan[0] < 32:
                            asum = ada_sum(adan[0])
                            ada_x[0] = (adan[0], asum)
                            adan[0] += 1
                            split_upto()
                    pend = (u, j, wds[u], z)
            if ada_x[0] is not None:
                t_mod[0] = ada_out(*ada_x[0])
                ada_x[0] = None
            return down(*pend, True)

        def ffn(tag, gain, xtoks):
            ht = norm(gain, xtoks, 1e-6)
            m = units(tag, 11, ht)
            r = []
            for b in range(4):
                xv = XT[:, 2 * b:2 * b + 2, :].rearrange("p a t -> p (a t)")
                x = stt(xv, ps[:, b, :], 0.5, xv, ALU.mult, ALU.add, [m[b]], chain=False)
                bank[b] = [x]
                r.append(x)
            return r

        def proj_tok(tag, ncol, Z, ht, free=()):
            r = []
            for gi in range(5):
                w = min(512, ncol - 512 * gi)
                sl = [wtake((tag, gi, a)) for a in range(2)]
                for th in range(2):
                    b = (2 * gi + th) % 8
                    for k in range(8):
                        s = sl[k // 4]
                        m = mm3(ps[:, b, 0:w], HP[k].view(lambda h: h[:, th * 128:(th + 1) * 128]),
                                s.view(lambda v: v[:, (k % 4) * 512:(k % 4) * 512 + w]), k == 0, k == 7,
                                [s.t, ht[k], bank[b] if k == 0 else ()])
                        if th == 1 and k == 3:
                            wdone(sl[0], m)
                    if th == 1:
                        wdone(sl[1], m)
                    x = cp("act" if th else "dve", Z[:, th, 512 * gi:512 * gi + w], ps[:, b, 0:w], [m, free], chain=False)
                    bank[b] = [x]
                    r.append(x)
            return r

        def proj_out(tag, O, otoks, xin):
            OT = SQ
            tks = {}
            for n in range(4):
                b = n
                for q in range(4):
                    th, k = divmod(4 * n + q, 8)
                    m = mm(ps[:, b, q * 128:(q + 1) * 128], O[:, th, k * 128:(k + 1) * 128], ident, 1, 1,
                           [otoks, bank[b] if q == 0 else ()], tr=True)
                th, k0 = divmod(4 * n, 8)
                x = cp("act" if n % 2 else "dve", OT[:, k0:k0 + 4, th * 128:(th + 1) * 128],
                       ps[:, b, :].rearrange("p (k t) -> p k t", k=4), [m], chain=False)
                bank[b] = [x]
                tks[n] = x
            r = []
            for gi in range(4):
                s = take((tag, gi))
                w = s.ap.rearrange("p (k n) -> p k n", k=8)
                b = 4 + gi
                for j in range(2):
                    for k in range(8):
                        m = mm(ps[:, b, j * T:(j + 1) * T], w[:, k, j * 128:(j + 1) * 128], OT[:, k, :], k == 0, k == 7,
                               [s.t, list(tks.values()), bank[b] if k == 0 and j == 0 else ()])
                done(s, m)
                sqread[0] = m
                xv = XT[:, 2 * gi:2 * gi + 2, :].rearrange("p a t -> p (a t)")
                x = tt("dve", xv, ps[:, b, :], xv, ALU.add, [m], chain=False)
                bank[b] = [x]
                r.append(x)
            return r

        posf = small[:, 0:2]
        ang = small[:, 16:32]
        kk_ = small[:, 32:48]
        cosT = small[:, 64:80]
        sinT = small[:, 80:96]
        cp("dve", posf, pos[:, :], [t_p])
        for th in range(2):
            ts("dve", ang[:, th * 8:(th + 1) * 8], KC("inv"), posf[:, th:th + 1], None, ALU.mult, after=[t_k])
        MAGIC = 12582912.0
        ts("dve", kk_, ang, float(1 / (2 * np.pi)), None, ALU.mult)
        ts("dve", kk_, kk_, MAGIC, None, ALU.add)
        ts("dve", kk_, kk_, MAGIC, None, ALU.subtract)
        c1 = 6.28125
        c2 = float(np.float32(np.round((2 * np.pi - c1) * 2 ** 20) / 2 ** 20))
        c3 = float(2 * np.pi - c1 - c2)
        for c in (c1, c2, c3):
            stt(ang, kk_, -c, ang, ALU.mult, ALU.add)
        PI = 3.1415925
        ts("dve", ang, ang, PI, -PI, ALU.min, ALU.max)
        ts("dve", kk_, ang, -1.0, None, ALU.mult)
        tt("dve", kk_, kk_, ang, ALU.max)
        t = ts("dve", kk_, kk_, -1.0, float(np.pi / 2), ALU.mult, ALU.add)
        act(sinT, ang, ACT.Sin, [t])
        t_rope = act(cosT, kk_, ACT.Sin)

        def rope(Z, c0, nh, hd, half, tmp, after):
            zv = Z[:, :, c0:c0 + nh * hd].rearrange("p a (h d) -> p a h d", d=hd)
            x1, x2 = zv[:, :, :, 0:half], zv[:, :, :, half:2 * half]
            step = 8 // half
            sh = [P, 2, nh, half]
            cs = cosT.rearrange("p (a f s) -> p a f s", a=2, s=step)[:, :, :, 0].unsqueeze(2).broadcast_to(sh)
            sn = sinT.rearrange("p (a f s) -> p a f s", a=2, s=step)[:, :, :, 0].unsqueeze(2).broadcast_to(sh)
            n = 2 * nh * half
            t1 = tmp[:, 0:n].rearrange("p (a h f) -> p a h f", a=2, h=nh)
            t2 = tmp[:, n:2 * n].rearrange("p (a h f) -> p a h f", a=2, h=nh)
            tt("dve", t1, x1, sn, ALU.mult, [after, t_rope])
            tt("dve", t2, x2, sn, ALU.mult)
            tt("dve", x1, x1, cs, ALU.mult)
            tt("dve", x2, x2, cs, ALU.mult)
            tt("dve", x1, x1, t2, ALU.subtract)
            return tt("dve", x2, x2, t1, ALU.add)

        evn = [0]

        def ev():
            evn[0] += 1
            return "act" if evn[0] % 2 else "dve"

        def headT(Z, c0, nh, dst, after, banks, hd=64):
            r = []
            jobs = [(th, h) for th in range(2) for h in range(nh)]
            for i in range(0, len(jobs), 4):
                grp = jobs[i:i + 4]
                b = banks[(i // 4) % len(banks)]
                for q, (th, h) in enumerate(grp):
                    m = mm(ps[0:hd, b, q * 128:(q + 1) * 128], Z[:, th, c0 + h * hd:c0 + (h + 1) * hd], ident, 1, 1,
                           [after, bank[b] if q == 0 else ()], tr=True)
                x = cp(ev(), dst.rearrange("d a h t -> d (a h) t")[:, i:i + len(grp), :],
                       ps[0:hd, b, 0:128 * len(grp)].rearrange("d (h t) -> d h t", t=128), [m], chain=False)
                bank[b] = [x]
                r.append(x)
            return r

        def attention(items, SB, PT, stats, maskof, finish):
            n = len(items)
            stage = {}

            def s_stage(i):
                br, th, heads, qT, kT, V, deps = items[i]
                nk = 128 * (th + 1)
                b0 = 2 * (i % 2)
                sview = ps[:, b0:b0 + 2, :].rearrange("p b n -> p (b n)")[:, 0:4 * nk]
                for q, h in enumerate(heads):
                    m = mm(sview[:, q * nk:(q + 1) * nk], qT(h)[:, th, :], kT(h)[:, 0:th + 1, :], True, True,
                           [deps, bank[b0] if q == 0 else (), bank[b0 + 1] if q == 0 else ()])
                sbv = SB[:, i % 2, 0:4 * nk].rearrange("p (h k) -> p h k", h=4)
                mk, mt = maskof(br, th)
                mk = mk.unsqueeze(1).broadcast_to([P, 4, nk])
                x = stt(sbv, sview.rearrange("p (h k) -> p h k", h=4), 0.125, mk, ALU.mult, ALU.add,
                        [m, mt, stage.get(("pt", i - 2))])
                bank[b0] = bank[b0 + 1] = [x]
                mx = stats[:, i, 0:4]
                op("dve", lambda e: e.tensor_reduce(mx, sbv, AX.X, ALU.max))
                y = ts("dve", mx, mx, -1.0, None, ALU.mult)
                yield
                for q in range(4):
                    z = act(sbv[:, q, :], sbv[:, q, :], ACT.Exp, [y], chain=False, bias=stats[:, i, q:q + 1],
                            accum_out=stats[:, i, 4 + q:5 + q])
                stage[("e", i)] = z

            def t_stage(i):
                br, th, heads, qT, kT, V, deps = items[i]
                nk = 128 * (th + 1)
                sbv = SB[:, i % 2, 0:4 * nk].rearrange("p (h k) -> p h k", h=4)
                blk = [(q, kb) for q in range(4) for kb in range(th + 1)]
                ptk = []
                for c in range(0, len(blk), 4):
                    b = 4 + (c // 4)
                    for w, (q, kb) in enumerate(blk[c:c + 4]):
                        m = mm(ps[:, b, w * 128:(w + 1) * 128], sbv[:, q, kb * 128:(kb + 1) * 128], ident, 1, 1,
                               [stage[("e", i)], bank[b] if w == 0 else ()], tr=True)
                    x = cp("dve" if c else "act", PT[:, i % 2, c * 128:c * 128 + 512], ps[:, b, :], [m, stage.get(("o", i - 2))], chain=False)
                    bank[b] = [x]
                    ptk.append(x)
                stage[("pt", i)] = m
                stage[("pe", i)] = ptk

            def o_stage(i):
                br, th, heads, qT, kT, V, deps = items[i]
                ob = 6 + i % 2
                ptk = stage[("pe", i)]
                blk = [(q, kb) for q in range(4) for kb in range(th + 1)]
                for q, h in enumerate(heads):
                    for kb in range(th + 1):
                        w = blk.index((q, kb))
                        m = mm(ps[:, ob, q * 64:(q + 1) * 64], PT[:, i % 2, w * 128:(w + 1) * 128], V(h, kb),
                               kb == 0, kb == th, [ptk, bank[ob] if q == 0 and kb == 0 else ()])
                stage[("o", i)] = m
                w = op("dve", lambda e: e.reciprocal(stats[:, i, 8:12], stats[:, i, 4:8]), [stage[("e", i)]])
                x = finish(i, items[i], ps[:, ob, 0:256].rearrange("p (h d) -> p h d", h=4), stats[:, i, 8:12], [m, w])
                bank[ob] = [x]
                return x

            for i in range(-1, n + 1):
                sg_ = s_stage(i + 1) if i + 1 < n else iter(())
                next(sg_, None)
                if 0 <= i < n:
                    t_stage(i)
                next(sg_, None)
                if i >= 1:
                    last = o_stage(i - 1)
            return last

        def carve(*segs):
            segs = [list(x) for x in segs]

            def get(n):
                for sg_ in segs:
                    if sg_[1] - sg_[0] >= n:
                        sg_[0] += n
                        return AR[:, sg_[0] - n:sg_[0]]
                raise AssertionError((n, segs))
            return get

        RB = NAR - SRING * 4096

        enable({"f1_0d", "evin"})
        xt = ffn("f1_0", C("n1_0"), [t_x])
        ht = norm(C("nm_0"), xt, 1e-6)
        get = carve((4096, RB))
        Z = get(2 * 2468).rearrange("p (a n) -> p a n", a=2)
        get = carve((0, 2048), (RB, NAR), (2048, 4096))
        O = get(2 * 1024).rearrange("p (a n) -> p a n", a=2)
        zt = proj_tok("evin", 2468, Z, ht)
        QN = get(3072)[0:64, :].rearrange("p (a h t) -> p a h t", a=2, h=12)
        zt_all = zt
        tqn = headT(Z, 512, 12, QN, zt_all, [0, 1])
        kv2 = get(2 * 2 * 192 * 2).rearrange("p (a w h c d) -> p a w h c d", a=2, w=2, h=3, c=2)
        t2 = []
        for a in range(2):
            for w in range(2):
                src = Z[:, a, 1664 + 192 * w:1664 + 192 * (w + 1)].rearrange("p (h d) -> p h d", h=3)
                t2.append(op("pool", lambda e, a=a, w=w, src=src: e.tensor_copy(
                    kv2[:, a, w], src.unsqueeze(2).broadcast_to([P, 3, 2, 64])), [zt_all]))
        kct = get(2 * 3 * T).rearrange("p (w h t) -> p w h t", w=2, h=3)
        ktk = []
        for w in range(2):
            for h in range(3):
                b = 2 + (3 * w + h) % 2
                for a in range(2):
                    m = mm(ps[:, b, a * 128:(a + 1) * 128], kv2[:, a, w, h].rearrange("p c d -> p (c d)"), ident, 1, 1,
                           [t2, bank[b] if a == 0 else ()], tr=True)
                x1 = cp("act", kct[0:64, w, h, :], ps[0:64, b, 0:T], [m], chain=False)
                x2 = cp("dve", kct[64:128, w, h, 0:T - 1], ps[64:128, b, 1:T], [m], chain=False)
                bank[b] = [x1, x2]
                ktk += [x1, x2]
        blk = get(2 * 16 * 45).rearrange("p (w l h n) -> p w l h n", w=2, l=16, h=3)
        btk = []
        for w, pn in enumerate(("pos_k", "pos_v")):
            for h in range(3):
                base = kct[:, w, h, :]
                lo = base.rearrange("p (n l c) -> p l n c", n=16, c=2)[:, 0:8, 0:15, 0]
                hi = base.rearrange("p (n l c) -> p l n c", n=16, c=2)[:, 0:8, 1:16, 0]
                pv = C(pn).unsqueeze(2)
                tt("dve", blk[:, w, 0:8, h, :], lo, pv[:, 0:8].broadcast_to([P, 8, 15]), ALU.add, [ktk, t_c], chain=False)
                btk.append(tt("dve", blk[:, w, 8:16, h, :], hi, pv[:, 8:16].broadcast_to([P, 8, 15]), ALU.add, [ktk], chain=False))
        hid = get(2 * 2 * 45).rearrange("p (w c n) -> p w c n", w=2, c=2)
        htk = []
        for w, tag in enumerate(("cmpk", "cmpv")):
            s0, s1 = take((tag, 0)), take((tag, 1))
            for c in range(2):
                b = 4 + 2 * w + c
                for lp in range(16):
                    s = (s0, s1)[lp // 8]
                    wv = s.ap.rearrange("p (l n) -> p l n", l=8)
                    m = mm(ps[:, b, 0:45], wv[:, lp % 8, c * 128:(c + 1) * 128], blk[:, w, lp].rearrange("p h n -> p (h n)"),
                           lp == 0, lp == 15, [s.t, btk, bank[b] if lp == 0 else ()])
                x = act(hid[:, w, c, :], ps[:, b, 0:45], ACT.Gelu_apprx_tanh, [m])
                bank[b] = [x]
                htk.append(x)
            done(s0, m)
            done(s1, m)
        uv = get(2 * 512).rearrange("p (a n) -> p a n", a=2)
        tuv = act(uv, Z[:, :, 0:512], ACT.Gelu_apprx_tanh, [zt_all])
        KCT = get(48)[0:64, 0:45]
        for c in range(2):
            m = mm(ps[0:64, 4, 0:45], C("w2k", 64 * c, 64 * c + 64), hid[:, 0, c, :], c == 0, c == 1, [htk, bank[4]])
        tkc = cp("dve", KCT, ps[0:64, 4, 0:45], [m])
        bank[4] = [tkc]
        hd = get(2 * 3 * 128).rearrange("p (c g r n) -> p c g r n", c=2, g=3, r=4)
        op("dve", lambda e: e.memset(hd, 0.0), [zt_all])
        for c in range(2):
            thd = op("dve", lambda e, c=c: e.tensor_copy(
                hd[:, c, :, :, 0:15], hid[:, 1, c, :].rearrange("p (g n) -> p g n", g=3).unsqueeze(2).broadcast_to([P, 3, 4, 15])), [htk])
        VB = get(3 * 256).rearrange("p (g r d) -> p g r d", g=3, r=4)
        op("dve", lambda e: e.memset(VB, 0.0))
        for gi in range(3):
            for c in range(2):
                m = mm(ps[:, 5, gi * 64:(gi + 1) * 64], hd[:, c, gi].rearrange("p r n -> p (r n)"), C("w2v", 64 * c, 64 * c + 64),
                       c == 0, c == 1, [thd, bank[5] if c == 0 and gi == 0 else ()])
        for gi in range(3):
            for r in range(4):
                tvb = cp("dve", VB[32 * r:32 * r + 32, gi, r, :], ps[32 * r:32 * r + 32, 5, gi * 64:(gi + 1) * 64], [m])
        bank[5] = [tvb]
        tmp = get(2 * 576)
        trq = rope(Z, 512, 18, 64, 8, tmp, [zt_all, tqn])
        QT = get(3072)[0:64, :].rearrange("p (a h t) -> p a h t", a=2, h=12)
        KT = get(2 * 3 * 2 * 128)[0:64, :].rearrange("p (a h t) -> p a h t", a=2, h=6)
        tq = headT(Z, 512, 12, QT, trq, [0, 1])
        tk = headT(Z, 1280, 6, KT, trq, [2, 3])
        gts = get(72).rearrange("p (a n) -> p a n", a=2)
        tg = act(gts, Z[:, :, 2432:2468], ACT.Sigmoid, [zt_all])
        gv = gts.rearrange("p a (h r) -> p a h r", r=3)
        v = uv[:, :, 256:512]
        ssq = small[:, 100:102]
        for a in range(2):
            op("dve", lambda e, a=a: e.tensor_tensor_reduce(out=SQ[:, a, :], in0=v[:, a, :], in1=v[:, a, :], scale=1.0, scalar=0.0,
                                                            op0=ALU.mult, op1=ALU.add, accum_out=ssq[:, a:a + 1]), [tuv, ht])
        ts("dve", ssq, ssq, 1.0 / 256, 1e-6, ALU.mult, ALU.add)
        rsq(ssq, ssq, pw=-0.5)
        for a in range(2):
            tvn = stt(v[:, a, :], v[:, a, :], ssq[:, a:a + 1], C("sgu_n"), ALU.mult, ALU.mult)
        sw = C("sgu_wT").rearrange("p (g t) -> p g t", g=4)
        tsw = tt("dve", sw, sw, KC("triT").unsqueeze(1).broadcast_to([P, 4, 128]), ALU.mult)
        for a in range(2):
            for gi in range(4):
                m = mm(ps[:, 6 + a, gi * 64:(gi + 1) * 64], sw[:, gi, :], v[:, a, gi * 64:(gi + 1) * 64], True, True,
                       [tvn, tsw, bank[6 + a] if gi == 0 else ()])
            for gi in range(4):
                x = stt(O[:, a, gi * 64:(gi + 1) * 64], ps[:, 6 + a, gi * 64:(gi + 1) * 64], C("sgu_b", gi, gi + 1),
                        uv[:, a, gi * 64:(gi + 1) * 64], ALU.add, ALU.mult, [m], chain=False)
            bank[6 + a] = [x]
        Ob = O[:, :, 256:1024].rearrange("p a (h d) -> p a h d", h=12)
        pc = get(2 * 12 * 32).rearrange("p (a h n) -> p a h n", a=2, h=12)
        op("dve", lambda e: e.memset(pc, 0.0))
        cst = small[:, 128:200].rearrange("p (k a h) -> p k a h", k=3, a=2)
        for a in range(2):
            for h in range(12):
                m = mm(ps[:, 4 + a, h * 15:(h + 1) * 15], QN[:, a, h, :], KCT[:, (h // 4) * 15:(h // 4) * 15 + 15], True, True,
                       [tqn, tkc, bank[4 + a] if h == 0 else ()])
            pv = pc[:, a, :, 0:15]
            ma = KC("cmadd", 15 * a, 15 * a + 15).unsqueeze(1).broadcast_to([P, 12, 15])
            m01 = KC("cm01", 15 * a, 15 * a + 15).unsqueeze(1).broadcast_to([P, 12, 15])
            x = stt(pv, ps[:, 4 + a, 0:180].rearrange("p (h n) -> p h n", h=12), 0.125, ma, ALU.mult, ALU.add, [m])
            bank[4 + a] = [x]
            op("dve", lambda e, a=a, pv=pv: e.tensor_reduce(cst[:, 0, a, :], pv, AX.X, ALU.max))
            x = tt("dve", pv, pv, cst[:, 0, a, :].unsqueeze(2).broadcast_to([P, 12, 15]), ALU.subtract)
            x = act(pv, pv, ACT.Exp, [x])
            op("dve", lambda e, a=a, pv=pv: e.tensor_reduce(cst[:, 1, a, :], pv, AX.X, ALU.add), [x])
            op("dve", lambda e, a=a: e.reciprocal(cst[:, 1, a, :], cst[:, 1, a, :]))
            tt("dve", cst[:, 1, a, :], cst[:, 1, a, :], gv[:, a, :, 0], ALU.mult, [tg])
            tpc = tt("dve", pv, pv, m01, ALU.mult)
        pct = get(2 * 3 * 128).rearrange("p (a g t) -> p a g t", a=2, g=3)
        for a in range(2):
            for gi in range(3):
                m = mm(ps[:, 6 + a, gi * 128:(gi + 1) * 128], pc[:, a, 4 * gi:4 * gi + 4, :].rearrange("p h n -> p (h n)"), ident, 1, 1,
                       [tpc, bank[6 + a] if gi == 0 else ()], tr=True)
            x = cp("act", pct[:, a], ps[:, 6 + a, 0:384].rearrange("p (g t) -> p g t", g=3), [m])
            bank[6 + a] = [x]
            for gi in range(3):
                b = 4 + gi // 2
                m = mm(ps[:, b, (gi % 2) * 256:(gi % 2) * 256 + 256], pct[:, a, gi, :], VB[:, gi].rearrange("p r d -> p (r d)"), True, True,
                       [x, tvb, bank[4], bank[5]])
            ov = ps[:, 4:6, :].rearrange("p b (h d) -> p (b h) d", d=64)[:, 0:12, :]
            x = tt("dve", Ob[:, a], ov, cst[:, 1, a, :].unsqueeze(2).broadcast_to([P, 12, 64]), ALU.mult, [m])
            bank[4] = bank[5] = [x]
        tcmp = x
        SB = SQ[:, :, :].rearrange("p (a b) t -> p a (b t)", a=2)
        PT = get(2048).rearrange("p (a n) -> p a n", a=2)
        stats = small[:, 200:344].rearrange("p (i n) -> p i n", n=12)
        otmp = get(256).rearrange("p (h d) -> p h d", h=4)
        items = []
        for br in range(2):
            for th in range(2):
                for gi in range(3):
                    items.append((br, th, [4 * gi + r for r in range(4)],
                                  lambda h: QT[:, :, h, :],
                                  lambda h, br=br: KT[:, :, 3 * br + h // 4, :],
                                  lambda h, kb, br=br: Z[:, kb, 2048 + 192 * br + 64 * (h // 4):2048 + 192 * br + 64 * (h // 4) + 64],
                                  [tq, tk, zt_all]))

        def fin_even(i, item, o, r, after):
            br, th, heads = item[0], item[1], item[2]
            tt("dve", r, r, gv[:, th, heads[0]:heads[0] + 4, 1 + br], ALU.mult, after)
            y = tt("dve", otmp, o, r.unsqueeze(2).broadcast_to([P, 4, 64]), ALU.mult)
            z = Ob[:, th, heads[0]:heads[0] + 4, :]
            fin_last[0] = tt("dve", z, z, otmp, ALU.add)
            return y

        fin_last = [None]
        attention(items, SB, PT, stats, lambda br, th: (KC("madd%d" % th), t_k), fin_even)
        guard[0] = [fin_last[0], g.last["pe"], g.last["act"], g.last["dve"]]
        enable({"f2_0d"})
        xt = proj_out("evout", O, [fin_last[0]], xt)
        enable({"f1_1d", "odin"})
        xt = ffn("f2_0", C("n2_0"), xt)

        xt = ffn("f1_1", C("n1_1"), xt)
        ht = norm(C("nm_1"), xt, 1e-6)
        get = carve((4096, RB))
        Z = get(2 * 2340).rearrange("p (a n) -> p a n", a=2)
        get = carve((0, 2048), (RB, NAR), (2048, 4096))
        O = get(2 * 1024).rearrange("p (a n) -> p a n", a=2)
        zt = proj_tok("odin", 2340, Z, ht)
        tmp = get(2 * 800)
        r1 = rope(Z, 2176, 5, 32, 4, tmp, zt)
        tmp2 = tmp
        r2 = rope(Z, 0, 25, 64, 8, tmp2, zt)
        IT = get(2 * 5 * 128)[0:32, :].rearrange("p (a h t) -> p a h t", a=2, h=5)
        ti = headT(Z, 2176, 5, IT, r1, [0, 1], hd=32)
        QT = get(2 * 17 * 128)[0:64, :].rearrange("p (a h t) -> p a h t", a=2, h=17)
        tq = headT(Z, 0, 17, QT, r2, [2, 3])
        KT = get(2 * 8 * 128)[0:64, :].rearrange("p (a h t) -> p a h t", a=2, h=8)
        tk = headT(Z, 1088, 8, KT, r2, [4, 5])
        wi = small[:, 104:112].rearrange("p (a h) -> p a h", a=2)
        twi = ts("dve", wi, Z[:, :, 2336:2340], 0.5, None, ALU.mult)
        MS = get(384)
        wk = get(256)
        rl = get(1024)
        m8 = small[:, 112:120]
        mtok = []
        for th in range(2):
            nk = 128 * (th + 1)
            for h in range(4):
                b = 6 + h // 2
                for kb in range(th + 1):
                    m = mm(ps[:, b, (h % 2) * nk + kb * 128:(h % 2) * nk + kb * 128 + 128], IT[:, th, h, :], IT[:, kb, 4, :], True, True,
                           [ti, bank[6], bank[7]])
            rv = rl[:, 0:4 * nk].rearrange("p (b n) -> p b n", b=2)
            x = ts("dve", rv, ps[:, 6:8, 0:2 * nk], float(32 ** -0.5), 0.0, ALU.mult, ALU.max, after=[m])
            bank[6] = bank[7] = [x]
            rh = rl[:, 0:4 * nk].rearrange("p (h n) -> p h n", h=4)
            ms = MS[:, 0:128] if th == 0 else MS[:, 128:384]
            w_ = wk[:, 0:nk]
            ts("dve", w_, rh[:, 0, :], wi[:, th, 0:1], None, ALU.mult)
            for h in range(1, 4):
                stt(w_, rh[:, h, :], wi[:, th, h:h + 1], w_, ALU.mult, ALU.add)
            tt("dve", w_, w_, KC("madd%d" % th), ALU.add)
            for r in range(8):
                op("dve", lambda e, w_=w_: e.max(m8, w_))
                op("dve", lambda e, w_=w_: e.match_replace(w_, m8, w_, -3e38))
            ts("dve", ms, w_, -2e38, NEG, ALU.is_gt, ALU.mult)
            mtok.append(tt("dve", ms, ms, KC("madd%d" % th), ALU.add))
        SB = SQ[:, :, :].rearrange("p (a b) t -> p a (b t)", a=2)
        PT = get(2048).rearrange("p (a n) -> p a n", a=2)
        items = []
        for br in (1, 0):
            for th in range(2):
                for gi in range(2):
                    heads = [4 * gi + r for r in range(4)]
                    if br == 0:
                        items.append((0, th, heads, lambda h: QT[:, :, h, :], lambda h: QT[:, :, 8, :],
                                      lambda h, kb: Z[:, kb, 1600:1664], [tq, zt]))
                    else:
                        items.append((1, th, heads, lambda h: QT[:, :, 9 + h, :], lambda h: KT[:, :, h, :],
                                      lambda h, kb: Z[:, kb, 1664 + 64 * h:1728 + 64 * h], [tq, tk, zt]))
        Oh = O.rearrange("p a (h d) -> p a h d", d=64)

        def fin_odd(i, item, o, r, after):
            br, th, heads = item[0], item[1], item[2]
            h0 = heads[0] + 8 * br
            fin_last[0] = tt("dve", Oh[:, th, h0:h0 + 4, :], o, r.unsqueeze(2).broadcast_to([P, 4, 64]), ALU.mult, after)
            return fin_last[0]

        attention(items, SB, PT, stats,
                  lambda br, th: (KC("madd%d" % th), t_k) if br else ((MS[:, 0:128] if th == 0 else MS[:, 128:384]), mtok), fin_odd)
        guard[0] = [fin_last[0], g.last["pe"], g.last["act"], g.last["dve"]]
        enable({"f2_1d"})
        xt = proj_out("odout", O, [fin_last[0]], xt)
        xt = ffn("f2_1", C("n2_1"), xt)

        xt = norm(C("nf"), xt, 1e-6, out=XT, split=False)
        gm = small[:, 416:440]
        for n, (gn, o) in enumerate((("g_mix", 8), ("g_ffn", 32), ("g_final", 56))):
            tgm = stt(gm[:, 8 * n:8 * n + 8], MOD[:, o:o + 8], 1.0, C(gn), ALU.add, ALU.mult, [t_mod[0]])
        ht = norm(gm[:, 0:8], xt, 1e-6, shift=MOD[:, 0:8], gaintok=[tgm, t_mod[0]])
        enable({"win2"})
        get = carve((4096, RB + 4096))
        RKV = get(12 * T).rearrange("p (c t) -> p c t", c=12)
        XG = get(8 * T + 12)
        XB = XG[:, 0:4 * (T + 3)].rearrange("p (c t) -> p c t", c=4)
        GB = XG[:, 4 * (T + 3):8 * T + 12].rearrange("p (c t) -> p c t", c=4)
        SG = get(16 * T).rearrange("p (c t) -> p c t", c=16)
        tz = op("pool", lambda e: e.memset(XB[:, :, 0:3], 0.0), [xt])
        pj = []
        for gi in range(18):
            s = wtake(("win2", gi))
            b = gi % 4
            for j in range(2):
                for k in range(8):
                    m = mm3(ps[:, b, j * T:(j + 1) * T], s.view(lambda w: w[:, k * 256 + j * 128:k * 256 + j * 128 + 128]), HP[k], k == 0, k == 7,
                            [s.t, ht[k], bank[b] if k == 0 and j == 0 else ()])
            wdone(s, m)
            c = 2 * gi
            pv = ps[:, b, :].rearrange("p (c t) -> p c t", c=2)
            if c < 12:
                x = cp("dve", RKV[:, c:c + 2, :], pv, [m], chain=False)
            elif c < 16:
                x = cp("dve", XB[:, c - 12:c - 10, 3:T + 3], pv, [m], chain=False)
            elif c < 20:
                x = act(GB[:, c - 16:c - 14, :], pv, ACT.Gelu_apprx_tanh, [m], chain=False)
            else:
                x = act(SG[:, c - 20:c - 18, :], pv, ACT.Sigmoid, [m], chain=False)
            bank[b] = [x]
            pj.append(x)
        get = carve((0, 4096), (4096 + 36 * T + 12, NAR))
        MG = get(2048).rearrange("p (c t) -> p c t", c=8)
        XX = get(2048).rearrange("p (i t) -> p i t", i=16)
        DX = AR[:, NAR - 2048:NAR].rearrange("p (c t) -> p c t", c=8)
        xm = get(8 * T).rearrange("p (c t) -> p c t", c=8)
        guard[0] = [pj]
        tt("dve", DX[:, :, 1:T], SQ[:, :, 0:T - 1], SQ[:, :, 1:T], ALU.subtract, [ht, pj])
        tdx = ts("dve", DX[:, :, 0:1], SQ[:, :, 0:1], -1.0, None, ALU.mult, chain=False)
        LW = get(4 * T).rearrange("p (c t) -> p c t", c=4)
        AI = get(4 * T).rearrange("p (c t) -> p c t", c=4)
        GG_ = get(4 * T).rearrange("p (c t) -> p c t", c=4)
        lr = get(T)
        free = None
        outs = {}
        for n, (w1n, w2n, r, dst) in enumerate((("lw1", "lw2", 64, LW), ("la1", "la2", 64, AI), ("lg1", "lg2", 128, GG_))):
            tk_ = []
            for k in range(8):
                tk_.append(stt(xm[:, k, :], DX[:, k, :], C("mu_wag", 8 * n + k, 8 * n + k + 1), SQ[:, k, :], ALU.mult, ALU.add,
                               [free, tdx], chain=False))
            for k in range(8):
                m = mm(ps[0:r, 4, 0:T], C(w1n, r * k, r * k + r), xm[:, k, :], k == 0, k == 7, [tk_[k], bank[4] if k == 0 else ()])
            free = m
            f = {0: ACT.Tanh, 1: ACT.Copy, 2: ACT.Sigmoid}[n]
            x = act(lr[0:r, :], ps[0:r, 4, 0:T], f, [m, outs.get("m")])
            bank[4] = [x]
            for c in range(4):
                b = 5 + c // 2
                m = mm(ps[:, b, (c % 2) * T:(c % 2) * T + T], C(w2n, 128 * c, 128 * c + 128)[0:r, :], lr[0:r, :], True, True,
                       [x, bank[b] if c % 2 == 0 else ()])
            outs["m"] = m
            for c in range(4):
                b = 5 + c // 2
                src = ps[:, b, (c % 2) * T:(c % 2) * T + T]
                if n == 0:
                    x = act(dst[:, c, :], src, ACT.Sigmoid, [m, t_c], bias=C("w0", c, c + 1))
                elif n == 1:
                    x = act(dst[:, c, :], src, ACT.Sigmoid, [m, t_c], bias=C("a0", c, c + 1))
                else:
                    x = cp("act", dst[:, c, :], src, [m])
                bank[b] = [x]
            outs[n] = x
        DX = SQ
        sp = small[:, 440:472].rearrange("p (n c) -> p n c", c=4)
        lam = C("lam")
        ts("dve", sp[:, 0], lam, -1.0, None, ALU.mult, after=[t_c])
        tt("dve", sp[:, 1], sp[:, 0], lam, ALU.max)
        x = ts("dve", sp[:, 0], sp[:, 0], 0.0, None, ALU.max)
        x = act(sp[:, 2], sp[:, 1], ACT.Exp, [x], scale=-1.0)
        ts("dve", sp[:, 3], sp[:, 2], 2.0, None, ALU.add, after=[x])
        op("dve", lambda e: e.reciprocal(sp[:, 3], sp[:, 3]))
        tt("dve", sp[:, 3], sp[:, 3], sp[:, 2], ALU.mult)
        tt("dve", sp[:, 4], sp[:, 3], sp[:, 3], ALU.mult)
        ts("dve", sp[:, 5], sp[:, 4], 1.0 / 17, 1.0 / 15, ALU.mult, ALU.add)
        for d in (13, 11, 9, 7, 5, 3, 1):
            tt("dve", sp[:, 5], sp[:, 5], sp[:, 4], ALU.mult)
            ts("dve", sp[:, 5], sp[:, 5], 1.0 / d, None, ALU.add)
        tt("dve", sp[:, 5], sp[:, 5], sp[:, 3], ALU.mult)
        stt(sp[:, 5], sp[:, 5], 2.0, sp[:, 0], ALU.mult, ALU.add)
        tsp = ts("dve", sp[:, 6], sp[:, 5], -8.0, None, ALU.mult)
        XC = get(4 * T).rearrange("p (c t) -> p c t", c=4)
        for c in range(4):
            ts("dve", XC[:, c, :], XB[:, c, 0:T], C("conv_w", 4 * c, 4 * c + 1), C("conv_b", c, c + 1), ALU.mult, ALU.add, after=[pj, tz])
            for j in range(1, 4):
                txc = stt(XC[:, c, :], XB[:, c, j:T + j], C("conv_w", 4 * c + j, 4 * c + j + 1), XC[:, c, :], ALU.mult, ALU.add)
        GR, GI = xm[:, 0:4, :], xm[:, 4:8, :]
        for wn, bn, dst in (("wr", "b_r", GR), ("wi", "b_i", GI)):
            for c in range(4):
                b = c // 2
                m = mm(ps[:, b, (c % 2) * T:(c % 2) * T + T], C(wn, 128 * c, 128 * c + 128), XC[:, c, :], True, True,
                       [txc, bank[b] if c % 2 == 0 else ()])
            for c in range(4):
                b = c // 2
                tgr = act(dst[:, c, :], ps[:, b, (c % 2) * T:(c % 2) * T + T], ACT.Sigmoid, [m, free], bias=C(bn, c, c + 1))
                bank[b] = [tgr]
        for c in range(4):
            x = ts("dve", GR[:, c, :], GR[:, c, :], sp[:, 6, c:c + 1], None, ALU.mult, after=[tgr, tsp])
        x = act(GR, GR, ACT.Tanh, [x])
        A_, U_ = XB[:, :, 0:T], RKV
        B_ = DX[:, 0:4, :]
        ts("dve", B_, GR, -1.0, 1.0, ALU.mult, ALU.add, after=[x, free])
        op("dve", lambda e: e.reciprocal(B_, B_))
        stt(A_, GR, 1.0, B_, ALU.add, ALU.mult)
        rsq(A_, A_, pw=0.5)
        stt(GR, GR, -2.0, B_, ALU.mult, ALU.mult)
        rsq(GR, GR, pw=0.5)
        tt("dve", GI, GI, XC, ALU.mult)
        tt("dve", GR, GR, GI, ALU.mult)
        for c in range(4):
            op("dve", lambda e, c=c: e.tensor_tensor_scan(XC[:, c, :], A_[:, c, :], GR[:, c, :], 0.0, ALU.mult, ALU.add))
        YB = GB
        tyb = tt("dve", YB, XC, GB, ALU.mult)

        def proj_p(tag, Y, ytok, half, acc, b0):
            for gi in range(2):
                s = take((tag, gi))
                w = s.ap.rearrange("p (k n) -> p k n", k=4)
                for j in range(4):
                    b = b0 + j // 2
                    for k in range(4):
                        m = mm(ps[:, b, (j % 2) * T:(j % 2) * T + T], w[:, k, j * 128:(j + 1) * 128], Y[:, k, :], k == 0, k == 3,
                               [s.t, ytok, bank[b] if k == 0 and j % 2 == 0 else ()])
                    if j % 2 == 1:
                        c = 4 * gi + j - 1
                        pv = ps[:, b, :].rearrange("p (c t) -> p c t", c=2)
                        sgv = SG[:, half + c:half + c + 2, :]
                        if not acc:
                            x = tt("dve", MG[:, c:c + 2, :], sgv, pv, ALU.mult, [m, free, ht])
                            bank[b] = [x]
                        else:
                            x = tt("dve", sgv, sgv, pv, ALU.mult, [m])
                            bank[b] = [x]
                            x = tt("dve", MG[:, c:c + 2, :], MG[:, c:c + 2, :], sgv, ALU.add)
                done(s, m)
            return x

        proj_p("pb", YB, tyb, 8, False, 0)

        d4 = DX[:, 4:8, :]
        for q in range(3):
            X = RKV[:, 4 * q:4 * q + 4, :]
            tt("dve", d4[:, :, 1:T], X[:, :, 0:T - 1], X[:, :, 1:T], ALU.subtract, [pj])
            ts("dve", d4[:, :, 0:1], X[:, :, 0:1], -1.0, None, ALU.mult)
            for c in range(4):
                x = stt(X[:, c, :], d4[:, c, :], C("mu_rkv", 4 * q + c, 4 * q + c + 1), X[:, c, :], ALU.mult, ALU.add)
        Rr, Kr, Vr = RKV[:, 0:4, :], RKV[:, 4:8, :], RKV[:, 8:12, :]
        KKn = xm[:, 0:4, :]
        for c in range(4):
            ts("dve", KKn[:, c, :], Kr[:, c, :], C("k_k", c, c + 1), None, ALU.mult)
        x = tt("dve", d4, KKn, KKn, ALU.mult)
        for c in range(4):
            m = mm(ps[:, 4 + c // 2, (c % 2) * T:(c % 2) * T + T], KC("bones"), d4[:, c, :], True, True, [x, bank[4 + c // 2] if c % 2 == 0 else ()])
        pv = ps[:, 4:6, :].rearrange("p b (c t) -> p (b c) t", c=2)
        x = ts("dve", d4, pv, 1e-12, None, ALU.add, after=[m, outs[2]])
        bank[4] = bank[5] = [x]
        rsq(d4, d4)
        tt("dve", KKn, KKn, d4, ALU.mult)
        for c in range(4):
            ts("dve", d4[:, c, :], AI[:, c, :], 1.0, C("k_a", c, c + 1), ALU.subtract, ALU.mult)
        stt(Kr, d4, 1.0, Kr, ALU.add, ALU.mult)
        for c in range(4):
            x = stt(d4[:, c, :], Rr[:, c, :], C("r_k", c, c + 1), Kr[:, c, :], ALU.mult, ALU.mult)
        for c in range(4):
            m = mm(ps[:, 4 + c // 2, (c % 2) * T:(c % 2) * T + T], KC("bones"), d4[:, c, :], True, True, [x, bank[4 + c // 2] if c % 2 == 0 else ()])
        BN = XC
        x = tt("dve", BN, pv, Vr, ALU.mult, [m])
        bank[4] = bank[5] = [x]
        ts("dve", LW, LW, -float(np.exp(-0.5)), None, ALU.mult, after=[outs[0]])
        CU = DX[:, 0:4, :]
        for c in range(4):
            op("dve", lambda e, c=c: e.tensor_tensor_scan(CU[:, c, :], KC("seg"), LW[:, c, :], 0.0, ALU.mult, ALU.add))
        x = tt("dve", LW, CU, LW, ALU.subtract)
        PP = xm[:, 4:8, :]
        te = act(LW, LW, ACT.Exp, [x])
        te = act(PP, CU, ACT.Exp)
        te = act(CU, CU, ACT.Exp, scale=-1.0)
        GXt = get(8 * T).rearrange("p (c j w t) -> p c j w t", c=4, j=2, w=2)
        KKj = KKn.rearrange("p c (j t) -> p c j t", j=2)
        for c in range(4):
            stt(GXt[:, c, :, 0, :], KKj[:, c], -1.0, LW[:, c, :].rearrange("p (j t) -> p j t", j=2), ALU.mult, ALU.mult, [te])
            tt("dve", GXt[:, c, :, 1, :], Rr[:, c, :].rearrange("p (j t) -> p j t", j=2), PP[:, c, :].rearrange("p (j t) -> p j t", j=2), ALU.mult)
        BT = AI
        tt("dve", BT, KKn, AI, ALU.mult, [outs[1]])
        tt("dve", BT, BT, CU, ALU.mult)
        KTt = Kr
        tk_ = tt("dve", KTt, Kr, CU, ALU.mult)
        PPe = small[:, 472:488].rearrange("p (q c) -> p q c", q=4)
        for q in range(4):
            tpe = cp("dve", PPe[:, q, :], PP[:, :, 64 * q + 63])
        TM = {}
        tmt = {}
        spaces = [LW, xm[:, 0:4, :], xm[:, 4:8, :], DX[:, 0:4, :]]
        srcs = {"b": lambda c, j: BT[:, c, 128 * j:128 * j + 128], "k": lambda c, j: KTt[:, c, 128 * j:128 * j + 128],
                "a": lambda c, j: GXt[:, c, j, 0, :], "v": lambda c, j: Vr[:, c, 128 * j:128 * j + 128]}
        for n, nm in enumerate(("b", "k", "a", "v")):
            dst = spaces[n].rearrange("p c t -> p (c t)").rearrange("p (j c t) -> p j c t", j=2, c=4)
            TM[nm] = dst
            tmt[nm] = []
            for j in range(2):
                b = 4 + (2 * n + j) % 4
                for c in range(4):
                    m = mm(ps[:, b, c * 128:(c + 1) * 128], srcs[nm](c, j), ident, 1, 1, [tpe, tk_, bank[b] if c == 0 else ()], tr=True)
                x = cp("dve", dst[:, j], ps[:, b, :].rearrange("p (c t) -> p c t", c=4), [m])
                bank[b] = [x]
                tmt[nm].append(x)
        SA = d4.rearrange("p c t -> p (c t)").rearrange("p (j h v) -> p j h v", j=2, h=8)
        UT = Rr.rearrange("p c t -> p (c t)").rearrange("p (q c v) -> p q c v", q=4, c=4)
        GM = get(16 * 512).rearrange("p (i n) -> p i n", i=16)
        tG = {}
        for h in range(8):
            r0, c = 64 * (h % 2), h // 2
            for j in range(2):
                i = 2 * h + j
                b = (i // 2) % 2 * 2 + (h % 2) + 4 * (j)
                rr = GXt[r0:r0 + 64, c, j].rearrange("p w t -> p (w t)")
                mm(ps[:, b, 0:256], BT[r0:r0 + 64, c, 128 * j:128 * j + 128], rr, True, True, [tk_, tmt["v"], bank[b]])
                m = mm(ps[:, b, 256:512], KTt[r0:r0 + 64, c, 128 * j:128 * j + 128], rr, True, True)
                x = tt("dve", GM[:, i, :], ps[:, b, :], KC("gmask"), ALU.mult, [m], chain=False)
                bank[b] = [x]
                tG[i] = x
        gall = list(tG.values())
        TN = XG[:, 0:2048].rearrange("p (i t) -> p i t", i=16)
        TTt = RKV[:, 4:12, :].rearrange("p c t -> p (c t)").rearrange("p (i t) -> p i t", i=16)
        x1 = op("dve", lambda e: e.tensor_copy(TN, ident.unsqueeze(1).broadcast_to([P, 16, 128])), gall)
        x2 = op("dve", lambda e: e.tensor_copy(TTt, ident.unsqueeze(1).broadcast_to([P, 16, 128])))
        l0 = KC("lv0").bitcast(U32)
        t0m = KC("lt0").bitcast(U32)
        tT = {}
        for q in range(4):
            b = q
            for w in range(4):
                i = 4 * q + w
                m = mm(ps[:, b, w * 128:(w + 1) * 128], GM[:, i, 0:128], ident, True, True, [x2, bank[b] if w == 0 else ()])
            op("dve", lambda e, q=q: e.copy_predicated(TTt[:, 4 * q:4 * q + 4, :], t0m.unsqueeze(1).broadcast_to([P, 4, 128]),
                                                       GM[:, 4 * q:4 * q + 4, 0:128]))
            x = op("dve", lambda e, q=q, b=b: e.copy_predicated(
                TN[:, 4 * q:4 * q + 4, :], l0.unsqueeze(1).broadcast_to([P, 4, 128]), ps[:, b, :].rearrange("p (w t) -> p w t", w=4)), [m])
            bank[b] = [x]
            tT[q] = x
        for n in range(1, 6):
            lv = KC(f"lv{n}").bitcast(U32).unsqueeze(1).broadcast_to([P, 4, 128])
            lt = KC(f"lt{n}").bitcast(U32).unsqueeze(1).broadcast_to([P, 4, 128])
            tx = {}
            for q in range(4):
                b = q
                for w in range(4):
                    i = 4 * q + w
                    m = mm(ps[:, b, w * 128:(w + 1) * 128], GM[:, i, 0:128], TN[:, i, :], True, True, [tT[q], bank[b] if w == 0 else ()])
                tx[q] = cp("act", XX[:, 4 * q:4 * q + 4, :], ps[:, b, :].rearrange("p (w t) -> p w t", w=4), [m])
                bank[b] = [tx[q]]
            for q in range(4):
                b1, b2 = 4 + (2 * q) % 4, 4 + (2 * q + 1) % 4
                for w in range(4):
                    i = 4 * q + w
                    m2 = mm(ps[:, b2, w * 128:(w + 1) * 128], XX[:, i, :], TTt[:, i, :], True, True, [tx[q], bank[b2] if w == 0 else ()])
                m1 = None
                if n < 5:
                    for w in range(4):
                        i = 4 * q + w
                        m1 = mm(ps[:, b1, w * 128:(w + 1) * 128], TTt[:, i, :], XX[:, i, :], True, True, [tx[q], bank[b1] if w == 0 else ()])
                x = op("dve", lambda e, q=q, b2=b2, lt=lt: e.copy_predicated(
                    TTt[:, 4 * q:4 * q + 4, :], lt, ps[:, b2, :].rearrange("p (w t) -> p w t", w=4)), [m2, m1])
                bank[b2] = [x]
                if n < 5:
                    x = op("dve", lambda e, q=q, b1=b1, lv=lv: e.copy_predicated(
                        TN[:, 4 * q:4 * q + 4, :], lv, ps[:, b1, :].rearrange("p (w t) -> p w t", w=4)), [m1])
                    bank[b1] = [x]
                tT[q] = x
        AV = TN[:, 0:8, :].rearrange("p n t -> p (n t)").rearrange("p (i v) -> p i v", i=16)
        for i in range(16):
            h, j = divmod(i, 2)
            b = i // 8
            m = mm(ps[:, b, (i % 8) * 64:(i % 8) * 64 + 64], GM[:, i, 256:384], TM["v"][:, j, h // 2, 64 * (h % 2):64 * (h % 2) + 64], True, True,
                   [tT[3], tmt["v"], bank[b] if i % 8 == 0 else ()])
        for b in range(2):
            tav = cp("dve", AV[:, 8 * b:8 * b + 8, :], ps[:, b, :].rearrange("p (i v) -> p i v", i=8), [m])
            bank[b] = [tav]
        WT = XX[:, 0:8, :].rearrange("p (c j) t -> p c j t", c=4)
        for i in range(16):
            h, j = divmod(i, 2)
            r0, c = 64 * (h % 2), h // 2
            b = 2 + c // 2
            o = ((c % 2) * 2 + j) * 128
            m = mm(ps[r0:r0 + 64, b, o:o + 128], TM["a"][:, j, c, r0:r0 + 64], TTt[:, i, :], True, True,
                   [tT[0], tT[1], tT[2], tT[3], tmt["a"], bank[b] if i % 8 == 0 else ()], skip=True)
        for b in range(2):
            twt = cp("dve", WT[:, 2 * b:2 * b + 2], ps[:, 2 + b, :].rearrange("p (c j t) -> p c j t", c=2, j=2), [m])
            bank[2 + b] = [twt]
        tu = None
        tsa = {}
        for q in range(4):
            j, b0 = q // 2, 64 * (q % 2)
            for h in range(8):
                r0, c = 64 * (h % 2), h // 2
                bb = 4 + h % 2
                o = c * 64
                if q:
                    mm(ps[b0:b0 + 64, bb, o:o + 64], WT[r0:r0 + 64, c, j, b0:b0 + 64], UT[r0:r0 + 64, q, c, :], True, False,
                       [tu, twt, bank[bb]], skip=True)
                m = mm(ps[b0:b0 + 64, bb, o:o + 64], TTt[:, 2 * h + j, b0:b0 + 64], AV[:, 2 * h + j, :], q == 0, True,
                       [tav, twt, bank[bb]], skip=True)
            for pr in range(2):
                x = cp("dve", SA[b0:b0 + 64, j, :, :].rearrange("p (c r) v -> p c r v", r=2)[:, :, pr, :],
                       ps[b0:b0 + 64, 4 + pr, 0:256].rearrange("p (c v) -> p c v", c=4), [m])
                bank[4 + pr] = [x]
            tsa[q] = x
            if q < 3:
                for h in range(8):
                    r0, c = 64 * (h % 2), h // 2
                    o = c * 64
                    mm(ps[r0:r0 + 64, 6, o:o + 64], TM["k"][b0:b0 + 64, j, c, r0:r0 + 64], TM["v"][b0:b0 + 64, j, c, r0:r0 + 64], True, False,
                       [tmt["v"], tmt["k"], tmt["b"], bank[6]], skip=True)
                    m = mm(ps[r0:r0 + 64, 6, o:o + 64], TM["b"][b0:b0 + 64, j, c, r0:r0 + 64], SA[b0:b0 + 64, j, h, :], False, True, [x], skip=True)
                src = ps[:, 6, 0:256].rearrange("p (c v) -> p c v", c=4)
                un = UT[:, q + 1]
                if q:
                    x = tt("dve", un, src, UT[:, q], ALU.add, [m])
                    bank[6] = [x]
                    tu = tt("dve", un, un, PPe[:, q, :].unsqueeze(2).broadcast_to([P, 4, 64]), ALU.mult)
                else:
                    tu = tt("dve", un, src, PPe[:, q, :].unsqueeze(2).broadcast_to([P, 4, 64]), ALU.mult, [m])
                    bank[6] = [tu]
        for h in range(8):
            r0, c = 64 * (h % 2), h // 2
            b = 2 * (h % 2) + c // 2
            for j in range(2):
                o = (c % 2) * T + j * 128
                out = ps[r0:r0 + 64, b, o:o + 128]
                i = 2 * h + j
                mm(out, TM["v"][:, j, c, r0:r0 + 64], GM[:, i, 384:512], True, False, [tsa[3], tu, bank[b]], skip=True)
                m = mm(out, SA[:, j, h, :], GM[:, i, 128:256], False, j == 0 and False, [], skip=True)
                for qq in (2 * j, 2 * j + 1):
                    if qq == 0:
                        continue
                    m = mm(ps[r0:r0 + 64, b, o + 64 * (qq % 2):o + 64 * (qq % 2) + 64], UT[r0:r0 + 64, qq, c, :],
                           GXt[r0:r0 + 64, c, j, 1, 64 * (qq % 2):64 * (qq % 2) + 64], False, True, [], skip=True)
        Y = RKV[:, 0:4, :]
        for pr in range(2):
            x = cp("dve", Y[64 * pr:64 * pr + 64], ps[64 * pr:64 * pr + 64, 2 * pr:2 * pr + 2, :].rearrange("p b (c t) -> p (b c) t", c=2), [m])
            bank[2 * pr] = bank[2 * pr + 1] = [x]
        Y2 = RKV[:, 4:8, :]

        def headsum(src, after, b0=4):
            for c in range(4):
                m = mm(ps[:, b0 + c // 2, (c % 2) * T:(c % 2) * T + T], KC("bones"), src[:, c, :], True, True, [after, bank[b0 + c // 2] if c % 2 == 0 else ()])
            return m

        m = headsum(Y, [x])
        x = stt(Y, pv, -1.0 / 64, Y, ALU.mult, ALU.add, [m])
        bank[4] = bank[5] = [x]
        x = tt("dve", Y2, Y, Y, ALU.mult)
        m = headsum(Y2, [x])
        x = ts("dve", Y2, pv, 1.0 / 64, 64e-5, ALU.mult, ALU.add, after=[m])
        bank[4] = bank[5] = [x]
        rsq(Y2, Y2, pw=-0.5)
        tt("dve", Y, Y, Y2, ALU.mult)
        for c in range(4):
            ts("dve", Y[:, c, :], Y[:, c, :], C("lnx_g", c, c + 1), C("lnx_b", c, c + 1), ALU.mult, ALU.add)
        tt("dve", Y, Y, BN, ALU.add)
        tya = tt("dve", Y, Y, GG_, ALU.mult, [outs[2]])
        tmg = proj_p("pa", Y, tya, 0, True, 6)
        guard[0] = [tmg, g.last["pe"], g.last["act"], g.last["dve"]]
        enable({"moed"})
        r = []
        for gi in range(4):
            s = take(("wout2", gi))
            w = s.ap.rearrange("p (k n) -> p k n", k=8)
            b = gi
            for jj in range(2):
                for k in range(8):
                    m = mm(ps[:, b, jj * T:(jj + 1) * T], w[:, k, jj * 128:(jj + 1) * 128], MG[:, k, :], k == 0, k == 7,
                           [s.t, tmg, bank[b] if k == 0 and jj == 0 else ()])
            done(s, m)
            for jj in range(2):
                c = 2 * gi + jj
                x = stt(XT[:, c, :], ps[:, b, jj * T:(jj + 1) * T], MOD[:, 16 + c:17 + c], XT[:, c, :], ALU.mult, ALU.add, [m], chain=False)
            bank[b] = [x]
            r.append(x)
        xt = r
        ht = norm(gm[:, 8:16], xt, 1e-6, shift=MOD[:, 24:32], gaintok=[tgm], outfree=[m])
        get = carve((7168, RB))
        LG = get(2 * 36).rearrange("p (a n) -> p a n", a=2)
        for th in range(2):
            for k in range(8):
                m = mm(ps[:, 4 + th, 0:36], SQ[:, k, th * 128:(th + 1) * 128], C("wre", 36 * k, 36 * k + 36), k == 0, k == 7,
                       [ht[k], bank[4 + th] if k == 0 else ()])
        x = tt("dve", LG, ps[:, 4:6, 0:36], C("bre").unsqueeze(1).broadcast_to([P, 2, 36]), ALU.add, [m])
        bank[4] = bank[5] = [x]
        st8 = get(32 * 2).rearrange("p (n a) -> p n a", a=2)
        gsel = get(8).rearrange("p (a g) -> p a g", a=2)
        le = LG[:, :, 4:36].rearrange("p a (g e) -> p a g e", g=4)
        lg = LG[:, :, 0:4]
        op("dve", lambda e: e.tensor_reduce(st8[:, 0, :], lg, AX.X, ALU.max))
        b4 = st8[:, 0, :].unsqueeze(2).broadcast_to([P, 2, 4])
        tt("dve", gsel, lg, b4, ALU.subtract)
        eg = get(8).rearrange("p (a g) -> p a g", a=2)
        x = ts("dve", gsel, gsel, 0.0, None, ALU.is_ge)
        x = tt("dve", eg, lg, b4, ALU.subtract)
        x = act(eg, eg, ACT.Exp, [x])
        op("dve", lambda e: e.tensor_reduce(st8[:, 1, :], eg, AX.X, ALU.add), [x])
        op("dve", lambda e: e.reciprocal(st8[:, 1, :], st8[:, 1, :]))
        for gi in range(1, 4):
            for g2 in range(gi):
                stt(gsel[:, :, gi], gsel[:, :, g2], 0.0, gsel[:, :, gi], ALU.is_equal, ALU.mult)
        gm1 = get(8).rearrange("p (a g) -> p a g", a=2)
        ts("dve", gm1, gsel, 1.0, 1e30, ALU.subtract, ALU.mult)
        EW = get(80).rearrange("p (a n) -> p a n", a=2)
        op("dve", lambda e: e.memset(EW, -3e38))
        EL = EW[:, :, 0:32].rearrange("p a (g e) -> p a g e", g=4)
        tt("dve", EL, le, gm1.unsqueeze(3).broadcast_to([P, 2, 4, 8]), ALU.add)
        ELf = EW[:, :, 0:32]
        WKf = get(80).rearrange("p (a n) -> p a n", a=2)
        M8 = get(32).rearrange("p (a n) -> p a n", a=2)
        for a in range(2):
            op("dve", lambda e, a=a: e.max(M8[:, a, 0:8], EW[:, a, :]))
            op("dve", lambda e, a=a: e.memset(M8[:, a, 8:16], -3e38))
            op("dve", lambda e, a=a: e.tensor_copy(M8[:, a, 8:10], M8[:, a, 0:2]))
            op("dve", lambda e, a=a: e.match_replace(WKf[:, a, :], M8[:, a, 8:16], EW[:, a, :], -3e38))
        sel2 = get(64).rearrange("p (a n) -> p a n", a=2)
        ts("dve", sel2, WKf[:, :, 0:32], -2e38, None, ALU.is_lt)
        tt("dve", ELf, ELf, M8[:, :, 0:1].broadcast_to([P, 2, 32]), ALU.subtract)
        x = ts("dve", ELf, ELf, -200.0, None, ALU.max)
        x = act(ELf, ELf, ACT.Exp, [x])
        tt("dve", ELf, ELf, sel2, ALU.mult, [x])
        op("dve", lambda e: e.tensor_reduce(st8[:, 2, :], ELf, AX.X, ALU.add))
        op("dve", lambda e: e.reciprocal(st8[:, 2, :], st8[:, 2, :]))
        tt("dve", st8[:, 2, :], st8[:, 2, :], st8[:, 1, :], ALU.mult)
        x = tt("dve", ELf, ELf, st8[:, 2, :].unsqueeze(2).broadcast_to([P, 2, 32]), ALU.mult)
        for a in range(2):
            m = mm(ps[0:32, 6, a * 128:(a + 1) * 128], ELf[:, a, :], ident, 1, 1, [x, bank[6] if a == 0 else ()], tr=True)
        CW = get(T)
        tcw = cp("dve", CW[0:32, :], ps[0:32, 6, 0:T], [m])
        bank[6] = [tcw]

        def scale_unit(u):
            b = 6 + u % 2
            m = mm(ps[:, b, 0:T], ident[0:32, u:u + 1].broadcast_to([32, 128]), CW[0:32, :], True, True,
                   [tcw, bank[b]])
            return ps[:, b, 0:T], m

        m = units("moe", 32, ht, scale_unit)
        r = []
        for c in range(8):
            x = stt(XT[:, c, :], ps[:, c // 2, (c % 2) * T:(c % 2) * T + T], MOD[:, 40 + c:41 + c], XT[:, c, :], ALU.mult, ALU.add, [m[c // 2]], chain=False)
            r.append(x)
            bank[c // 2] = [x]
        ht = norm(gm[:, 16:24], r, 1e-6, shift=MOD[:, 48:56], gaintok=[tgm], split=False)
        for n in range(4):
            to = g.dma("sp", lambda e, n=n: e.dma_start(OUT[:, 2 * n:2 * n + 2, :], SQ[:, 2 * n:2 * n + 2, :]), osem, 16 * (n + 1), [ht[2 * n + 1]])
        op("sp", lambda e: e.wait_ge(osem, 64) and None, [])
        assert st["take"] == len(order)
        block = ctx.enter_context(nc.Block())
        g.emit(block)


def pack_weights(i):
    def units(tag, wg, wu, wd):
        n = wd.shape[0] // 256 if wd.ndim == 2 else wd.shape[0]
        for u in range(n):
            if wd.ndim == 2:
                gg, uu, dd = wg[:, 256 * u:256 * u + 256], wu[:, 256 * u:256 * u + 256], wd[256 * u:256 * u + 256]
            else:
                gg, uu, dd = wg[u], wu[u], wd[u]
            out[(tag + "g", u)] = kcols(gg)
            out[(tag + "u", u)] = kcols(uu)
            out[(tag + "d", u)] = kcols(dd)

    def kcols(w):
        k = w.shape[0] // 128
        return w.reshape(k, 128, w.shape[1]).transpose(1, 0, 2).reshape(128, -1)

    out = {}
    for l in range(2):
        units(f"f1_{l}", i["ffn1_w_gate"][l], i["ffn1_w_up"][l], i["ffn1_w_down"][l])
        units(f"f2_{l}", i["ffn2_w_gate"][l], i["ffn2_w_up"][l], i["ffn2_w_down"][l])
    w = i["ev_w_in"][0]
    b = [0, 512, 1280, 1472, 1664, 1856, 2048, 2240, 2432, 2468]
    a_, q, kc, vc, ksl, vsl, kw, vw, gl = [w[:, b[n]:b[n + 1]] for n in range(9)]
    ev = np.concatenate([a_, q, ksl, kw, kc, vc, vsl, vw, gl], 1)
    w = i["od_w_in"][0]
    sz = [512, 64, 64, 128, 32, 4, 512, 512, 512]
    b = [0]
    for s in sz:
        b.append(b[-1] + s)
    qc, kc, vc, qi, ki, wi, qd, kd, vd = [w[:, b[n]:b[n + 1]] for n in range(9)]
    od = np.concatenate([qc, kc, qd, kd, vc, vd, qi, ki, wi], 1)
    for tag, m in (("evin", ev), ("odin", od)):
        m = np.concatenate([m, np.zeros((1024, 2560 - m.shape[1]), m.dtype)], 1)
        for gi in range(5):
            for a in range(2):
                out[(tag, gi, a)] = kcols(m[512 * a:512 * a + 512, 512 * gi:512 * gi + 512])
    for tag, n in (("cmpk", "ev_cmp_w1_k"), ("cmpv", "ev_cmp_w1_v")):
        for a in range(2):
            out[(tag, a)] = kcols(i[n][0][1024 * a:1024 * a + 1024])
    for tag, m in (("evout", i["ev_w_out"][0]), ("odout", i["od_w_out"][0]), ("win2", i["w_in_2"][0]), ("wout2", i["w_out_2"][0]),
                   ("ada", np.concatenate([i["w_ada_2"][0], i["w_ada_f_2"]], 1))):
        for gi in range(m.shape[1] // 256):
            out[(tag, gi)] = kcols(m[:, 256 * gi:256 * gi + 256])
    for tag, m in (("pa", i["p_a_2"][0]), ("pb", i["p_b_2"][0])):
        for gi in range(2):
            out[(tag, gi)] = kcols(m[:, 512 * gi:512 * gi + 512])
    units("moe", i["w1e_2"][0], i["w3e_2"][0], i["w2e_2"][0])
    order = slot_order()
    W = np.empty((len(order), P, SLOT), np.float32)
    for n, k in enumerate(order):
        W[n] = out[k]
    return W


def pack_cols(i):
    a = np.zeros((P, NCOL), np.float32)

    def put(n, v):
        o, w = COFF[n]
        a[:v.shape[0], o:o + w] = v.reshape(v.shape[0], w)

    def col(v):
        return v.reshape(-1, P).T

    for l in range(2):
        put(f"n1_{l}", col(i["ffn1_norm"][l]))
        put(f"nm_{l}", col(i["mix_norm"][l]))
        put(f"n2_{l}", col(i["ffn2_norm"][l]))
    put("nf", col(i["final_norm"]))
    put("g_mix", col(i["g_mix_2"][0]))
    put("g_ffn", col(i["g_ffn_2"][0]))
    put("g_final", col(i["g_final_2"]))
    put("c", col(i["c_2"][0]))
    put("b_ada", col(np.concatenate([i["b_ada_2"][0], i["b_ada_f_2"]])))
    put("mu_rkv", col(i["mu_rkv_2"][0]))
    put("mu_wag", np.ascontiguousarray(i["mu_wag_2"][0].reshape(3, 8, P).transpose(2, 0, 1)).reshape(P, 24))
    for n, k in (("w0", "w0_2"), ("a0", "a0_2"), ("k_k", "k_k_2"), ("k_a", "k_a_2"), ("lnx_g", "lnx_g_2"), ("lnx_b", "lnx_b_2"),
                 ("conv_b", "conv_b_2"), ("b_r", "b_rgate_2"), ("b_i", "b_igate_2"), ("lam", "lam_2"), ("r_k", "r_k_2")):
        put(n, col(i[k][0].reshape(-1)))
    put("conv_w", i["conv_w_2"][0][:, 0, :].reshape(4, 4, P).transpose(2, 1, 0))
    put("sgu_b", i["ev_sgu_b"][0].T)
    put("sgu_wT", i["ev_sgu_w"][0].transpose(2, 0, 1))
    put("sgu_n", np.broadcast_to(i["ev_sgu_norm"][0][None, :], (P, 256)))
    for n, k in (("w2k", "ev_cmp_w2_k"), ("w2v", "ev_cmp_w2_v")):
        put(n, i[k][0].reshape(2, P, 64).transpose(1, 0, 2))
    for n, k in (("pos_k", "ev_cmp_pos_k"), ("pos_v", "ev_cmp_pos_v")):
        put(n, i[k][0].reshape(16, P).T)
    for n, k in (("lw1", "w1_2"), ("la1", "a1_2"), ("lg1", "g1_2")):
        m = i[k][0]
        put(n, m.reshape(8, P, m.shape[1]).transpose(1, 0, 2))
    for n, k in (("lw2", "w2_2"), ("la2", "a2_2"), ("lg2", "g2_2")):
        put(n, i[k][0])
    for n, k in (("wr", "w_rgate_2"), ("wi", "w_igate_2")):
        m = np.zeros((P, 4, P), np.float32)
        for c in range(4):
            m[0:64, c, 0:64] = i[k][0][2 * c]
            m[64:128, c, 64:128] = i[k][0][2 * c + 1]
        put(n, m)
    m = np.concatenate([i["w_rg_2"][0], i["w_re_2"][0]], 1)
    put("wre", m.reshape(8, P, 36).transpose(1, 0, 2))
    put("bre", np.broadcast_to(np.concatenate([i["b_rg_2"][0], i["b_re_2"][0]])[None, :], (P, 36)))
    return a


def kernel(**inputs):
    import concourse.bacc as _bacc
    from concourse.bass_utils import run_bass_kernel_spmd as _run

    i = {k: np.asarray(v) for k, v in inputs.items()}
    nc = _bacc.Bacc("TRN2", target_bir_lowering=False, num_devices=1)
    arrays = {
        "in_w": pack_weights(i), "in_s": pack_cols(i), "in_k": const_array(),
        "in_x": np.ascontiguousarray(i["x"][0].T.reshape(8, P, T).transpose(1, 0, 2)),
        "in_p": np.ascontiguousarray(i["positions"][0].reshape(2, P).T),
    }
    args = [nc.dram_tensor(n, a.shape, mybir.dt.from_np(a.dtype), kind="ExternalInput").ap() for n, a in arrays.items()]
    out = nc.dram_tensor("out_0", (P, 8, T), F32, kind="ExternalOutput").ap()
    build(nc, *args, out)
    r = _run(nc, [arrays], core_ids=[0])
    y = r.results[0]["out_0"]
    return np.ascontiguousarray(y.transpose(1, 0, 2).reshape(D, T).T)[None]
```

```python
from contextlib import ExitStack

import numpy as np
import concourse.bass as bass
from concourse import mybir

ALU = mybir.AluOpType
ACT = mybir.ActivationFunctionType
F32 = mybir.dt.float32
F32R = mybir.dt.float32r
I32 = mybir.dt.int32
U32 = mybir.dt.uint32
AX = mybir.AxisListType

P = 128
T = 256
D = 1024
NEG = -1e30
RING = 4
SLOT = 2048


def ada_at(tag, u):
    return tag in ("f1_0", "f2_0", "f1_1", "f2_1") and u < 10 and (tag != "f1_0" or u > 7)


SPLIT_TAGS = {a + b for a in ("f1_0", "f2_0", "f1_1", "f2_1", "moe") for b in "gud"} | {"evin", "evout", "odin", "odout", "win2", "wout2"}
NAR = 30000
SRING = 5

UNITS = {"ffn": 11, "moe": 32}


def slot_order():
    o = []

    ada = [0]

    def units(tag, n):
        for u in range(n):
            o.extend([(tag + "g", u), (tag + "u", u), (tag + "d", u)])
            if ada_at(tag, u) and ada[0] < 32:
                o.append(("ada", ada[0]))
                ada[0] += 1

    units("f1_0", 11)
    o.extend([("evin", g, a) for g in range(5) for a in range(2)])
    o.extend([("cmpk", 0), ("cmpk", 1), ("cmpv", 0), ("cmpv", 1)])
    o.extend([("evout", g) for g in range(4)])
    units("f2_0", 11)
    units("f1_1", 11)
    o.extend([("odin", g, a) for g in range(5) for a in range(2)])
    o.extend([("odout", g) for g in range(4)])
    units("f2_1", 11)
    assert ada[0] == 32
    o.extend([("win2", g) for g in range(18)])
    o.extend([("pb", g) for g in range(2)] + [("pa", g) for g in range(2)])
    o.extend([("wout2", g) for g in range(4)])
    units("moe", 32)
    return o


COLS = [
    ("n1_0", 8), ("nm_0", 8), ("n2_0", 8), ("n1_1", 8), ("nm_1", 8), ("n2_1", 8), ("nf", 8),
    ("g_mix", 8), ("g_ffn", 8), ("g_final", 8), ("c", 8), ("b_ada", 64),
    ("mu_rkv", 12), ("mu_wag", 24), ("w0", 4), ("a0", 4), ("k_k", 4), ("k_a", 4), ("r_k", 4),
    ("lnx_g", 4), ("lnx_b", 4), ("conv_w", 16), ("conv_b", 4), ("b_r", 4), ("b_i", 4), ("lam", 4),
    ("sgu_b", 4),
    ("sgu_wT", 512), ("sgu_n", 256), ("w2k", 128), ("w2v", 128), ("pos_k", 16), ("pos_v", 16),
    ("lw1", 512), ("la1", 512), ("lg1", 1024), ("lw2", 512), ("la2", 512), ("lg2", 512),
    ("wr", 512), ("wi", 512), ("wre", 288), ("bre", 36),
]
CONSTS = [
    ("ident", 128), ("ones", 128), ("bones", 128), ("triT", 128), ("madd0", 128), ("madd1", 256),
    ("cm01", 30), ("cmadd", 30), ("inv", 8), ("gmask", 512), ("seg", 256),
] + [(f"lv{m}", 128) for m in range(6)] + [(f"lt{m}", 128) for m in range(6)]


def offsets(spec):
    at, out = 0, {}
    for n, w in spec:
        out[n] = (at, w)
        at += w
    return out, at


COFF, NCOL = offsets(COLS)
KOFF, NCON = offsets(CONSTS)


def const_array():
    a = np.zeros((P, NCON), np.float32)

    def put(n, v):
        o, w = KOFF[n]
        a[:v.shape[0], o:o + w] = v.reshape(v.shape[0], w)

    i = np.arange(P)
    put("ident", np.eye(P))
    put("ones", np.ones((P, P)))
    put("bones", (i[:, None] // 64 == i[None, :] // 64) * 1.0)
    put("triT", (i[:, None] <= i[None, :]) * 1.0)
    tri = np.where(i[None, :] <= i[:, None], 0.0, NEG)
    put("madd0", tri)
    put("madd1", np.concatenate([np.zeros((P, P)), tri], 1))
    t = i[:, None, None] + 128 * np.arange(2)[None, :, None]
    ok = (np.arange(15)[None, None, :] * 16 + 31) <= t
    put("cm01", ok * 1.0)
    put("cmadd", np.where(ok, 0.0, NEG))
    inv = np.float32(500000.0) ** (-np.arange(0, 16, 2, dtype=np.float32) / np.float32(16))
    put("inv", np.broadcast_to(inv[None, :], (P, 8)))
    same = i[:, None] // 64 == i[None, :] // 64
    su = same & (i[:, None] < i[None, :])
    u = same & (i[:, None] <= i[None, :])
    put("gmask", np.stack([su, u, su, u], 1) * 1.0)
    put("seg", np.broadcast_to((np.arange(256) % 64 != 0)[None, :] * 1.0, (P, 256)))
    for n in range(6):
        m = 1 << n
        lo = (i[:, None] // (2 * m) == i[None, :] // (2 * m)) & (i[:, None] // m % 2 == 1) & (i[None, :] // m % 2 == 0)
        put(f"lv{n}", lo * 1.0)
        put(f"lt{n}", lo.T * 1.0)
    return a


class Tok:

    def __init__(self, sem=None, val=None):
        self.sem, self.val, self.used = sem, val, False


class Prog:

    ENG = ("pe", "act", "dve", "pool", "sp")

    def __init__(self, nc, ctx):
        self.nc = nc
        self.q = {e: [] for e in self.ENG}
        self.sem = {e: ctx.enter_context(nc.semaphore("s_" + e)) for e in self.ENG}
        self.last = {e: None for e in self.ENG}

    def op(self, e, fn, after=(), chain=None):
        t = Tok(self.sem[e])
        after = [a for a in flat(after) if a is not None]
        if (chain if chain is not None else e in ("act", "dve", "pool")) and self.last[e] is not None:
            after.append(self.last[e])
        for a in after:
            a.used = True
        self.q[e].append((fn, after, t, 1))
        if fn is not None:
            self.last[e] = t
        return t

    def dma(self, e, fn, sem, val, after=()):
        t = Tok(sem, val)
        after = [a for a in flat(after) if a is not None]
        for a in after:
            a.used = True
        self.q[e].append((fn, after, t, 16))
        return t

    def emit(self, block):
        for e in self.ENG:
            n = 0
            for fn, after, t, inc in self.q[e]:
                if inc == 1 and t.used:
                    n += 1
                    t.val = n
        reg = {"pe": block.tensor, "act": block.scalar, "dve": block.vector, "pool": block.gpsimd, "sp": block.sync}
        for e in self.ENG:
            def body(eng, e=e):
                seen = {}
                for fn, after, t, inc in self.q[e]:
                    need = {}
                    for a in after:
                        if a.val > seen.get(id(a.sem), 0):
                            need[id(a.sem)] = max(need.get(id(a.sem), (0, None))[0], a.val), a.sem
                    for k, (v, s) in need.items():
                        eng.wait_ge(s, v)
                        seen[k] = v
                    ins = fn(eng) if fn is not None else None
                    if ins is not None and (inc == 16 or t.used):
                        ins.then_inc(t.sem, inc)
            reg[e](body)


def flat(x):
    if x is None or isinstance(x, Tok):
        return [x] if x is not None else []
    out = []
    for y in x:
        out += flat(y)
    return out


def build(nc, W, S, K, XI, POS, OUT):
    with ExitStack() as ctx:
        def sb(name, shape, dt=F32):
            return ctx.enter_context(nc.sbuf_tensor(name, shape, dt))

        g = Prog(nc, ctx)
        op = g.op
        order = slot_order()

        ring = sb("ring", [P, RING, SLOT])
        cols = sb("cols", [P, NCOL])
        cons = sb("cons", [P, NCON])
        XT = sb("XT", [P, 8, T])
        SQ = sb("SQ", [P, 8, T])
        RS = sb("RS", [P, T])
        pos = sb("pos", [P, 2], I32)
        small = sb("small", [P, 512])
        acc = sb("acc", [P, 2, 256])
        with ExitStack() as c2:
            AR = c2.enter_context(nc.sbuf_tensor("AR", [P, NAR], F32))
        with ExitStack() as c2:
            HH = c2.enter_context(nc.sbuf_tensor("HH", [P, 8, T], F32R))
            HL = c2.enter_context(nc.sbuf_tensor("HL", [P, 8, T], F32R))
            AH = c2.enter_context(nc.sbuf_tensor("AH", [P, 4, T], F32R))
            AL = c2.enter_context(nc.sbuf_tensor("AL", [P, 4, T], F32R))
            AF = c2.enter_context(nc.sbuf_tensor("AF", [P, 4, T], F32))
            WGAP = c2.enter_context(nc.sbuf_tensor("WGAP", [P, NAR - 7168 - SRING * 4096], F32))
            WH = c2.enter_context(nc.sbuf_tensor("WH", [P, SRING, SLOT], F32R))
            WL = c2.enter_context(nc.sbuf_tensor("WL", [P, SRING, SLOT], F32R))
        with ExitStack() as c2:
            c2.enter_context(nc.sbuf_tensor("OGAP", [P, 5120], F32))
            OH = c2.enter_context(nc.sbuf_tensor("OH", [P, 8, T], F32R))
            OL = c2.enter_context(nc.sbuf_tensor("OL", [P, 8, T], F32R))
        ps = ctx.enter_context(nc.psum_tensor("ps", [P, 8, 512], F32))
        wsem = [ctx.enter_context(nc.semaphore(f"w{i}")) for i in range(RING)]
        isem = [ctx.enter_context(nc.semaphore(f"i{i}")) for i in range(5)]
        osem = ctx.enter_context(nc.semaphore("o"))

        def C(n, a=None, b=None):
            o, w = COFF[n]
            a, b = (0, w) if a is None else (a, b)
            return cols[:, o + a:o + b]

        def KC(n, a=None, b=None):
            o, w = KOFF[n]
            a, b = (0, w) if a is None else (a, b)
            return cons[:, o + a:o + b]

        ident = KC("ident")

        NC0 = COFF["sgu_wT"][0]
        t_p = g.dma("act", lambda e: e.dma_start(pos[:, :], POS), isem[3], 16)
        t_x = g.dma("sp", lambda e: e.dma_start(XT[:, :, :], XI), isem[0], 16)
        t_k = g.dma("act", lambda e: e.dma_start(cons[:, :], K), isem[1], 16)
        t_c = g.dma("act", lambda e: e.dma_start(cols[:, 0:NC0], S[:, 0:NC0]), isem[2], 16)

        class Slot:
            pass

        st = {"load": 0, "take": 0}
        freed = {}

        def load(after=()):
            n = st["load"]
            if n >= len(order):
                return
            st["load"] += 1
            freed[n] = g.dma("sp", lambda e, n=n: e.dma_start(ring[:, n % RING, :], W[n]),
                             wsem[n % RING], 16 * (n // RING + 1), after)

        for _ in range(RING):
            load()
        t_c2 = g.dma("sp", lambda e: e.dma_start(cols[:, NC0:NCOL], S[:, NC0:NCOL]), isem[4], 16)

        def take(key):
            n = st["take"]
            assert order[n] == key, (order[n], key)
            st["take"] += 1
            s = Slot()
            s.t, s.n = freed[n], n
            s.ap = ring[:, n % RING, :]
            return s

        read = {}

        def done(s, tok):
            read[s.n] = tok
            while st["load"] < len(order) and st["load"] - RING in read:
                load([read[st["load"] - RING]])

        sp_st = {"n": 0, "on": 0}
        sread = {}
        order_split = [i for i, k in enumerate(order) if k[0] in SPLIT_TAGS]
        spos = {i: n for n, i in enumerate(order_split)}
        rpos, rprev, user, cyc = [], [], {}, 0
        for i in order_split:
            cyc = (cyc + 1) % SRING
            if order[i][0] == "win2" and cyc < 2:
                cyc = 2
            rpos.append(cyc)
            rprev.append(user.get(cyc))
            user[cyc] = len(rpos) - 1
        stok = {}
        ssl = {}
        guard = [None]

        def split_upto():
            while sp_st["n"] < min(len(order_split), sp_st["on"]):
                n = sp_st["n"]
                if rprev[n] is not None and rprev[n] not in sread:
                    return
                i = order_split[n]
                if i != st["take"] or i not in freed:
                    return
                s = take(order[i])
                r = rpos[n]
                prev = sread.get(rprev[n])
                hs = []
                for q in range(4):
                    c = slice(q * 512, q * 512 + 512)
                    a = op("act", lambda e, c=c, r=r, s=s: e.activation(WH[:, r, c], s.ap[:, c], ACT.Copy), [s.t, prev, guard], chain=False)
                    b = op("dve", lambda e, c=c, r=r, s=s: e.tensor_tensor(WL[:, r, c], s.ap[:, c], WH[:, r, c].bitcast(F32), ALU.subtract),
                           [s.t, prev, guard, a], chain=False)
                done(s, b)
                stok[n] = b
                sp_st["n"] += 1

        class Pair:
            def __init__(self, h, l, n=None, t=None):
                self.h, self.l, self.n, self.t = h, l, n, t

            def view(self, f):
                return Pair(f(self.h), f(self.l), self.n, self.t)

        def enable_more(n):
            sp_st["on"] += n
            split_upto()

        def enable(n_tags):
            sp_st["on"] = max([spos[i] for i in order_split if order[i][0] in n_tags]) + 1
            split_upto()

        def wtake(key):
            n = ssl.setdefault("n", 0)
            ssl["n"] = n + 1
            assert order[order_split[n]] == key, (key, order[order_split[n]])
            split_upto()
            r = rpos[n]
            return Pair(WH[:, r, :], WL[:, r, :], n, stok[n])

        def wdone(p, tok):
            sread[p.n] = tok
            split_upto()

        def mm3(out, A, B, start, stop, after=(), skip=False):
            op("pe", lambda e: e.matmul(out, A.h, B.h, start=start, stop=False, skip_group_check=skip), after)
            op("pe", lambda e: e.matmul(out, A.h, B.l, start=False, stop=False, skip_group_check=skip))
            return op("pe", lambda e: e.matmul(out, A.l, B.h, start=False, stop=stop, skip_group_check=skip))

        def mm(out, lhsT, rhs, start, stop, after=(), skip=False, tr=False):
            if tr:
                return op("pe", lambda e: e.transpose(out, lhsT, rhs), after)
            return op("pe", lambda e: e.matmul(out, lhsT, rhs, start=start, stop=stop, skip_group_check=skip), after)

        def tt(e, out, a, b, o, after=(), chain=None):
            return op(e, lambda q: q.tensor_tensor(out, a, b, o), after, chain)

        def ts(e, out, a, s1, s2, o0, o1=None, after=(), chain=None):
            if o1 is None:
                return op(e, lambda q: q.tensor_scalar(out, a, s1, None, o0), after, chain)
            return op(e, lambda q: q.tensor_scalar(out, a, s1, s2, o0, o1), after, chain)

        def rsq(out, a, after=(), pw=-0.5):
            x = act(out, a, ACT.Sqrt, [after, g.last["dve"]])
            if pw < 0:
                return op("dve", lambda q: q.reciprocal(out, out), [x])
            op("dve", None, [x], chain=False)
            return x

        def stt(out, a, s, b, o0, o1, after=(), chain=None):
            return op("dve", lambda q: q.scalar_tensor_tensor(out=out, in0=a, scalar=s, in1=b, op0=o0, op1=o1), after, chain)

        def act(out, a, f, after=(), chain=None, **kw):
            return op("act", lambda q: q.activation(out, a, f, **kw), after, chain)

        def cp(e, out, a, after=(), chain=None):
            if e == "act":
                return act(out, a, ACT.Copy, after, chain)
            return op(e, lambda q: q.tensor_copy(out, a), after, chain)

        MOD = small[:, 344:408]
        warm = small[:, 488:489]
        cs = small[:, 408:416]
        t_cs = []
        ada_free = {}

        def ada_sum(gi):
            s = take(("ada", gi))
            w = s.ap.rearrange("p (k n) -> p k n", k=8)
            a = acc[:, gi % 2, :]
            x = ts("dve", a, w[:, 0, :], cs[:, 0:1], None, ALU.mult, after=[s.t, t_cs, ada_free.get(gi - 2)], chain=False)
            for k in range(1, 8):
                x = stt(a, w[:, k, :], cs[:, k:k + 1], a, ALU.mult, ALU.add, [x], chain=False)
            done(s, x)
            return x

        def ada_out(gi, x):
            for j in range(2):
                m = mm(ps[:, 7, j:j + 1], acc[:, gi % 2, j * 128:(j + 1) * 128], KC("ones", 0, 1), True, True, [x, bank[7]])
            ada_free[gi] = m
            y = tt("dve", MOD[:, 2 * gi:2 * gi + 2], ps[:, 7, 0:2], C("b_ada", 2 * gi, 2 * gi + 2), ALU.add, [m], chain=False)
            bank[7] = [y]
            return y

        bank = {i: [] for i in range(8)}

        epsc = small[:, 489:490]
        t_eps = op("dve", lambda e: e.memset(epsc, 1e-6))

        def norm(gain, xtoks, shift=None, gaintok=(), out=SQ, bk=7, outfree=(), split=True, nextf=ACT.Silu, mid=None):
            tk = []
            for i in range(4):
                xd = xtoks[len(xtoks) // 4 * (i + 1) - 1] if len(xtoks) >= 4 else xtoks
                tk.append(act(SQ[:, 2 * i:2 * i + 2, :], XT[:, 2 * i:2 * i + 2, :], ACT.Square, [xd], chain=i == 0))
            act(warm, KC("ones", 0, 1), ACT.Sqrt, [t_k], chain=False)
            for k in range(8):
                m = mm(ps[:, bk, 0:T], KC("ones"), SQ[:, k, :], k == 0, k == 7, [tk[k // 2], t_k, bank[bk] if k == 0 else ()])
            if mid is not None:
                enable_more(1)
            a = act(RS[:, :], ps[:, bk, 0:T], ACT.Sqrt, [m, t_eps, g.last["dve"]], scale=1.0 / D, bias=epsc)
            bank[bk] = [a]
            op("dve", lambda q: q.reciprocal(RS[:, :], RS[:, :]), [a])
            act(warm, KC("ones", 0, 1), nextf, chain=False)
            r, xs, ys = [], {}, {}
            for k in range(0, 10, 2):
                if k < 8:
                    for kk in (k, k + 1):
                        x = stt(out[:, kk, :], XT[:, kk, :], gain[:, kk:kk + 1], RS[:, :], ALU.mult, ALU.mult, [t_c, gaintok, outfree], chain=kk == 0)
                        if shift is not None:
                            x = ts("dve", out[:, kk, :], out[:, kk, :], shift[:, kk:kk + 1], None, ALU.add, after=[gaintok, x], chain=False)
                    xs[k] = x
                    if split:
                        ys[k] = cp("act", HH[:, k:k + 2, :], out[:, k:k + 2, :], [x, guard], chain=False)
                k -= 2
                if k >= 0:
                    z = ()
                    if split:
                        z = tt("dve", HL[:, k:k + 2, :], out[:, k:k + 2, :], HH[:, k:k + 2, :].bitcast(F32), ALU.subtract, [ys[k], guard], chain=False)
                    r += [[xs[k], z]] * 2
            return r

        HP = [Pair(HH[:, k, :], HL[:, k, :]) for k in range(8)]

        adan, ada_x, t_mod = [0], [None], [None]

        def units(tag, n, ht, scale_unit=None, extra=None):
            firstw = [list(bank[b]) for b in range(4)]
            nb = 3 if scale_unit is None else 2
            used = {}
            readd = {}

            def down(u, j, wd, tok, last):
                per = {}
                for d in range(8):
                    first = u == 0 and j == 0 and d % 2 == 0
                    m = mm3(ps[:, d // 2, (d % 2) * T:(d % 2) * T + T], wd.view(lambda w: w[:, j * 1024 + d * 128:j * 1024 + (d + 1) * 128]),
                            Pair(AH[:, (2 * u + j) % 4, :], AL[:, (2 * u + j) % 4, :]), first, last,
                            [wd.t, tok, firstw[d // 2] if first else ()], skip=True)
                    if d % 2:
                        per[d // 2] = m
                readd[2 * u + j] = m
                if j == 1:
                    wdone(wd, m)
                return per

            pend = None
            wds = {}
            for u in range(n):
                wg, wu = wtake((tag + "g", u)), wtake((tag + "u", u))
                for j in range(2):
                    i = 2 * u + j
                    b = 4 + i % nb
                    for k in range(8):
                        mm3(ps[:, b, 0:T], wg.view(lambda w: w[:, k * 256 + j * 128:k * 256 + j * 128 + 128]), HP[k], k == 0, k == 7,
                            [wg.t, ht[k], bank[b] if k == 0 else ()])
                    for k in range(8):
                        mu = mm3(ps[:, b, T:2 * T], wu.view(lambda w: w[:, k * 256 + j * 128:k * 256 + j * 128 + 128]), HP[k], k == 0, k == 7, [wu.t])
                    if scale_unit is not None and i == 0:
                        nextcw = scale_unit(0)
                    si = i % 4
                    a = act(AF[:, si, :], ps[:, b, 0:T], ACT.Silu, [mu, used.get(i - 4), guard], chain=False)
                    x = tt("dve", AF[:, si, :], AF[:, si, :], ps[:, b, T:2 * T], ALU.mult, [a, mu], chain=False)
                    bank[b] = [x]
                    if scale_unit is not None:
                        x = tt("dve", AF[:, si, :], AF[:, si, :], nextcw[0], ALU.mult, [x, nextcw[1]], chain=False)
                        bank[6 + u % 2] = [x]
                    y = cp("act", AH[:, si, :], AF[:, si, :], [x, readd.get(i - 4)], chain=False)
                    z = tt("dve", AL[:, si, :], AF[:, si, :], AH[:, si, :].bitcast(F32), ALU.subtract, [y, readd.get(i - 4)], chain=False)
                    used[i] = z
                    if j == 1:
                        wdone(wg, mu)
                        wdone(wu, mu)
                    if pend is not None:
                        m = down(*pend, False)
                    if scale_unit is not None and j == 1 and u + 1 < n:
                        nextcw = scale_unit(u + 1)
                    if j == 0:
                        wds[u] = wtake((tag + "d", u))
                        if ada_x[0] is not None:
                            t_mod[0] = ada_out(*ada_x[0])
                            ada_x[0] = None
                        if ada_at(tag, u) and adan[0] < 32:
                            asum = ada_sum(adan[0])
                            ada_x[0] = (adan[0], asum)
                            adan[0] += 1
                            split_upto()
                    if extra is not None and (u, j) == (3, 0):
                        extra()
                    pend = (u, j, wds[u], z)
            if ada_x[0] is not None:
                t_mod[0] = ada_out(*ada_x[0])
                ada_x[0] = None
            return down(*pend, True)

        def ffn(tag, gain, xtoks, extra=None, mid=None):
            ht = norm(gain, xtoks, mid=mid)
            if mid is not None:
                enable(mid)
            m = units(tag, 11, ht, extra=extra)
            r = []
            for b in range(4):
                xv = XT[:, 2 * b:2 * b + 2, :].rearrange("p a t -> p (a t)")
                x = stt(xv, ps[:, b, :], 0.5, xv, ALU.mult, ALU.add, [m[b]], chain=False)
                bank[b] = [x]
                r.append(x)
            return r

        def proj_tok(tag, ncol, Z, ht, free=()):
            r = []
            for gi in range(5):
                w = min(512, ncol - 512 * gi)
                sl = [wtake((tag, gi, a)) for a in range(2)]
                for th in range(2):
                    b = (2 * gi + th) % 8
                    for k in range(8):
                        s = sl[k // 4]
                        m = mm3(ps[:, b, 0:w], HP[k].view(lambda h: h[:, th * 128:(th + 1) * 128]),
                                s.view(lambda v: v[:, (k % 4) * 512:(k % 4) * 512 + w]), k == 0, k == 7,
                                [s.t, ht[k], bank[b] if k == 0 else ()])
                        if th == 1 and k == 3:
                            wdone(sl[0], m)
                    if th == 1:
                        wdone(sl[1], m)
                    x = cp("act" if th else "dve", Z[:, th, 512 * gi:512 * gi + w], ps[:, b, 0:w], [m, free], chain=False)
                    bank[b] = [x]
                    r.append(x)
            return r

        def proj_out(tag, O, otoks, nxt):
            tks = []
            enable_more(1)
            for n in range(4):
                for q in range(4):
                    th, k = divmod(4 * n + q, 8)
                    m = mm(ps[:, n, q * 128:(q + 1) * 128], O[:, th, k * 128:(k + 1) * 128], ident, 1, 1,
                           [otoks, bank[n] if q == 0 else ()], tr=True)
                th, k0 = divmod(4 * n, 8)
                v = ps[:, n, :].rearrange("p (k t) -> p k t", k=4)
                oh, ol = [o[:, k0:k0 + 4, th * 128:(th + 1) * 128] for o in (OH, OL)]
                x = cp("act", oh, v, [m], chain=False)
                x = tt("dve", ol, v, oh.bitcast(F32), ALU.subtract, [x], chain=False)
                bank[n] = [x]
                tks.append(x)
            enable(nxt)
            return proj_res(tag, tks, 4, None)

        def proj_res(tag, tks, b0, gate):
            r = []
            for gi in range(4):
                s = wtake((tag, gi))
                b = b0 + gi
                for j in range(2):
                    for k in range(8):
                        m = mm3(ps[:, b, j * T:(j + 1) * T], s.view(lambda w: w[:, k * 256 + j * 128:k * 256 + j * 128 + 128]),
                                Pair(OH[:, k, :], OL[:, k, :]), k == 0, k == 7, [s.t, tks, bank[b] if k == 0 and j == 0 else ()])
                wdone(s, m)
                if gate is None:
                    xv = XT[:, 2 * gi:2 * gi + 2, :].rearrange("p a t -> p (a t)")
                    x = tt("dve", xv, ps[:, b, :], xv, ALU.add, [m], chain=False)
                else:
                    for c in (2 * gi, 2 * gi + 1):
                        x = stt(XT[:, c, :], ps[:, b, (c % 2) * T:(c % 2) * T + T], gate[:, c:c + 1], XT[:, c, :], ALU.mult, ALU.add, [m], chain=False)
                bank[b] = [x]
                r.append(x)
            return r

        posf = small[:, 0:2]
        ang = small[:, 16:32]
        kk_ = small[:, 32:48]
        cosT = small[:, 64:80]
        sinT = small[:, 80:96]
        t_rope = []

        def tables():
            t_cs.append(act(cs, C("c"), ACT.Silu, [t_c]))
            cp("dve", posf, pos[:, :], [t_p])
            for th in range(2):
                ts("dve", ang[:, th * 8:(th + 1) * 8], KC("inv"), posf[:, th:th + 1], None, ALU.mult, after=[t_k])
            MAGIC = 12582912.0
            ts("dve", kk_, ang, float(1 / (2 * np.pi)), None, ALU.mult)
            ts("dve", kk_, kk_, MAGIC, None, ALU.add)
            ts("dve", kk_, kk_, MAGIC, None, ALU.subtract)
            c1 = 6.28125
            c2 = float(np.float32(np.round((2 * np.pi - c1) * 2 ** 20) / 2 ** 20))
            c3 = float(2 * np.pi - c1 - c2)
            for c in (c1, c2, c3):
                stt(ang, kk_, -c, ang, ALU.mult, ALU.add)
            PI = 3.1415925
            ts("dve", ang, ang, PI, -PI, ALU.min, ALU.max)
            ts("dve", kk_, ang, -1.0, None, ALU.mult)
            tt("dve", kk_, kk_, ang, ALU.max)
            t = ts("dve", kk_, kk_, -1.0, float(np.pi / 2), ALU.mult, ALU.add)
            act(sinT, ang, ACT.Sin, [t])
            t_rope.append(act(cosT, kk_, ACT.Sin))

        def rope(Z, c0, nh, hd, half, tmp, after):
            zv = Z[:, :, c0:c0 + nh * hd].rearrange("p a (h d) -> p a h d", d=hd)
            x1, x2 = zv[:, :, :, 0:half], zv[:, :, :, half:2 * half]
            step = 8 // half
            sh = [P, 2, nh, half]
            cs = cosT.rearrange("p (a f s) -> p a f s", a=2, s=step)[:, :, :, 0].unsqueeze(2).broadcast_to(sh)
            sn = sinT.rearrange("p (a f s) -> p a f s", a=2, s=step)[:, :, :, 0].unsqueeze(2).broadcast_to(sh)
            n = 2 * nh * half
            t1 = tmp[:, 0:n].rearrange("p (a h f) -> p a h f", a=2, h=nh)
            t2 = tmp[:, n:2 * n].rearrange("p (a h f) -> p a h f", a=2, h=nh)
            tt("dve", t1, x1, sn, ALU.mult, [after, t_rope])
            tt("dve", t2, x2, sn, ALU.mult)
            tt("dve", x1, x1, cs, ALU.mult)
            tt("dve", x2, x2, cs, ALU.mult)
            tt("dve", x1, x1, t2, ALU.subtract)
            return tt("dve", x2, x2, t1, ALU.add)

        evn = [0]

        def ev():
            evn[0] += 1
            return "act" if evn[0] % 2 else "dve"

        def headT(Z, c0, nh, dst, after, banks, hd=64):
            r = []
            jobs = [(th, h) for th in range(2) for h in range(nh)]
            for i in range(0, len(jobs), 4):
                grp = jobs[i:i + 4]
                b = banks[(i // 4) % len(banks)]
                for q, (th, h) in enumerate(grp):
                    m = mm(ps[0:hd, b, q * 128:(q + 1) * 128], Z[:, th, c0 + h * hd:c0 + (h + 1) * hd], ident, 1, 1,
                           [after, bank[b] if q == 0 else ()], tr=True)
                x = cp(ev(), dst.rearrange("d a h t -> d (a h) t")[:, i:i + len(grp), :],
                       ps[0:hd, b, 0:128 * len(grp)].rearrange("d (h t) -> d h t", t=128), [m], chain=False)
                bank[b] = [x]
                r.append(x)
            return r

        def attention(items, SB, PT, stats, maskof, finish, side=iter(())):
            n = len(items)
            stage = {}

            def s_stage(i):
                br, th, heads, qT, kT, V, deps = items[i]
                nk = 128 * (th + 1)
                b0 = 2 * (i % 2)
                sview = ps[:, b0:b0 + 2, :].rearrange("p b n -> p (b n)")[:, 0:4 * nk]
                for q, h in enumerate(heads):
                    m = mm(sview[:, q * nk:(q + 1) * nk], qT(h)[:, th, :], kT(h)[:, 0:th + 1, :], True, True,
                           [deps, bank[b0] if q == 0 else (), bank[b0 + 1] if q == 0 else ()])
                sbv = SB[:, i % 2, 0:4 * nk].rearrange("p (h k) -> p h k", h=4)
                mk, mt = maskof(br, th)
                mk = mk.unsqueeze(1).broadcast_to([P, 4, nk])
                x = stt(sbv, sview.rearrange("p (h k) -> p h k", h=4), 0.125, mk, ALU.mult, ALU.add,
                        [m, mt, stage.get(("pt", i - 2))])
                bank[b0] = bank[b0 + 1] = [x]
                mx = stats[:, i, 0:4]
                op("dve", lambda e: e.tensor_reduce(mx, sbv, AX.X, ALU.max))
                y = ts("dve", mx, mx, -1.0, None, ALU.mult)
                yield
                for q in range(4):
                    z = act(sbv[:, q, :], sbv[:, q, :], ACT.Exp, [y], chain=False, bias=stats[:, i, q:q + 1],
                            accum_out=stats[:, i, 4 + q:5 + q])
                stage[("e", i)] = z

            def t_stage(i):
                br, th, heads, qT, kT, V, deps = items[i]
                nk = 128 * (th + 1)
                sbv = SB[:, i % 2, 0:4 * nk].rearrange("p (h k) -> p h k", h=4)
                blk = [(q, kb) for q in range(4) for kb in range(th + 1)]
                ptk = []
                for c in range(0, len(blk), 4):
                    b = 4 + (c // 4)
                    for w, (q, kb) in enumerate(blk[c:c + 4]):
                        m = mm(ps[:, b, w * 128:(w + 1) * 128], sbv[:, q, kb * 128:(kb + 1) * 128], ident, 1, 1,
                               [stage[("e", i)], bank[b] if w == 0 else ()], tr=True)
                    x = cp("dve" if c else "act", PT[:, i % 2, c * 128:c * 128 + 512], ps[:, b, :], [m, stage.get(("o", i - 2))], chain=False)
                    bank[b] = [x]
                    ptk.append(x)
                stage[("pt", i)] = m
                stage[("pe", i)] = ptk

            def o_stage(i):
                br, th, heads, qT, kT, V, deps = items[i]
                ob = 6 + i % 2
                ptk = stage[("pe", i)]
                blk = [(q, kb) for q in range(4) for kb in range(th + 1)]
                for q, h in enumerate(heads):
                    for kb in range(th + 1):
                        w = blk.index((q, kb))
                        m = mm(ps[:, ob, q * 64:(q + 1) * 64], PT[:, i % 2, w * 128:(w + 1) * 128], V(h, kb),
                               kb == 0, kb == th, [ptk, bank[ob] if q == 0 and kb == 0 else ()])
                stage[("o", i)] = m
                w = op("dve", lambda e: e.reciprocal(stats[:, i, 8:12], stats[:, i, 4:8]), [stage[("e", i)]])
                x = finish(i, items[i], ps[:, ob, 0:256].rearrange("p (h d) -> p h d", h=4), stats[:, i, 8:12], [m, w])
                bank[ob] = [x]
                return x

            for i in range(-1, n + 1):
                sg_ = s_stage(i + 1) if i + 1 < n else iter(())
                next(sg_, None)
                if 0 <= i < n:
                    t_stage(i)
                next(side, None)
                next(sg_, None)
                if i >= 1:
                    last = o_stage(i - 1)
                next(side, None)
            return last

        def carve(*segs):
            segs = [list(x) for x in segs]

            def get(n):
                for sg_ in segs:
                    if sg_[1] - sg_[0] >= n:
                        sg_[0] += n
                        return AR[:, sg_[0] - n:sg_[0]]
                raise AssertionError((n, segs))
            return get

        RB = NAR - SRING * 4096

        sp = small[:, 440:472].rearrange("p (n c) -> p n c", c=4)
        tsp = [None]

        def softplus():
            lam = C("lam")
            ts("dve", sp[:, 0], lam, -1.0, None, ALU.mult, after=[t_c])
            tt("dve", sp[:, 1], sp[:, 0], lam, ALU.max)
            x = ts("dve", sp[:, 0], sp[:, 0], 0.0, None, ALU.max)
            x = act(sp[:, 2], sp[:, 1], ACT.Exp, [x], scale=-1.0)
            ts("dve", sp[:, 3], sp[:, 2], 2.0, None, ALU.add, after=[x])
            op("dve", lambda e: e.reciprocal(sp[:, 3], sp[:, 3]))
            tt("dve", sp[:, 3], sp[:, 3], sp[:, 2], ALU.mult)
            tt("dve", sp[:, 4], sp[:, 3], sp[:, 3], ALU.mult)
            ts("dve", sp[:, 5], sp[:, 4], 1.0 / 17, 1.0 / 15, ALU.mult, ALU.add)
            for d in (13, 11, 9, 7, 5, 3, 1):
                tt("dve", sp[:, 5], sp[:, 5], sp[:, 4], ALU.mult)
                ts("dve", sp[:, 5], sp[:, 5], 1.0 / d, None, ALU.add)
            tt("dve", sp[:, 5], sp[:, 5], sp[:, 3], ALU.mult)
            stt(sp[:, 5], sp[:, 5], 2.0, sp[:, 0], ALU.mult, ALU.add)
            tsp[0] = ts("dve", sp[:, 6], sp[:, 5], -8.0, None, ALU.mult)

        xt = ffn("f1_0", C("n1_0"), [t_x], tables, {"f1_0d", "evin"})
        for e_ in ("pe", "act", "dve"):
            op(e_, None, [t_c2], chain=False)
        ht = norm(C("nm_0"), xt)
        get = carve((4096, RB))
        Z = get(2 * 2468).rearrange("p (a n) -> p a n", a=2)
        get = carve((0, 2048), (RB, NAR), (2048, 4096))
        O = get(2 * 1024).rearrange("p (a n) -> p a n", a=2)
        zt = proj_tok("evin", 2468, Z, ht)
        QN = get(3072)[0:64, :].rearrange("p (a h t) -> p a h t", a=2, h=12)
        zt_all = zt
        tqn = headT(Z, 512, 12, QN, zt_all, [0, 1])
        kv2 = get(2 * 2 * 192 * 2).rearrange("p (a w h c d) -> p a w h c d", a=2, w=2, h=3, c=2)
        t2 = []
        for a in range(2):
            for w in range(2):
                src = Z[:, a, 1664 + 192 * w:1664 + 192 * (w + 1)].rearrange("p (h d) -> p h d", h=3)
                t2.append(op("pool", lambda e, a=a, w=w, src=src: e.tensor_copy(
                    kv2[:, a, w], src.unsqueeze(2).broadcast_to([P, 3, 2, 64])), [zt_all]))
        kct = get(2 * 3 * T).rearrange("p (w h t) -> p w h t", w=2, h=3)
        ktk = []
        for w in range(2):
            for h in range(3):
                b = 2 + (3 * w + h) % 2
                for a in range(2):
                    m = mm(ps[:, b, a * 128:(a + 1) * 128], kv2[:, a, w, h].rearrange("p c d -> p (c d)"), ident, 1, 1,
                           [t2, bank[b] if a == 0 else ()], tr=True)
                x1 = cp("act", kct[0:64, w, h, :], ps[0:64, b, 0:T], [m], chain=False)
                x2 = cp("dve", kct[64:128, w, h, 0:T - 1], ps[64:128, b, 1:T], [m], chain=False)
                bank[b] = [x1, x2]
                ktk += [x1, x2]
        blk = get(2 * 16 * 45).rearrange("p (w l h n) -> p w l h n", w=2, l=16, h=3)
        btk = []
        for w, pn in enumerate(("pos_k", "pos_v")):
            for h in range(3):
                base = kct[:, w, h, :]
                lo = base.rearrange("p (n l c) -> p l n c", n=16, c=2)[:, 0:8, 0:15, 0]
                hi = base.rearrange("p (n l c) -> p l n c", n=16, c=2)[:, 0:8, 1:16, 0]
                pv = C(pn).unsqueeze(2)
                tt("dve", blk[:, w, 0:8, h, :], lo, pv[:, 0:8].broadcast_to([P, 8, 15]), ALU.add, [ktk, t_c], chain=False)
                btk.append(tt("dve", blk[:, w, 8:16, h, :], hi, pv[:, 8:16].broadcast_to([P, 8, 15]), ALU.add, [ktk], chain=False))
        uv = get(2 * 512).rearrange("p (a n) -> p a n", a=2)
        tuv = act(uv, Z[:, :, 0:512], ACT.Gelu_apprx_tanh, [zt_all])
        tmp = get(2 * 576)
        trq = rope(Z, 512, 18, 64, 8, tmp, [zt_all, tqn])
        hd = get(2 * 3 * 128).rearrange("p (c g r n) -> p c g r n", c=2, g=3, r=4)
        op("dve", lambda e: e.memset(hd, 0.0), [zt_all])
        VB = get(3 * 256).rearrange("p (g r d) -> p g r d", g=3, r=4)
        op("pool", lambda e: e.memset(VB, 0.0), [zt_all])
        pc = get(2 * 12 * 32).rearrange("p (a h n) -> p a h n", a=2, h=12)
        tms = op("pool", lambda e: e.memset(pc, 0.0), [zt_all])
        v = uv[:, :, 256:512]
        ssq = small[:, 100:102]
        for a in range(2):
            op("dve", lambda e, a=a: e.tensor_tensor_reduce(out=SQ[:, a, :], in0=v[:, a, :], in1=v[:, a, :], scale=1.0, scalar=0.0,
                                                            op0=ALU.mult, op1=ALU.add, accum_out=ssq[:, a:a + 1]), [tuv, ht])
        ts("dve", ssq, ssq, 1.0 / 256, 1e-6, ALU.mult, ALU.add)
        rsq(ssq, ssq, pw=-0.5)
        for a in range(2):
            tvn = stt(v[:, a, :], v[:, a, :], ssq[:, a:a + 1], C("sgu_n"), ALU.mult, ALU.mult)
        sw = C("sgu_wT").rearrange("p (g t) -> p g t", g=4)
        tsw = tt("dve", sw, sw, KC("triT").unsqueeze(1).broadcast_to([P, 4, 128]), ALU.mult)
        hid = get(2 * 2 * 45).rearrange("p (w c n) -> p w c n", w=2, c=2)
        hidt = get(2 * 256).rearrange("p (w n) -> p w n", w=2)
        for w, tag in enumerate(("cmpk", "cmpv")):
            s0, s1 = take((tag, 0)), take((tag, 1))
            b = 4 + w
            for lp in range(16):
                s = (s0, s1)[lp // 8]
                m = mm(ps[0:45, b, 0:256], blk[:, w, lp].rearrange("p h n -> p (h n)"), s.ap.rearrange("p (l n) -> p l n", l=8)[:, lp % 8, :],
                       lp == 0, lp == 15, [s.t, btk, bank[b] if lp == 0 else ()])
                if lp % 8 == 7:
                    done(s, m)
            x = act(hidt[0:45, w, :], ps[0:45, b, 0:256], ACT.Gelu_apprx_tanh, [m], chain=False)
            bank[b] = [x]
            hidt_tok = x
        htk = []
        for w in range(2):
            for c in range(2):
                m = mm(ps[:, 6 + w, 45 * c:45 * c + 45], hidt[0:45, w, c * 128:(c + 1) * 128], ident[0:45, 0:45], 1, 1,
                       [hidt_tok, bank[6 + w] if c == 0 else ()], tr=True)
            x = cp("dve", hid[:, w], ps[:, 6 + w, 0:90].rearrange("p (c n) -> p c n", c=2), [m], chain=False)
            bank[6 + w] = [x]
            htk.append(x)
        KCT = get(48)[0:64, 0:45]
        for c in range(2):
            m = mm(ps[0:64, 4, 0:45], C("w2k", 64 * c, 64 * c + 64), hid[:, 0, c, :], c == 0, c == 1, [htk, bank[4]])
        tkc = cp("dve", KCT, ps[0:64, 4, 0:45], [m])
        bank[4] = [tkc]
        for c in range(2):
            thd = op("dve", lambda e, c=c: e.tensor_copy(
                hd[:, c, :, :, 0:15], hid[:, 1, c, :].rearrange("p (g n) -> p g n", g=3).unsqueeze(2).broadcast_to([P, 3, 4, 15])), [htk])
        for gi in range(3):
            for c in range(2):
                m = mm(ps[:, 5, gi * 64:(gi + 1) * 64], hd[:, c, gi].rearrange("p r n -> p (r n)"), C("w2v", 64 * c, 64 * c + 64),
                       c == 0, c == 1, [thd, bank[5] if c == 0 and gi == 0 else ()])
        for gi in range(3):
            for r in range(4):
                tvb = cp("dve", VB[32 * r:32 * r + 32, gi, r, :], ps[32 * r:32 * r + 32, 5, gi * 64:(gi + 1) * 64], [m, tms], chain=False)
        bank[5] = [tvb]
        QT = get(3072)[0:64, :].rearrange("p (a h t) -> p a h t", a=2, h=12)
        KT = get(2 * 3 * 2 * 128)[0:64, :].rearrange("p (a h t) -> p a h t", a=2, h=6)
        tq = headT(Z, 512, 12, QT, trq, [0, 1])
        tk = headT(Z, 1280, 6, KT, trq, [2, 3])
        gts = get(72).rearrange("p (a n) -> p a n", a=2)
        tg = act(gts, Z[:, :, 2432:2468], ACT.Sigmoid, [zt_all])
        gv = gts.rearrange("p a (h r) -> p a h r", r=3)
        for a in range(2):
            for gi in range(4):
                m = mm(ps[:, 6 + a, gi * 64:(gi + 1) * 64], sw[:, gi, :], v[:, a, gi * 64:(gi + 1) * 64], True, True,
                       [tvn, tsw, bank[6 + a] if gi == 0 else ()])
            for gi in range(4):
                x = stt(O[:, a, gi * 64:(gi + 1) * 64], ps[:, 6 + a, gi * 64:(gi + 1) * 64], C("sgu_b", gi, gi + 1),
                        uv[:, a, gi * 64:(gi + 1) * 64], ALU.add, ALU.mult, [m], chain=False)
            bank[6 + a] = [x]
        Ob = O[:, :, 256:1024].rearrange("p a (h d) -> p a h d", h=12)
        cst = small[:, 128:200].rearrange("p (k a h) -> p k a h", k=3, a=2)
        for a in range(2):
            for h in range(12):
                m = mm(ps[:, 4 + a, h * 15:(h + 1) * 15], QN[:, a, h, :], KCT[:, (h // 4) * 15:(h // 4) * 15 + 15], True, True,
                       [tqn, tkc, bank[4 + a] if h == 0 else ()])
            pv = pc[:, a, :, 0:15]
            ma = KC("cmadd", 15 * a, 15 * a + 15).unsqueeze(1).broadcast_to([P, 12, 15])
            m01 = KC("cm01", 15 * a, 15 * a + 15).unsqueeze(1).broadcast_to([P, 12, 15])
            x = stt(pv, ps[:, 4 + a, 0:180].rearrange("p (h n) -> p h n", h=12), 0.125, ma, ALU.mult, ALU.add, [m, tms])
            bank[4 + a] = [x]
            op("dve", lambda e, a=a, pv=pv: e.tensor_reduce(cst[:, 0, a, :], pv, AX.X, ALU.max))
            x = tt("dve", pv, pv, cst[:, 0, a, :].unsqueeze(2).broadcast_to([P, 12, 15]), ALU.subtract)
            x = act(pv, pv, ACT.Exp, [x])
            op("dve", lambda e, a=a, pv=pv: e.tensor_reduce(cst[:, 1, a, :], pv, AX.X, ALU.add), [x])
            op("dve", lambda e, a=a: e.reciprocal(cst[:, 1, a, :], cst[:, 1, a, :]))
            tt("dve", cst[:, 1, a, :], cst[:, 1, a, :], gv[:, a, :, 0], ALU.mult, [tg])
            tpc = tt("dve", pv, pv, m01, ALU.mult)
        pct = get(2 * 3 * 128).rearrange("p (a g t) -> p a g t", a=2, g=3)
        for a in range(2):
            for gi in range(3):
                m = mm(ps[:, 6 + a, gi * 128:(gi + 1) * 128], pc[:, a, 4 * gi:4 * gi + 4, :].rearrange("p h n -> p (h n)"), ident, 1, 1,
                       [tpc, bank[6 + a] if gi == 0 else ()], tr=True)
            x = cp("act", pct[:, a], ps[:, 6 + a, 0:384].rearrange("p (g t) -> p g t", g=3), [m])
            bank[6 + a] = [x]
            for gi in range(3):
                b = 4 + gi // 2
                m = mm(ps[:, b, (gi % 2) * 256:(gi % 2) * 256 + 256], pct[:, a, gi, :], VB[:, gi].rearrange("p r d -> p (r d)"), True, True,
                       [x, tvb, bank[4], bank[5]])
            ov = ps[:, 4:6, :].rearrange("p b (h d) -> p (b h) d", d=64)[:, 0:12, :]
            x = tt("dve", Ob[:, a], ov, cst[:, 1, a, :].unsqueeze(2).broadcast_to([P, 12, 64]), ALU.mult, [m])
            bank[4] = bank[5] = [x]
        tcmp = x
        SB = SQ[:, :, :].rearrange("p (a b) t -> p a (b t)", a=2)
        PT = get(2048).rearrange("p (a n) -> p a n", a=2)
        stats = small[:, 200:344].rearrange("p (i n) -> p i n", n=12)
        otmp = get(256).rearrange("p (h d) -> p h d", h=4)
        items = []
        for br in range(2):
            for th in range(2):
                for gi in range(3):
                    items.append((br, th, [4 * gi + r for r in range(4)],
                                  lambda h: QT[:, :, h, :],
                                  lambda h, br=br: KT[:, :, 3 * br + h // 4, :],
                                  lambda h, kb, br=br: Z[:, kb, 2048 + 192 * br + 64 * (h // 4):2048 + 192 * br + 64 * (h // 4) + 64],
                                  [tq, tk, zt_all]))

        def fin_even(i, item, o, r, after):
            br, th, heads = item[0], item[1], item[2]
            tt("dve", r, r, gv[:, th, heads[0]:heads[0] + 4, 1 + br], ALU.mult, after)
            y = tt("dve", otmp, o, r.unsqueeze(2).broadcast_to([P, 4, 64]), ALU.mult)
            z = Ob[:, th, heads[0]:heads[0] + 4, :]
            fin_last[0] = tt("dve", z, z, otmp, ALU.add)
            return y

        fin_last = [None]
        attention(items, SB, PT, stats, lambda br, th: (KC("madd%d" % th), t_k), fin_even)
        guard[0] = [fin_last[0], g.last["pe"], g.last["act"], g.last["dve"]]
        xt = proj_out("evout", O, [fin_last[0]], {"f2_0d"})
        enable({"f1_1d", "odin"})
        xt = ffn("f2_0", C("n2_0"), xt)

        xt = ffn("f1_1", C("n1_1"), xt, softplus)
        ht = norm(C("nm_1"), xt)
        get = carve((4096, RB))
        Z = get(2 * 2340).rearrange("p (a n) -> p a n", a=2)
        get = carve((0, 2048), (RB, NAR), (2048, 4096))
        O = get(2 * 1024).rearrange("p (a n) -> p a n", a=2)
        zt = proj_tok("odin", 2340, Z, ht)
        tmp = get(2 * 800)
        r1 = rope(Z, 2176, 5, 32, 4, tmp, zt)
        tmp2 = tmp
        r2 = rope(Z, 0, 25, 64, 8, tmp2, zt)
        IT = get(2 * 5 * 128)[0:32, :].rearrange("p (a h t) -> p a h t", a=2, h=5)
        ti = headT(Z, 2176, 5, IT, r1, [0, 1], hd=32)
        QT = get(2 * 17 * 128)[0:64, :].rearrange("p (a h t) -> p a h t", a=2, h=17)
        tq = headT(Z, 0, 17, QT, r2, [2, 3])
        KT = get(2 * 8 * 128)[0:64, :].rearrange("p (a h t) -> p a h t", a=2, h=8)
        tk = headT(Z, 1088, 8, KT, r2, [4, 5])
        wi = small[:, 104:112].rearrange("p (a h) -> p a h", a=2)
        twi = ts("dve", wi, Z[:, :, 2336:2340], 0.5, None, ALU.mult)
        MS = get(384)
        wk = get(384)
        rl = get(1024)
        m8 = small[:, 112:120]
        mtok, todo = [], []
        for th in range(2):
            nk = 128 * (th + 1)
            for h in range(4):
                b = 6 + h // 2
                for kb in range(th + 1):
                    m = mm(ps[:, b, (h % 2) * nk + kb * 128:(h % 2) * nk + kb * 128 + 128], IT[:, th, h, :], IT[:, kb, 4, :], True, True,
                           [ti, bank[6], bank[7]])
            rv = rl[:, 0:4 * nk].rearrange("p (b n) -> p b n", b=2)
            x = ts("dve", rv, ps[:, 6:8, 0:2 * nk], float(32 ** -0.5), 0.0, ALU.mult, ALU.max, after=[m])
            bank[6] = bank[7] = [x]
            rh = rl[:, 0:4 * nk].rearrange("p (h n) -> p h n", h=4)
            ms = MS[:, 0:128] if th == 0 else MS[:, 128:384]
            w_ = wk[:, 0:128] if th == 0 else wk[:, 128:384]
            ts("dve", w_, rh[:, 0, :], wi[:, th, 0:1], None, ALU.mult)
            for h in range(1, 4):
                stt(w_, rh[:, h, :], wi[:, th, h:h + 1], w_, ALU.mult, ALU.add)
            tt("dve", w_, w_, KC("madd%d" % th), ALU.add)
            todo.append((th, w_, ms))

        def topk():
            for th, w_, ms in todo:
                for r in range(8):
                    op("dve", lambda e, w_=w_: e.max(m8, w_))
                    op("dve", lambda e, w_=w_: e.match_replace(w_, m8, w_, -3e38))
                    if r % 2:
                        yield
                ts("dve", ms, w_, -2e38, NEG, ALU.is_gt, ALU.mult)
                mtok.append(tt("dve", ms, ms, KC("madd%d" % th), ALU.add))
                if th == 1:
                    yield

        SB = SQ[:, :, :].rearrange("p (a b) t -> p a (b t)", a=2)
        PT = get(2048).rearrange("p (a n) -> p a n", a=2)
        items = []
        for br in (1, 0):
            for th in range(2):
                for gi in range(2):
                    heads = [4 * gi + r for r in range(4)]
                    if br == 0:
                        items.append((0, th, heads, lambda h: QT[:, :, h, :], lambda h: QT[:, :, 8, :],
                                      lambda h, kb: Z[:, kb, 1600:1664], [tq, zt]))
                    else:
                        items.append((1, th, heads, lambda h: QT[:, :, 9 + h, :], lambda h: KT[:, :, h, :],
                                      lambda h, kb: Z[:, kb, 1664 + 64 * h:1728 + 64 * h], [tq, tk, zt]))
        Oh = O.rearrange("p a (h d) -> p a h d", d=64)

        def fin_odd(i, item, o, r, after):
            br, th, heads = item[0], item[1], item[2]
            h0 = heads[0] + 8 * br
            fin_last[0] = tt("dve", Oh[:, th, h0:h0 + 4, :], o, r.unsqueeze(2).broadcast_to([P, 4, 64]), ALU.mult, after)
            return fin_last[0]

        attention(items, SB, PT, stats,
                  lambda br, th: (KC("madd%d" % th), t_k) if br else ((MS[:, 0:128] if th == 0 else MS[:, 128:384]), mtok[th]), fin_odd, topk())
        guard[0] = [fin_last[0], g.last["pe"], g.last["act"], g.last["dve"]]
        xt = proj_out("odout", O, [fin_last[0]], {"f2_1d"})
        xt = ffn("f2_1", C("n2_1"), xt)

        xt = norm(C("nf"), xt, out=XT, split=False)
        gm = small[:, 416:440]
        for n, (gn, o) in enumerate((("g_mix", 8), ("g_ffn", 32), ("g_final", 56))):
            tgm = stt(gm[:, 8 * n:8 * n + 8], MOD[:, o:o + 8], 1.0, C(gn), ALU.add, ALU.mult, [t_mod[0]])
        ht = norm(gm[:, 0:8], xt, shift=MOD[:, 0:8], gaintok=[tgm, t_mod[0]], mid=True)
        enable({"win2"})
        get = carve((4096, RB + 4096))
        RKV = get(12 * T).rearrange("p (c t) -> p c t", c=12)
        XG = get(8 * T + 12)
        XB = XG[:, 0:4 * (T + 3)].rearrange("p (c t) -> p c t", c=4)
        GB = XG[:, 4 * (T + 3):8 * T + 12].rearrange("p (c t) -> p c t", c=4)
        SG = get(16 * T).rearrange("p (c t) -> p c t", c=16)
        tz = op("pool", lambda e: e.memset(XB[:, :, 0:3], 0.0), [xt])
        pj = []
        for gi in range(18):
            s = wtake(("win2", gi))
            b = gi % 4
            for j in range(2):
                for k in range(8):
                    m = mm3(ps[:, b, j * T:(j + 1) * T], s.view(lambda w: w[:, k * 256 + j * 128:k * 256 + j * 128 + 128]), HP[k], k == 0, k == 7,
                            [s.t, ht[k], bank[b] if k == 0 and j == 0 else ()])
            wdone(s, m)
            c = 2 * gi
            pv = ps[:, b, :].rearrange("p (c t) -> p c t", c=2)
            if c < 12:
                x = cp("dve", RKV[:, c:c + 2, :], pv, [m], chain=False)
            elif c < 16:
                x = cp("dve", XB[:, c - 12:c - 10, 3:T + 3], pv, [m], chain=False)
            elif c < 20:
                x = act(GB[:, c - 16:c - 14, :], pv, ACT.Gelu_apprx_tanh, [m], chain=False)
            else:
                x = act(SG[:, c - 20:c - 18, :], pv, ACT.Sigmoid, [m, txc, sgfree], chain=False)
            bank[b] = [x]
            pj.append(x)
            if gi in (6, 7, 8):
                q = gi - 6
                X = RKV[:, 4 * q:4 * q + 4, :]
                y = tt("dve", SG[:, 12:16, 1:T], X[:, :, 0:T - 1], X[:, :, 1:T], ALU.subtract, [pj])
                ts("dve", SG[:, 12:16, 0:1], X[:, :, 0:1], -1.0, None, ALU.mult, chain=False)
                y = g.last["dve"]
                for c in range(4):
                    trkv = stt(X[:, c, :], SG[:, 12 + c, :], C("mu_rkv", 4 * q + c, 4 * q + c + 1), X[:, c, :], ALU.mult, ALU.add, [y], chain=False)
                sgfree = trkv
            if gi in (8, 9):
                for c in (2 * gi - 16, 2 * gi - 15):
                    y = ts("dve", SG[:, 8 + c, :], XB[:, c, 0:T], C("conv_w", 4 * c, 4 * c + 1), C("conv_b", c, c + 1), ALU.mult, ALU.add, after=[pj, tz])
                    for j in range(1, 3):
                        y = stt(SG[:, 8 + c, :], XB[:, c, j:T + j], C("conv_w", 4 * c + j, 4 * c + j + 1), SG[:, 8 + c, :], ALU.mult, ALU.add)
                    txc = stt(XB[:, c, 3:T + 3], XB[:, c, 3:T + 3], C("conv_w", 4 * c + 3, 4 * c + 4), SG[:, 8 + c, :], ALU.mult, ALU.add)
        get = carve((0, 4096), (4096 + 36 * T + 12, NAR))
        MG = get(2048).rearrange("p (c t) -> p c t", c=8)
        XX = get(2048).rearrange("p (i t) -> p i t", i=16)
        DX = AR[:, NAR - 2048:NAR].rearrange("p (c t) -> p c t", c=8)
        xm = get(8 * T).rearrange("p (c t) -> p c t", c=8)
        guard[0] = [pj]
        GR, GI = MG[:, 0:4, :], MG[:, 4:8, :]
        XC = XB[:, :, 3:T + 3]
        tgr = {}
        for n, (wn, bn, dst) in enumerate((("wr", "b_r", GR), ("wi", "b_i", GI))):
            for c in range(4):
                b = 2 * n + c // 2
                m = mm(ps[:, b, (c % 2) * T:(c % 2) * T + T], C(wn, 128 * c, 128 * c + 128), XC[:, c, :], True, True,
                       [txc, bank[b] if c % 2 == 0 else ()])
            for c in range(4):
                b = 2 * n + c // 2
                tgr[n] = act(dst[:, c, :], ps[:, b, (c % 2) * T:(c % 2) * T + T], ACT.Sigmoid, [m, pj, ht], bias=C(bn, c, c + 1), chain=False)
                bank[b] = [tgr[n]]
        tt("dve", DX[:, :, 1:T], SQ[:, :, 0:T - 1], SQ[:, :, 1:T], ALU.subtract, [ht, pj])
        ts("dve", DX[:, :, 0:1], SQ[:, :, 0:1], -1.0, None, ALU.mult, chain=False)
        tdx = g.last["dve"]
        LW = get(4 * T).rearrange("p (c t) -> p c t", c=4)
        AI = get(4 * T).rearrange("p (c t) -> p c t", c=4)
        GG_ = get(4 * T).rearrange("p (c t) -> p c t", c=4)
        lr = get(T)
        A_ = get(4 * T).rearrange("p (c t) -> p c t", c=4)
        GXf = get(8 * T)
        B_ = GXf[:, 0:4 * T].rearrange("p (c t) -> p c t", c=4)
        outs, lfree = {}, {}

        def lora(n, w1n, w2n, r, dst, mix):
            tk_ = []
            for k in range(8):
                tk_.append(stt(mix[:, k, :], DX[:, k, :], C("mu_wag", 8 * n + k, 8 * n + k + 1), SQ[:, k, :], ALU.mult, ALU.add,
                               [lfree.get(n - 2), tdx, pj], chain=False))
            for k in range(8):
                m = mm(ps[0:r, 4, 0:T], C(w1n, r * k, r * k + r), mix[:, k, :], k == 0, k == 7, [tk_[k], bank[4] if k == 0 else ()])
            lfree[n] = m
            f = {0: ACT.Tanh, 1: ACT.Copy, 2: ACT.Sigmoid}[n]
            x = act(lr[0:r, :], ps[0:r, 4, 0:T], f, [m, outs.get("m")], chain=False)
            bank[4] = [x]
            for c in range(4):
                b = 5 + c // 2
                m = mm(ps[:, b, (c % 2) * T:(c % 2) * T + T], C(w2n, 128 * c, 128 * c + 128)[0:r, :], lr[0:r, :], True, True,
                       [x, bank[b] if c % 2 == 0 else ()])
            outs["m"] = m
            for c in range(4):
                b = 5 + c // 2
                src = ps[:, b, (c % 2) * T:(c % 2) * T + T]
                if n < 2:
                    x = act(dst[:, c, :], src, ACT.Sigmoid, [m], bias=C(("w0", "a0")[n], c, c + 1), chain=False)
                else:
                    x = cp("act", dst[:, c, :], src, [m], chain=False)
                bank[b] = [x]
            outs[n] = x

        lora(0, "lw1", "lw2", 64, LW, xm)
        for c in range(4):
            x = ts("dve", GR[:, c, :], GR[:, c, :], sp[:, 6, c:c + 1], None, ALU.mult, after=[tgr[0], tsp[0]], chain=False)
        xt_ = act(GR, GR, ACT.Tanh, [x], chain=False)
        lora(1, "la1", "la2", 64, AI, XX.rearrange("p i t -> p (i t)").rearrange("p (k t) -> p k t", k=8))
        ts("dve", B_, GR, -1.0, 1.0, ALU.mult, ALU.add, after=[xt_])
        op("dve", lambda e: e.reciprocal(B_, B_))
        y = stt(A_, GR, 1.0, B_, ALU.add, ALU.mult)
        y = stt(GR, GR, -2.0, B_, ALU.mult, ALU.mult)
        lora(2, "lg1", "lg2", 128, GG_, xm)
        tA = act(A_, A_, ACT.Sqrt, [y], chain=False)
        tR = act(GR, GR, ACT.Sqrt, [y], chain=False)
        d4 = SQ[:, 4:8, :]
        Rr, Kr, Vr = RKV[:, 0:4, :], RKV[:, 4:8, :], RKV[:, 8:12, :]
        KKn = AR[:, 2048:3072].rearrange("p (c t) -> p c t", c=4)
        for c in range(4):
            x = ts("dve", KKn[:, c, :], Kr[:, c, :], C("k_k", c, c + 1), None, ALU.mult, after=[trkv, lfree[1]], chain=False)
        x = tt("dve", d4, KKn, KKn, ALU.mult)
        for c in range(4):
            m = mm(ps[:, 4 + c // 2, (c % 2) * T:(c % 2) * T + T], KC("bones"), d4[:, c, :], True, True, [x, bank[4 + c // 2] if c % 2 == 0 else ()])
        tkk = m
        tt("dve", GI, GI, XC, ALU.mult, [tgr[1]])
        tt("dve", GR, GR, GI, ALU.mult, [tR])
        for c in range(4):
            op("dve", lambda e, c=c: e.tensor_tensor_scan(XC[:, c, :], A_[:, c, :], GR[:, c, :], 0.0, ALU.mult, ALU.add), [tA])
        YB = GB
        tyb = tt("dve", YB, XC, GB, ALU.mult)

        def proj_p(tag, Y, ytok, b0):
            r = []
            for gi in range(2):
                s = take((tag, gi))
                w = s.ap.rearrange("p (k n) -> p k n", k=4)
                for j in range(4):
                    b = b0 + 2 * gi + j // 2
                    for k in range(4):
                        m = mm(ps[:, b, (j % 2) * T:(j % 2) * T + T], w[:, k, j * 128:(j + 1) * 128], Y[:, k, :], k == 0, k == 3,
                               [s.t, ytok, bank[b] if k == 0 and j % 2 == 0 else ()])
                    if j % 2 == 1:
                        r.append((4 * gi + j - 1, b, m))
                done(s, m)
            return r

        pbs = proj_p("pb", YB, tyb, 0)

        pv = ps[:, 4:6, :].rearrange("p b (c t) -> p (b c) t", c=2)
        x = ts("dve", d4, pv, 1e-12, None, ALU.add, after=[tkk])
        bank[4] = bank[5] = [x]
        xs = act(d4, d4, ACT.Sqrt, [x], chain=False)
        kf = GXf[:, 4 * T:8 * T].rearrange("p (c t) -> p c t", c=4)
        for c in range(4):
            y = ts("dve", kf[:, c, :], AI[:, c, :], 1.0, C("k_a", c, c + 1), ALU.subtract, ALU.mult, after=[outs[1]], chain=False)
        stt(Kr, kf, 1.0, Kr, ALU.add, ALU.mult)
        for c in range(4):
            x = stt(kf[:, c, :], Rr[:, c, :], C("r_k", c, c + 1), Kr[:, c, :], ALU.mult, ALU.mult)
        for c in range(4):
            mbn = mm(ps[:, 4 + c // 2, (c % 2) * T:(c % 2) * T + T], KC("bones"), kf[:, c, :], True, True, [x, bank[4 + c // 2] if c % 2 == 0 else ()])
        op("dve", lambda e: e.reciprocal(d4, d4), [xs])
        tt("dve", KKn, KKn, d4, ALU.mult)
        BN = A_
        ts("dve", LW, LW, -float(np.exp(-0.5)), None, ALU.mult, after=[outs[0]])
        CU = SQ[:, 0:4, :]
        for c in range(4):
            op("dve", lambda e, c=c: e.tensor_tensor_scan(CU[:, c, :], KC("seg"), LW[:, c, :], 0.0, ALU.mult, ALU.add))
        x = tt("dve", LW, CU, LW, ALU.subtract)
        PP = xm[:, 4:8, :]
        te = act(LW, LW, ACT.Exp, [x])
        te = act(PP, CU, ACT.Exp)
        te = act(CU, CU, ACT.Exp, scale=-1.0)
        x = tt("dve", BN, pv, Vr, ALU.mult, [mbn])
        bank[4] = bank[5] = [x]
        GXt = GXf.rearrange("p (c j w t) -> p c j w t", c=4, j=2, w=2)
        KKj = KKn.rearrange("p c (j t) -> p c j t", j=2)
        for c in range(4):
            stt(GXt[:, c, :, 0, :], KKj[:, c], -1.0, LW[:, c, :].rearrange("p (j t) -> p j t", j=2), ALU.mult, ALU.mult, [te])
            tt("dve", GXt[:, c, :, 1, :], Rr[:, c, :].rearrange("p (j t) -> p j t", j=2), PP[:, c, :].rearrange("p (j t) -> p j t", j=2), ALU.mult)
        BT = AI
        tt("dve", BT, KKn, AI, ALU.mult, [outs[1]])
        tt("dve", BT, BT, CU, ALU.mult)
        KTt = Kr
        tk_ = tt("dve", KTt, Kr, CU, ALU.mult)
        PPe = small[:, 472:488].rearrange("p (q c) -> p q c", q=4)
        for q in range(4):
            tpe = cp("dve", PPe[:, q, :], PP[:, :, 64 * q + 63])
        TM = {}
        tmt = {}
        spaces = [LW, xm[:, 0:4, :], xm[:, 4:8, :], SQ[:, 0:4, :]]
        srcs = {"b": lambda c, j: BT[:, c, 128 * j:128 * j + 128], "k": lambda c, j: KTt[:, c, 128 * j:128 * j + 128],
                "a": lambda c, j: GXt[:, c, j, 0, :], "v": lambda c, j: Vr[:, c, 128 * j:128 * j + 128]}
        for n, nm in enumerate(("b", "k", "a", "v")):
            dst = spaces[n].rearrange("p c t -> p (c t)").rearrange("p (j c t) -> p j c t", j=2, c=4)
            TM[nm] = dst
            tmt[nm] = []
            for j in range(2):
                b = 4 + (2 * n + j) % 4
                for c in range(4):
                    m = mm(ps[:, b, c * 128:(c + 1) * 128], srcs[nm](c, j), ident, 1, 1, [tpe, tk_, bank[b] if c == 0 else ()], tr=True)
                x = cp("act" if j else "dve", dst[:, j], ps[:, b, :].rearrange("p (c t) -> p c t", c=4), [m], chain=False)
                bank[b] = [x]
                tmt[nm].append(x)
        for c, b, m in pbs:
            x = tt("dve", MG[:, c:c + 2, :], SG[:, 8 + c:10 + c, :], ps[:, b, :].rearrange("p (c t) -> p c t", c=2), ALU.mult, [m], chain=False)
            bank[b] = [x]
        SA = d4.rearrange("p c t -> p (c t)").rearrange("p (j h v) -> p j h v", j=2, h=8)
        UT = Rr.rearrange("p c t -> p (c t)").rearrange("p (q c v) -> p q c v", q=4, c=4)
        GM = get(16 * 512).rearrange("p (i n) -> p i n", i=16)
        tG = {}
        for h in range(8):
            r0, c = 64 * (h % 2), h // 2
            for j in range(2):
                i = 2 * h + j
                b = (i // 2) % 2 * 2 + (h % 2) + 4 * (j)
                rr = GXt[r0:r0 + 64, c, j].rearrange("p w t -> p (w t)")
                mm(ps[:, b, 0:256], BT[r0:r0 + 64, c, 128 * j:128 * j + 128], rr, True, True, [tk_, tmt["v"], bank[b]])
                m = mm(ps[:, b, 256:512], KTt[r0:r0 + 64, c, 128 * j:128 * j + 128], rr, True, True)
                x = tt("dve", GM[:, i, :], ps[:, b, :], KC("gmask"), ALU.mult, [m], chain=False)
                bank[b] = [x]
                tG[i] = x
        gall = list(tG.values())
        TN = XG[:, 0:2048].rearrange("p (i t) -> p i t", i=16)
        TTt = RKV[:, 4:12, :].rearrange("p c t -> p (c t)").rearrange("p (i t) -> p i t", i=16)
        x1 = cp("act", TN, ident.unsqueeze(1).broadcast_to([P, 16, 128]), [gall, tyb, pbs[-1][2]])
        x2 = op("dve", lambda e: e.tensor_copy(TTt, ident.unsqueeze(1).broadcast_to([P, 16, 128])), gall)
        l0 = KC("lv0").bitcast(U32)
        t0m = KC("lt0").bitcast(U32)
        tT = {}
        for q in range(4):
            b = q
            for w in range(4):
                i = 4 * q + w
                m = mm(ps[:, b, w * 128:(w + 1) * 128], GM[:, i, 0:128], ident, True, True, [x2, bank[b] if w == 0 else ()])
            op("dve", lambda e, q=q: e.copy_predicated(TTt[:, 4 * q:4 * q + 4, :], t0m.unsqueeze(1).broadcast_to([P, 4, 128]),
                                                       GM[:, 4 * q:4 * q + 4, 0:128]))
            x = op("dve", lambda e, q=q, b=b: e.copy_predicated(
                TN[:, 4 * q:4 * q + 4, :], l0.unsqueeze(1).broadcast_to([P, 4, 128]), ps[:, b, :].rearrange("p (w t) -> p w t", w=4)), [m, x1])
            bank[b] = [x]
            tT[q] = x
        for n in range(1, 6):
            lv = KC(f"lv{n}").bitcast(U32).unsqueeze(1).broadcast_to([P, 4, 128])
            lt = KC(f"lt{n}").bitcast(U32).unsqueeze(1).broadcast_to([P, 4, 128])
            tx = {}
            for q in range(4):
                b = q
                for w in range(4):
                    i = 4 * q + w
                    m = mm(ps[:, b, w * 128:(w + 1) * 128], GM[:, i, 0:128], TN[:, i, :], True, True, [tT[q], bank[b] if w == 0 else ()])
                tx[q] = cp("act", XX[:, 4 * q:4 * q + 4, :], ps[:, b, :].rearrange("p (w t) -> p w t", w=4), [m])
                bank[b] = [tx[q]]
            for q in range(4):
                b1, b2 = 4 + (2 * q) % 4, 4 + (2 * q + 1) % 4
                for w in range(4):
                    i = 4 * q + w
                    m2 = mm(ps[:, b2, w * 128:(w + 1) * 128], XX[:, i, :], TTt[:, i, :], True, True, [tx[q], bank[b2] if w == 0 else ()])
                m1 = None
                if n < 5:
                    for w in range(4):
                        i = 4 * q + w
                        m1 = mm(ps[:, b1, w * 128:(w + 1) * 128], TTt[:, i, :], XX[:, i, :], True, True, [tx[q], bank[b1] if w == 0 else ()])
                x = op("dve", lambda e, q=q, b2=b2, lt=lt: e.copy_predicated(
                    TTt[:, 4 * q:4 * q + 4, :], lt, ps[:, b2, :].rearrange("p (w t) -> p w t", w=4)), [m2, m1])
                bank[b2] = [x]
                if n < 5:
                    x = op("dve", lambda e, q=q, b1=b1, lv=lv: e.copy_predicated(
                        TN[:, 4 * q:4 * q + 4, :], lv, ps[:, b1, :].rearrange("p (w t) -> p w t", w=4)), [m1])
                    bank[b1] = [x]
                tT[q] = x
        AV = TN[:, 0:8, :].rearrange("p n t -> p (n t)").rearrange("p (i v) -> p i v", i=16)
        for i in range(16):
            h, j = divmod(i, 2)
            b = i // 8
            m = mm(ps[:, b, (i % 8) * 64:(i % 8) * 64 + 64], GM[:, i, 256:384], TM["v"][:, j, h // 2, 64 * (h % 2):64 * (h % 2) + 64], True, True,
                   [tT[3], tmt["v"], bank[b] if i % 8 == 0 else ()])
        for b in range(2):
            tav = cp("dve", AV[:, 8 * b:8 * b + 8, :], ps[:, b, :].rearrange("p (i v) -> p i v", i=8), [m])
            bank[b] = [tav]
        WT = XX[:, 0:8, :].rearrange("p (c j) t -> p c j t", c=4)
        for i in range(16):
            h, j = divmod(i, 2)
            r0, c = 64 * (h % 2), h // 2
            b = 2 + c // 2
            o = ((c % 2) * 2 + j) * 128
            m = mm(ps[r0:r0 + 64, b, o:o + 128], TM["a"][:, j, c, r0:r0 + 64], TTt[:, i, :], True, True,
                   [tT[0], tT[1], tT[2], tT[3], tmt["a"], bank[b] if i % 8 == 0 else ()], skip=True)
        for b in range(2):
            twt = cp("dve", WT[:, 2 * b:2 * b + 2], ps[:, 2 + b, :].rearrange("p (c j t) -> p c j t", c=2, j=2), [m])
            bank[2 + b] = [twt]
        tu = None
        tsa = {}
        for q in range(4):
            j, b0 = q // 2, 64 * (q % 2)
            for h in range(8):
                r0, c = 64 * (h % 2), h // 2
                bb = 4 + h % 2
                o = c * 64
                if q:
                    mm(ps[b0:b0 + 64, bb, o:o + 64], WT[r0:r0 + 64, c, j, b0:b0 + 64], UT[r0:r0 + 64, q, c, :], True, False,
                       [tu, twt, bank[bb]], skip=True)
                m = mm(ps[b0:b0 + 64, bb, o:o + 64], TTt[:, 2 * h + j, b0:b0 + 64], AV[:, 2 * h + j, :], q == 0, True,
                       [tav, twt, bank[bb]], skip=True)
            for pr in range(2):
                x = cp("dve", SA[b0:b0 + 64, j, :, :].rearrange("p (c r) v -> p c r v", r=2)[:, :, pr, :],
                       ps[b0:b0 + 64, 4 + pr, 0:256].rearrange("p (c v) -> p c v", c=4), [m])
                bank[4 + pr] = [x]
            tsa[q] = x
            if q < 3:
                for h in range(8):
                    r0, c = 64 * (h % 2), h // 2
                    o = c * 64
                    mm(ps[r0:r0 + 64, 6, o:o + 64], TM["k"][b0:b0 + 64, j, c, r0:r0 + 64], TM["v"][b0:b0 + 64, j, c, r0:r0 + 64], True, False,
                       [tmt["v"], tmt["k"], tmt["b"], bank[6]], skip=True)
                    m = mm(ps[r0:r0 + 64, 6, o:o + 64], TM["b"][b0:b0 + 64, j, c, r0:r0 + 64], SA[b0:b0 + 64, j, h, :], False, True, [x], skip=True)
                src = ps[:, 6, 0:256].rearrange("p (c v) -> p c v", c=4)
                un = UT[:, q + 1]
                if q:
                    x = tt("dve", un, src, UT[:, q], ALU.add, [m])
                    bank[6] = [x]
                    tu = tt("dve", un, un, PPe[:, q, :].unsqueeze(2).broadcast_to([P, 4, 64]), ALU.mult)
                else:
                    tu = tt("dve", un, src, PPe[:, q, :].unsqueeze(2).broadcast_to([P, 4, 64]), ALU.mult, [m])
                    bank[6] = [tu]
        for h in range(8):
            r0, c = 64 * (h % 2), h // 2
            b = 2 * (h % 2) + c // 2
            for j in range(2):
                o = (c % 2) * T + j * 128
                out = ps[r0:r0 + 64, b, o:o + 128]
                i = 2 * h + j
                mm(out, TM["v"][:, j, c, r0:r0 + 64], GM[:, i, 384:512], True, False, [tsa[3], tu, bank[b]], skip=True)
                m = mm(out, SA[:, j, h, :], GM[:, i, 128:256], False, j == 0 and False, [], skip=True)
                for qq in (2 * j, 2 * j + 1):
                    if qq == 0:
                        continue
                    m = mm(ps[r0:r0 + 64, b, o + 64 * (qq % 2):o + 64 * (qq % 2) + 64], UT[r0:r0 + 64, qq, c, :],
                           GXt[r0:r0 + 64, c, j, 1, 64 * (qq % 2):64 * (qq % 2) + 64], False, True, [], skip=True)
        Y = RKV[:, 0:4, :]
        for pr in range(2):
            x = cp("dve", Y[64 * pr:64 * pr + 64], ps[64 * pr:64 * pr + 64, 2 * pr:2 * pr + 2, :].rearrange("p b (c t) -> p (b c) t", c=2), [m])
            bank[2 * pr] = bank[2 * pr + 1] = [x]
        Y2 = RKV[:, 4:8, :]

        def headsum(src, after, b0=4):
            for c in range(4):
                m = mm(ps[:, b0 + c // 2, (c % 2) * T:(c % 2) * T + T], KC("bones"), src[:, c, :], True, True, [after, bank[b0 + c // 2] if c % 2 == 0 else ()])
            return m

        m = headsum(Y, [x])
        for c in range(4):
            stt(BN[:, c, :], BN[:, c, :], C("lnx_b", c, c + 1), GG_[:, c, :], ALU.add, ALU.mult, [outs[2]], chain=c == 0)
        for c in range(4):
            ts("dve", GG_[:, c, :], GG_[:, c, :], C("lnx_g", c, c + 1), None, ALU.mult, chain=c == 0)
        x = stt(Y, pv, -1.0 / 64, Y, ALU.mult, ALU.add, [m])
        bank[4] = bank[5] = [x]
        x = tt("dve", Y2, Y, Y, ALU.mult)
        m = headsum(Y2, [x])
        x = ts("dve", Y2, pv, 1.0 / 64, 64e-5, ALU.mult, ALU.add, after=[m])
        bank[4] = bank[5] = [x]
        xs = act(Y2, Y2, ACT.Sqrt, [x], chain=False)
        tt("dve", Y, Y, GG_, ALU.mult)
        op("dve", lambda e: e.reciprocal(Y2, Y2), [xs])
        tt("dve", Y, Y, Y2, ALU.mult)
        tya = tt("dve", Y, Y, BN, ALU.add)
        tks = []
        for c, b, m in proj_p("pa", Y, tya, 4):
            sgv = SG[:, c:c + 2, :]
            x = tt("dve", sgv, sgv, ps[:, b, :].rearrange("p (c t) -> p c t", c=2), ALU.mult, [m])
            bank[b] = [x]
            x = tt("dve", MG[:, c:c + 2, :], MG[:, c:c + 2, :], sgv, ALU.add)
            y = cp("act", OH[:, c:c + 2, :], MG[:, c:c + 2, :], [x], chain=False)
            tks.append(tt("dve", OL[:, c:c + 2, :], MG[:, c:c + 2, :], OH[:, c:c + 2, :].bitcast(F32), ALU.subtract, [y], chain=False))
        guard[0] = [tks, g.last["pe"], g.last["act"], g.last["dve"]]
        enable({"moed"})
        xt = proj_res("wout2", tks, 0, MOD[:, 16:24])
        ht = norm(gm[:, 8:16], xt, shift=MOD[:, 24:32], gaintok=[tgm])
        get = carve((7168, RB))
        LG = get(2 * 36).rearrange("p (a n) -> p a n", a=2)
        for th in range(2):
            for k in range(8):
                m = mm(ps[:, 4 + th, 0:36], SQ[:, k, th * 128:(th + 1) * 128], C("wre", 36 * k, 36 * k + 36), k == 0, k == 7,
                       [ht[k], bank[4 + th] if k == 0 else ()])
        x = tt("dve", LG, ps[:, 4:6, 0:36], C("bre").unsqueeze(1).broadcast_to([P, 2, 36]), ALU.add, [m])
        bank[4] = bank[5] = [x]
        st8 = get(32 * 2).rearrange("p (n a) -> p n a", a=2)
        gsel = get(8).rearrange("p (a g) -> p a g", a=2)
        le = LG[:, :, 4:36].rearrange("p a (g e) -> p a g e", g=4)
        lg = LG[:, :, 0:4]
        op("dve", lambda e: e.tensor_reduce(st8[:, 0, :], lg, AX.X, ALU.max))
        b4 = st8[:, 0, :].unsqueeze(2).broadcast_to([P, 2, 4])
        tt("dve", gsel, lg, b4, ALU.subtract)
        eg = get(8).rearrange("p (a g) -> p a g", a=2)
        x = ts("dve", gsel, gsel, 0.0, None, ALU.is_ge)
        x = tt("dve", eg, lg, b4, ALU.subtract)
        x = act(eg, eg, ACT.Exp, [x])
        op("dve", lambda e: e.tensor_reduce(st8[:, 1, :], eg, AX.X, ALU.add), [x])
        op("dve", lambda e: e.reciprocal(st8[:, 1, :], st8[:, 1, :]))
        for gi in range(1, 4):
            for g2 in range(gi):
                stt(gsel[:, :, gi], gsel[:, :, g2], 0.0, gsel[:, :, gi], ALU.is_equal, ALU.mult)
        gm1 = get(8).rearrange("p (a g) -> p a g", a=2)
        ts("dve", gm1, gsel, 1.0, 1e30, ALU.subtract, ALU.mult)
        EW = get(80).rearrange("p (a n) -> p a n", a=2)
        op("dve", lambda e: e.memset(EW, -3e38))
        EL = EW[:, :, 0:32].rearrange("p a (g e) -> p a g e", g=4)
        tt("dve", EL, le, gm1.unsqueeze(3).broadcast_to([P, 2, 4, 8]), ALU.add)
        ELf = EW[:, :, 0:32]
        WKf = get(80).rearrange("p (a n) -> p a n", a=2)
        M8 = get(32).rearrange("p (a n) -> p a n", a=2)
        for a in range(2):
            op("dve", lambda e, a=a: e.max(M8[:, a, 0:8], EW[:, a, :]))
            op("dve", lambda e, a=a: e.memset(M8[:, a, 8:16], -3e38))
            op("dve", lambda e, a=a: e.tensor_copy(M8[:, a, 8:10], M8[:, a, 0:2]))
            op("dve", lambda e, a=a: e.match_replace(WKf[:, a, :], M8[:, a, 8:16], EW[:, a, :], -3e38))
        sel2 = get(64).rearrange("p (a n) -> p a n", a=2)
        ts("dve", sel2, WKf[:, :, 0:32], -2e38, None, ALU.is_lt)
        tt("dve", ELf, ELf, M8[:, :, 0:1].broadcast_to([P, 2, 32]), ALU.subtract)
        x = ts("dve", ELf, ELf, -200.0, None, ALU.max)
        x = act(ELf, ELf, ACT.Exp, [x])
        tt("dve", ELf, ELf, sel2, ALU.mult, [x])
        op("dve", lambda e: e.tensor_reduce(st8[:, 2, :], ELf, AX.X, ALU.add))
        op("dve", lambda e: e.reciprocal(st8[:, 2, :], st8[:, 2, :]))
        tt("dve", st8[:, 2, :], st8[:, 2, :], st8[:, 1, :], ALU.mult)
        twt2 = tt("dve", ELf, ELf, st8[:, 2, :].unsqueeze(2).broadcast_to([P, 2, 32]), ALU.mult)
        CW = get(T)
        tcw = []

        def scale_unit(u):
            b = 6 + u % 2
            if u == 0:
                for a in range(2):
                    m = mm(ps[0:32, 6, a * 128:(a + 1) * 128], ELf[:, a, :], ident, 1, 1, [twt2, bank[6] if a == 0 else ()], tr=True)
                tcw.append(cp("dve", CW[0:32, :], ps[0:32, 6, 0:T], [m]))
                bank[6] = list(tcw)
            m = mm(ps[:, b, 0:T], ident[0:32, u:u + 1].broadcast_to([32, 128]), CW[0:32, :], True, True,
                   [tcw, bank[b]])
            return ps[:, b, 0:T], m

        m = units("moe", 32, ht, scale_unit)
        r = []
        for c in range(8):
            x = stt(XT[:, c, :], ps[:, c // 2, (c % 2) * T:(c % 2) * T + T], MOD[:, 40 + c:41 + c], XT[:, c, :], ALU.mult, ALU.add, [m[c // 2]], chain=False)
            r.append(x)
            bank[c // 2] = [x]
        ht = norm(gm[:, 16:24], r, shift=MOD[:, 48:56], gaintok=[tgm], split=False)
        for n in range(4):
            to = g.dma("sp", lambda e, n=n: e.dma_start(OUT[:, 2 * n:2 * n + 2, :], SQ[:, 2 * n:2 * n + 2, :]), osem, 16 * (n + 1), [ht[2 * n + 1]])
        op("sp", lambda e: e.wait_ge(osem, 64) and None, [])
        assert st["take"] == len(order)
        block = ctx.enter_context(nc.Block())
        g.emit(block)


def pack_weights(i):
    def units(tag, wg, wu, wd):
        n = wd.shape[0] // 256 if wd.ndim == 2 else wd.shape[0]
        for u in range(n):
            if wd.ndim == 2:
                gg, uu, dd = wg[:, 256 * u:256 * u + 256], wu[:, 256 * u:256 * u + 256], wd[256 * u:256 * u + 256]
            else:
                gg, uu, dd = wg[u], wu[u], wd[u]
            out[(tag + "g", u)] = kcols(gg)
            out[(tag + "u", u)] = kcols(uu)
            out[(tag + "d", u)] = kcols(dd)

    def kcols(w):
        k = w.shape[0] // 128
        return w.reshape(k, 128, w.shape[1]).transpose(1, 0, 2).reshape(128, -1)

    out = {}
    for l in range(2):
        units(f"f1_{l}", i["ffn1_w_gate"][l], i["ffn1_w_up"][l], i["ffn1_w_down"][l])
        units(f"f2_{l}", i["ffn2_w_gate"][l], i["ffn2_w_up"][l], i["ffn2_w_down"][l])
    w = i["ev_w_in"][0]
    b = [0, 512, 1280, 1472, 1664, 1856, 2048, 2240, 2432, 2468]
    a_, q, kc, vc, ksl, vsl, kw, vw, gl = [w[:, b[n]:b[n + 1]] for n in range(9)]
    ev = np.concatenate([a_, q, ksl, kw, kc, vc, vsl, vw, gl], 1)
    w = i["od_w_in"][0]
    sz = [512, 64, 64, 128, 32, 4, 512, 512, 512]
    b = [0]
    for s in sz:
        b.append(b[-1] + s)
    qc, kc, vc, qi, ki, wi, qd, kd, vd = [w[:, b[n]:b[n + 1]] for n in range(9)]
    od = np.concatenate([qc, kc, qd, kd, vc, vd, qi, ki, wi], 1)
    for tag, m in (("evin", ev), ("odin", od)):
        m = np.concatenate([m, np.zeros((1024, 2560 - m.shape[1]), m.dtype)], 1)
        for gi in range(5):
            for a in range(2):
                out[(tag, gi, a)] = kcols(m[512 * a:512 * a + 512, 512 * gi:512 * gi + 512])
    for tag, n in (("cmpk", "ev_cmp_w1_k"), ("cmpv", "ev_cmp_w1_v")):
        for a in range(2):
            out[(tag, a)] = kcols(i[n][0][1024 * a:1024 * a + 1024])
    for tag, m in (("evout", i["ev_w_out"][0]), ("odout", i["od_w_out"][0]), ("win2", i["w_in_2"][0]), ("wout2", i["w_out_2"][0]),
                   ("ada", np.concatenate([i["w_ada_2"][0], i["w_ada_f_2"]], 1))):
        for gi in range(m.shape[1] // 256):
            out[(tag, gi)] = kcols(m[:, 256 * gi:256 * gi + 256])
    for tag, m in (("pa", i["p_a_2"][0]), ("pb", i["p_b_2"][0])):
        for gi in range(2):
            out[(tag, gi)] = kcols(m[:, 512 * gi:512 * gi + 512])
    units("moe", i["w1e_2"][0], i["w3e_2"][0], i["w2e_2"][0])
    order = slot_order()
    W = np.empty((len(order), P, SLOT), np.float32)
    for n, k in enumerate(order):
        W[n] = out[k]
    return W


def pack_cols(i):
    a = np.zeros((P, NCOL), np.float32)

    def put(n, v):
        o, w = COFF[n]
        a[:v.shape[0], o:o + w] = v.reshape(v.shape[0], w)

    def col(v):
        return v.reshape(-1, P).T

    for l in range(2):
        put(f"n1_{l}", col(i["ffn1_norm"][l]))
        put(f"nm_{l}", col(i["mix_norm"][l]))
        put(f"n2_{l}", col(i["ffn2_norm"][l]))
    put("nf", col(i["final_norm"]))
    put("g_mix", col(i["g_mix_2"][0]))
    put("g_ffn", col(i["g_ffn_2"][0]))
    put("g_final", col(i["g_final_2"]))
    put("c", col(i["c_2"][0]))
    put("b_ada", col(np.concatenate([i["b_ada_2"][0], i["b_ada_f_2"]])))
    put("mu_rkv", col(i["mu_rkv_2"][0]))
    put("mu_wag", np.ascontiguousarray(i["mu_wag_2"][0].reshape(3, 8, P).transpose(2, 0, 1)).reshape(P, 24))
    for n, k in (("w0", "w0_2"), ("a0", "a0_2"), ("k_k", "k_k_2"), ("k_a", "k_a_2"), ("lnx_g", "lnx_g_2"), ("lnx_b", "lnx_b_2"),
                 ("conv_b", "conv_b_2"), ("b_r", "b_rgate_2"), ("b_i", "b_igate_2"), ("lam", "lam_2"), ("r_k", "r_k_2")):
        put(n, col(i[k][0].reshape(-1)))
    put("conv_w", i["conv_w_2"][0][:, 0, :].reshape(4, 4, P).transpose(2, 1, 0))
    put("sgu_b", i["ev_sgu_b"][0].T)
    put("sgu_wT", i["ev_sgu_w"][0].transpose(2, 0, 1))
    put("sgu_n", np.broadcast_to(i["ev_sgu_norm"][0][None, :], (P, 256)))
    for n, k in (("w2k", "ev_cmp_w2_k"), ("w2v", "ev_cmp_w2_v")):
        put(n, i[k][0].reshape(2, P, 64).transpose(1, 0, 2))
    for n, k in (("pos_k", "ev_cmp_pos_k"), ("pos_v", "ev_cmp_pos_v")):
        put(n, i[k][0].reshape(16, P).T)
    for n, k in (("lw1", "w1_2"), ("la1", "a1_2"), ("lg1", "g1_2")):
        m = i[k][0]
        put(n, m.reshape(8, P, m.shape[1]).transpose(1, 0, 2))
    for n, k in (("lw2", "w2_2"), ("la2", "a2_2"), ("lg2", "g2_2")):
        put(n, i[k][0])
    for n, k in (("wr", "w_rgate_2"), ("wi", "w_igate_2")):
        m = np.zeros((P, 4, P), np.float32)
        for c in range(4):
            m[0:64, c, 0:64] = i[k][0][2 * c]
            m[64:128, c, 64:128] = i[k][0][2 * c + 1]
        put(n, m)
    m = np.concatenate([i["w_rg_2"][0], i["w_re_2"][0]], 1)
    put("wre", m.reshape(8, P, 36).transpose(1, 0, 2))
    put("bre", np.broadcast_to(np.concatenate([i["b_rg_2"][0], i["b_re_2"][0]])[None, :], (P, 36)))
    return a


def kernel(**inputs):
    import concourse.bacc as _bacc
    from concourse.bass_utils import run_bass_kernel_spmd as _run

    i = {k: np.asarray(v) for k, v in inputs.items()}
    nc = _bacc.Bacc("TRN2", target_bir_lowering=False, num_devices=1)
    arrays = {
        "in_w": pack_weights(i), "in_s": pack_cols(i), "in_k": const_array(),
        "in_x": np.ascontiguousarray(i["x"][0].T.reshape(8, P, T).transpose(1, 0, 2)),
        "in_p": np.ascontiguousarray(i["positions"][0].reshape(2, P).T),
    }
    args = [nc.dram_tensor(n, a.shape, mybir.dt.from_np(a.dtype), kind="ExternalInput").ap() for n, a in arrays.items()]
    out = nc.dram_tensor("out_0", (P, 8, T), F32, kind="ExternalOutput").ap()
    build(nc, *args, out)
    r = _run(nc, [arrays], core_ids=[0])
    y = r.results[0]["out_0"]
    return np.ascontiguousarray(y.transpose(1, 0, 2).reshape(D, T).T)[None]
```
